# Optimizing a Trainium2 kernel written in Bass

```python
import jax
import jax.numpy as jnp
from jax import lax
import numpy as np

D_MODEL = 1024
BATCH = 1
SEQ = 512
DEPTH = 1

RWKV_HEADS = 8
RWKV_HEAD = 64
RWKV_WIDTH = RWKV_HEADS * RWKV_HEAD
DECAY_LORA = 64
AAA_LORA = 64
GATE_LORA = 128
RWKV_COLS = 3 * RWKV_WIDTH + DECAY_LORA + AAA_LORA + GATE_LORA
RWKV_SPLITS = [RWKV_WIDTH, 2 * RWKV_WIDTH, 3 * RWKV_WIDTH,
               3 * RWKV_WIDTH + DECAY_LORA, 3 * RWKV_WIDTH + DECAY_LORA + AAA_LORA]
DECAY_SCALE = 0.606531
LN_X_EPS = 64e-5
ATT_HEADS = 8
ATT_HEAD = 64
ATT_WIDTH = ATT_HEADS * ATT_HEAD
ATT_COLS = 3 * ATT_WIDTH
MOBA_BLOCK = 256
MOBA_TOPK = 3
Q_BLOCK = 128
ROPE_THETA = 10000.0
GATE_COLS = 2 * D_MODEL
IN_COLS = RWKV_COLS + ATT_COLS + GATE_COLS
N_GROUPS = 4
EXPERTS_PER_GROUP = 8
N_EXPERTS = N_GROUPS * EXPERTS_PER_GROUP
EXPERT_TOPK = 2
D_EXPERT = D_MODEL // 2
NORM_EPS = 1e-6
NEG_INF = -1e30

kernel_name = 'hybrid_rwkv7_moba_hmoe'

def rms_norm(x, g, eps=NORM_EPS):
    xf = x.astype(jnp.float32)
    y = xf * lax.rsqrt(jnp.mean(xf * xf, axis=-1, keepdims=True) + eps)
    return (y * g.astype(jnp.float32)).astype(x.dtype)

def token_shift(z, mu):
    z_prev = jnp.pad(z, ((0, 0), (1, 0), (0, 0)))[:, :-1]
    return z + (z_prev - z) * mu

def rope(x, positions):
    half = x.shape[-1] // 2
    inv_freq = ROPE_THETA ** (-jnp.arange(half, dtype=jnp.float32) / half)
    ang = positions[:, None] * inv_freq[None, :]
    cos = jnp.cos(ang)[None, :, None, :]
    sin = jnp.sin(ang)[None, :, None, :]
    xf = x.astype(jnp.float32)
    x1, x2 = xf[..., :half], xf[..., half:]
    return jnp.concatenate([x1 * cos - x2 * sin, x2 * cos + x1 * sin], axis=-1).astype(x.dtype)

def rwkv7_time_mix(z, mu_shift, w0, w_lora_up, a0, a_lora_up, g_lora_up,
                   k_k, k_a, r_k, lnx_g, lnx_b):
    f32 = jnp.float32
    out_dtype = z.dtype
    B, S, _ = z.shape
    H, N = RWKV_HEADS, RWKV_HEAD
    z = token_shift(z.astype(f32), mu_shift.astype(f32))
    r, k, v, dw, da, dg = jnp.split(z, RWKV_SPLITS, axis=-1)
    log_w = -DECAY_SCALE * jax.nn.sigmoid(w0.astype(f32) + jnp.tanh(dw) @ w_lora_up.astype(f32))
    a = jax.nn.sigmoid(a0.astype(f32) + da @ a_lora_up.astype(f32))
    g = jax.nn.sigmoid(dg) @ g_lora_up.astype(f32)

    def heads(t):
        return t.reshape(B, S, H, N)

    kk = heads(k * k_k.astype(f32))
    kk = kk / jnp.maximum(jnp.sqrt(jnp.sum(kk * kk, axis=-1, keepdims=True)), 1e-12)
    k = heads(k * (1.0 + (a - 1.0) * k_a.astype(f32)))
    r, v, a, w = heads(r), heads(v), heads(a), heads(jnp.exp(log_w))

    def step(state, inp):
        r_t, w_t, k_t, v_t, a_t, b_t = inp
        sa = jnp.einsum('bhij,bhj->bhi', state, a_t)
        state = (state * w_t[:, :, None, :] + sa[..., None] * b_t[:, :, None, :]
                 + v_t[..., None] * k_t[:, :, None, :])
        y_t = jnp.einsum('bhij,bhj->bhi', state, r_t)
        return state, y_t

    xs = tuple(jnp.moveaxis(t, 1, 0) for t in (r, w, k, v, -kk, kk * a))
    s0 = jnp.zeros((B, H, N, N), f32)
    _, ys = lax.scan(step, s0, xs)
    y = jnp.moveaxis(ys, 0, 1)
    mean = jnp.mean(y, axis=-1, keepdims=True)
    var = jnp.mean(jnp.square(y - mean), axis=-1, keepdims=True)
    yn = ((y - mean) * lax.rsqrt(var + LN_X_EPS)).reshape(B, S, H * N)
    yn = yn * lnx_g.astype(f32) + lnx_b.astype(f32)
    bonus = (jnp.sum(r * k * r_k.astype(f32), axis=-1, keepdims=True) * v).reshape(B, S, H * N)
    return ((yn + bonus) * g).astype(out_dtype)

def moba_attention(z, q_norm_g, k_norm_g):
    f32 = jnp.float32
    B, S, _ = z.shape
    H, hd = ATT_HEADS, ATT_HEAD
    q, k, v = jnp.split(z, 3, axis=-1)
    q = q.reshape(B, S, H, hd)
    k = k.reshape(B, S, H, hd)
    v = v.reshape(B, S, H, hd)
    q = rms_norm(q, q_norm_g)
    k = rms_norm(k, k_norm_g)
    pos = jnp.arange(S, dtype=f32)
    q = rope(q, pos)
    k = rope(k, pos)

    n_blk = -(-S // MOBA_BLOCK)
    s_pad = n_blk * MOBA_BLOCK
    padw = ((0, 0), (0, s_pad - S), (0, 0), (0, 0))
    q = jnp.pad(q, padw).transpose(0, 2, 1, 3)
    k = jnp.pad(k, padw).transpose(0, 2, 1, 3)
    v = jnp.pad(v, padw).transpose(0, 2, 1, 3)
    kb = k.reshape(B, H, n_blk, MOBA_BLOCK, hd)
    vb = v.reshape(B, H, n_blk, MOBA_BLOCK, hd)

    k_mean = jnp.mean(kb.astype(f32), axis=3)
    gate = jnp.einsum('bhsd,bhnd->bhsn', q.astype(f32), k_mean)
    q_blk = jnp.arange(s_pad) // MOBA_BLOCK
    past = jnp.arange(n_blk)[None, :] < q_blk[:, None]
    gate = jnp.where(past, gate, NEG_INF)
    n_sel = min(MOBA_TOPK, n_blk)
    top_val, top_idx = lax.top_k(gate, n_sel)
    top_ok = top_val > 0.5 * NEG_INF

    n_qc = s_pad // Q_BLOCK

    def to_chunks(t):
        t = t.reshape((B, H, n_qc, Q_BLOCK) + t.shape[3:])
        t = jnp.moveaxis(t, 2, 1)
        return t.reshape((B * n_qc, H, Q_BLOCK) + t.shape[4:])

    qc, ic, oc = to_chunks(q), to_chunks(top_idx), to_chunks(top_ok)
    b_ids = jnp.repeat(jnp.arange(B, dtype=jnp.int32), n_qc)
    c_ids = jnp.tile(jnp.arange(n_qc, dtype=jnp.int32), B)
    h_ids = jnp.arange(H)[:, None, None]
    scale = ATT_HEAD ** -0.5

    def attend(args):
        q_c, idx_c, ok_c, b, ci = args
        kbb = kb[b]
        vbb = vb[b]
        k_sel = kbb[h_ids, idx_c]
        v_sel = vbb[h_ids, idx_c]
        s_sel = jnp.einsum('hqd,hqnld->hqnl', q_c, k_sel).astype(f32) * scale
        s_sel = jnp.where(ok_c[..., None], s_sel, NEG_INF).reshape(H, Q_BLOCK, n_sel * MOBA_BLOCK)
        own = (ci * Q_BLOCK) // MOBA_BLOCK
        k_own = lax.dynamic_index_in_dim(kbb, own, axis=1, keepdims=False)
        v_own = lax.dynamic_index_in_dim(vbb, own, axis=1, keepdims=False)
        s_own = jnp.einsum('hqd,hld->hql', q_c, k_own).astype(f32) * scale
        q_pos = ci * Q_BLOCK + jnp.arange(Q_BLOCK)
        k_pos = own * MOBA_BLOCK + jnp.arange(MOBA_BLOCK)
        s_own = jnp.where(k_pos[None, None, :] <= q_pos[None, :, None], s_own, NEG_INF)
        p = jax.nn.softmax(jnp.concatenate([s_sel, s_own], axis=-1), axis=-1).astype(v_own.dtype)
        p_sel = p[..., :n_sel * MOBA_BLOCK].reshape(H, Q_BLOCK, n_sel, MOBA_BLOCK)
        p_own = p[..., n_sel * MOBA_BLOCK:]
        return (jnp.einsum('hqnl,hqnld->hqd', p_sel, v_sel)
                + jnp.einsum('hql,hld->hqd', p_own, v_own))

    out = lax.map(attend, (qc, ic, oc, b_ids, c_ids))
    out = out.reshape(B, n_qc, H, Q_BLOCK, hd).transpose(0, 1, 3, 2, 4).reshape(B, s_pad, H * hd)
    return out[:, :S]

def hierarchical_moe(h, w_rg, b_rg, w_re, b_re, w1, w3, w2):
    f32 = jnp.float32
    B, S, D = h.shape
    T = B * S
    ht = h.reshape(T, D)
    p_group = jax.nn.softmax((ht @ w_rg + b_rg).astype(f32), axis=-1)
    pg_top, g_idx = lax.top_k(p_group, 1)
    e_logits = (ht @ w_re + b_re).astype(f32).reshape(T, N_GROUPS, EXPERTS_PER_GROUP)
    e_logits = jnp.take_along_axis(e_logits, g_idx[:, :, None], axis=1)[:, 0]
    p_exp = jax.nn.softmax(e_logits, axis=-1)
    pe_top, e_idx = lax.top_k(p_exp, EXPERT_TOPK)
    weights = pg_top * pe_top / jnp.sum(pe_top, axis=-1, keepdims=True)
    expert = g_idx * EXPERTS_PER_GROUP + e_idx
    flat = expert.reshape(-1)
    order = jnp.argsort(flat)
    tok = order // EXPERT_TOPK
    sizes = jnp.bincount(flat, length=N_EXPERTS).astype(jnp.int32)
    xs = ht[tok]
    hid = jax.nn.silu(lax.ragged_dot(xs, w1, sizes)) * lax.ragged_dot(xs, w3, sizes)
    ys = lax.ragged_dot(hid, w2, sizes) * weights.reshape(-1)[order][:, None].astype(h.dtype)
    out = jax.ops.segment_sum(ys, tok, num_segments=T)
    return out.reshape(B, S, D)

def setup_inputs(seed: int = 0) -> dict:
    key = jax.random.key(seed)
    ks = jax.random.split(key, 32)
    f32 = jnp.float32
    L = DEPTH

    def nrm(k, shape, scale):
        return jax.random.normal(k, shape, f32) * scale

    def gain(k, shape):
        return 1.0 + 0.05 * jax.random.normal(k, shape, f32)

    return {
        'x': nrm(ks[0], (BATCH, SEQ, D_MODEL), 1.0),
        'c': nrm(ks[1], (BATCH, D_MODEL), 1.0),
        'w_ada': nrm(ks[2], (L, D_MODEL, 6 * D_MODEL), 0.02),
        'b_ada': nrm(ks[3], (L, 6 * D_MODEL), 0.02),
        'ln1_g': gain(ks[4], (L, D_MODEL)),
        'ln2_g': gain(ks[5], (L, D_MODEL)),
        'w_in': nrm(ks[6], (L, D_MODEL, IN_COLS), D_MODEL ** -0.5),
        'mu_shift': jax.random.uniform(ks[7], (L, RWKV_COLS), f32, 0.1, 0.9),
        'w0': jax.random.uniform(ks[8], (L, RWKV_WIDTH), f32, -5.0, 1.0),
        'w_lora_up': nrm(ks[9], (L, DECAY_LORA, RWKV_WIDTH), 0.1),
        'a0': nrm(ks[10], (L, RWKV_WIDTH), 0.5),
        'a_lora_up': nrm(ks[11], (L, AAA_LORA, RWKV_WIDTH), 0.1),
        'g_lora_up': nrm(ks[12], (L, GATE_LORA, RWKV_WIDTH), GATE_LORA ** -0.5),
        'k_k': 0.85 + 0.05 * jax.random.normal(ks[13], (L, RWKV_WIDTH), f32),
        'k_a': gain(ks[14], (L, RWKV_WIDTH)),
        'r_k': nrm(ks[15], (L, RWKV_HEADS, RWKV_HEAD), 0.1),
        'lnx_g': gain(ks[16], (L, RWKV_WIDTH)),
        'lnx_b': nrm(ks[17], (L, RWKV_WIDTH), 0.01),
        'q_norm_g': gain(ks[18], (L, ATT_HEAD)),
        'k_norm_g': gain(ks[19], (L, ATT_HEAD)),
        'w_br_rwkv': nrm(ks[20], (L, RWKV_WIDTH, D_MODEL), RWKV_WIDTH ** -0.5),
        'w_br_moba': nrm(ks[21], (L, ATT_WIDTH, D_MODEL), ATT_WIDTH ** -0.5),
        'w_out': nrm(ks[22], (L, D_MODEL, D_MODEL), D_MODEL ** -0.5),
        'w_rg': nrm(ks[23], (L, D_MODEL, N_GROUPS), D_MODEL ** -0.5),
        'b_rg': nrm(ks[24], (L, N_GROUPS), 0.01),
        'w_re': nrm(ks[25], (L, D_MODEL, N_EXPERTS), D_MODEL ** -0.5),
        'b_re': nrm(ks[26], (L, N_EXPERTS), 0.01),
        'w1': nrm(ks[27], (L, N_EXPERTS, D_MODEL, D_EXPERT), D_MODEL ** -0.5),
        'w3': nrm(ks[28], (L, N_EXPERTS, D_MODEL, D_EXPERT), D_MODEL ** -0.5),
        'w2': nrm(ks[29], (L, N_EXPERTS, D_EXPERT, D_MODEL), D_EXPERT ** -0.5),
    }

def reference(x, c, w_ada, b_ada, ln1_g, ln2_g, w_in, mu_shift, w0, w_lora_up, a0,
              a_lora_up, g_lora_up, k_k, k_a, r_k, lnx_g, lnx_b, q_norm_g, k_norm_g,
              w_br_rwkv, w_br_moba, w_out, w_rg, b_rg, w_re, b_re, w1, w3, w2):
    for l in range(DEPTH):
        mod = jnp.einsum('bd,de->be', jax.nn.silu(c), w_ada[l]) + b_ada[l]
        shift1, scale1, gate1, shift2, scale2, gate2 = jnp.split(mod[:, None, :], 6, axis=-1)

        h = rms_norm(x, ln1_g[l]) * (1.0 + scale1) + shift1
        z = jnp.einsum('bsd,de->bse', h, w_in[l])
        z_rwkv = z[..., :RWKV_COLS]
        z_att = z[..., RWKV_COLS:RWKV_COLS + ATT_COLS]
        z_gate = z[..., RWKV_COLS + ATT_COLS:]
        y_a = rwkv7_time_mix(z_rwkv, mu_shift[l], w0[l], w_lora_up[l], a0[l], a_lora_up[l],
                             g_lora_up[l], k_k[l], k_a[l], r_k[l], lnx_g[l], lnx_b[l])
        y_b = moba_attention(z_att, q_norm_g[l], k_norm_g[l])
        g_a, g_b = jnp.split(jax.nn.sigmoid(z_gate), 2, axis=-1)
        merged = (g_a * jnp.einsum('bsc,cd->bsd', y_a, w_br_rwkv[l])
                  + g_b * jnp.einsum('bsc,cd->bsd', y_b, w_br_moba[l]))
        x = x + gate1 * jnp.einsum('bsd,de->bse', merged, w_out[l])

        h2 = rms_norm(x, ln2_g[l]) * (1.0 + scale2) + shift2
        x = x + gate2 * hierarchical_moe(h2, w_rg[l], b_rg[l], w_re[l], b_re[l], w1[l], w3[l], w2[l])
    return x


_drawn_inputs = setup_inputs


def setup_inputs(seed=0):
    import zlib

    import numpy as np

    out = dict(_drawn_inputs(seed))
    spreads = {}
    factors = {'ln1_g': 3.628,
     'w_lora_up': 3.454,
     'k_k': 35.168,
     'k_a': 3.467,
     'lnx_g': 37.351,
     'lnx_b': 64.0,
     'q_norm_g': 8.0,
     'k_norm_g': 8.0,
     'b_rg': 60.736,
     'b_re': 64.0,
     'ln2_g': 8.0,
     'w_rg': 2.943,
     'w_re': 2.944,
     'w1': 2.732}
    for name, (base, spread) in spreads.items():
        noise = np.random.default_rng([zlib.crc32(name.encode()), seed]).standard_normal(out[name].shape)
        drawn = base * np.exp(spread * noise) if base else spread * noise
        out[name] = jnp.asarray(drawn.astype(out[name].dtype))
    for name, factor in factors.items():
        out[name] = (out[name] * factor).astype(out[name].dtype)
    return out
```

```python
import numpy as np
import concourse.bass as bass
from concourse import mybir
from contextlib import ExitStack

P = 128
SEQ, D = 512, 1024
TT = SEQ // P
KT = D // P
HD = 64
HEADS = 8
W = HEADS * HD
CT = W // P
RW_COLS, ATT_COLS = 3 * W + 256, 3 * W
CH = 64
NCH = SEQ // CH
DECAY = 0.606531
LN_X_EPS, NORM_EPS = 64e-5, 1e-6
NEXP, GROUPS, EPG = 32, 4, 8
DE = D // 2
SLOTS = 64
MAXOV = 15
NPASS = NEXP + MAXOV
NEG = -1e30
BIG_INDEX = 1 << 20


def shape_constants():
    i = np.arange(P)
    r, c = i[:, None], i[None, :]
    same = (r // CH) == (c // CH)
    eye = np.eye(P)
    parts = {"ident": eye,
             "before": (r < c) * 1.0,
             "causal_t": np.concatenate([same & (r < c), same & (r <= c)], 1) * 1.0}
    for n, m in enumerate([1, 2, 4, 8, 16, 32]):
        low = (r // (2 * m) == c // (2 * m)) & (r // m % 2 == 1) & (c // m % 2 == 0)
        parts[f"level{n}"] = low + eye
        if n == 0:
            parts["level0_t"] = low.T + eye
    parts["head_ones"] = same * 1.0
    parts["scan_keep"] = np.broadcast_to((np.arange(SEQ) % CH != 0) * 1.0, (P, SEQ))
    parts["diag_mask"] = np.where(c <= r, 0.0, NEG)
    half = HD // 2
    inv_freq = 10000.0 ** (-np.arange(half, dtype=np.float32) / half)
    ang = np.arange(SEQ, dtype=np.float32)[:, None] * inv_freq[None, :].astype(np.float32)
    cos, sin = np.cos(ang), np.sin(ang)
    tiles = lambda a: a.reshape(TT, P, HD).transpose(1, 0, 2).reshape(P, TT * HD)
    parts["cos2"] = tiles(np.concatenate([cos, cos], 1))
    parts["sin2"] = tiles(np.concatenate([-sin, sin], 1))
    parts["expert_id"] = np.broadcast_to(np.arange(NEXP), (P, NEXP))
    parts["first_wins"] = np.broadcast_to(NEXP - np.arange(NEXP), (P, NEXP))
    parts["pass_id"] = np.broadcast_to(np.arange(MAXOV), (P, MAXOV))
    parts["token_id"] = i[:, None] + P * np.arange(TT)[None, :]
    at, cols = {}, 0
    for k, v in parts.items():
        at[k] = (cols, v.shape[1])
        cols += v.shape[1]
    return np.ascontiguousarray(np.concatenate([np.asarray(v, np.float32) for v in parts.values()], 1)), at


CONSTS, CONST_AT = shape_constants()


def hybrid_layer(nc, A, out):
    f32, f32r, i32, u32 = mybir.dt.float32, mybir.dt.float32r, mybir.dt.int32, mybir.dt.uint32
    ALU, ACT, AX = mybir.AluOpType, mybir.ActivationFunctionType, mybir.AxisListType
    IOA = bass.IndirectOffsetOnAxis

    ctx = ExitStack()
    with ctx:
        def sem(name):
            return ctx.enter_context(nc.semaphore(name))

        def pool_of(stack):
            return lambda name, shape, dt=f32: stack.enter_context(nc.sbuf_tensor(name, shape, dt))

        keep = pool_of(ctx)
        consts = keep("consts", [P, CONSTS.shape[1]])
        x = keep("x", [P, TT, D])
        mod = keep("mod", [P, 8, 512])
        bank = [ctx.enter_context(nc.psum_tensor(f"bank{i}", [P, 512], f32)) for i in range(8)]

        def const(name, parts=P):
            at, n = CONST_AT[name]
            return consts[0:parts, at:at + n]

        ident = const("ident")

        first = ExitStack()
        sb = pool_of(first)
        NRING = 3
        ring = sb("ring", [P, NRING, KT, 512])
        hT = sb("hT", [P, KT, SEQ])
        zr = sb("zr", [P, 14, SEQ])
        ahat = sb("ahat", [P, CT, SEQ])
        bhat = sb("bhat", [P, CT, SEQ])
        qkv = sb("qkv", [P, TT, 3 * W])
        tokm = sb("tokm", [P, TT, CT, 4, P])
        cols = sb("cols", [P, 14 + 14 + 4 * 8])
        small = sb("small", [P, 64])
        eps_x = small[:, 60:61]
        prow = tokm[:, 3, 2, 0, :]
        mu, mu1 = cols[:, 0:14], cols[:, 14:28]
        col = {n: cols[:, 28 + 4 * i:32 + 4 * i] for i, n in
               enumerate(["w0", "a0", "k_k", "k_a", "r_k", "lnx_g", "lnx_b", "k_a1"])}
        norm_rows = tokm[:, :, :, :, :].rearrange("p a b c d -> p (a b c d)")
        shift1_bc, scale1_bc = norm_rows[:, 0:D], norm_rows[:, D:2 * D]
        ln1_bc = norm_rows[:, 2 * D:3 * D]
        h_tok = qkv[:, :, 0:D]

        xs = [x[:, i // 2, 512 * (i % 2):512 * (i % 2) + 512] for i in range(8)]
        lora_wa = tokm[:, 3, 3, :, :].rearrange("p a b -> p (a b)")
        lora_g = xs[7]
        decay_end = sb("decay_end", [P, CT, NCH])
        decay_end8 = sb("decay_end8", [HD, HEADS, NCH])
        flat = ring[:, :, :, :].rearrange("p s k n -> p (s k n)")

        def pair(i, parts=P, n=512, off=0):
            return [flat[0:parts, 512 * (i + 12 * g) + off:512 * (i + 12 * g) + off + n].rearrange("p (h n) -> p h n", h=4)
                    for g in range(2)]

        TT1, RB, AK, RK, INV, INVT, PP, WU = (pair(i) for i in range(8))
        QQ = pair(8, HD)
        GG = [pair(9, HD, 256), pair(9, HD, 256, 256)]
        HH = [xs[3][0:HD, :], xs[4][0:HD, :]]
        XX, DE_ = pair(11, P, 256), pair(11, HD, 256, 256)
        STATE = [xs[i][0:HD, :].rearrange("p (h n) -> p h n", h=HEADS) for i in range(3)]

        gqk = zr[:, 12, 0:2 * HD].rearrange("p (a d) -> p a d", a=2)
        ssq = zr[:, 12, 128:192]
        rms_qk = zr[:, 12, 192:256]
        stat = zr[:, 12, 256:320]
        qT, kT = (tokm[:, i, :, :, :].rearrange("p c a b -> p c (a b)") for i in range(2))
        PROB = [[flat[:, 512 * (4 * b + i):512 * (4 * b + i) + P * (i + 1)] for i in range(TT)] for b in range(2)]
        PROBT = [[flat[:, 512 * (8 + 4 * b + i):512 * (8 + 4 * b + i) + P * (TT - i)] for i in range(TT)] for b in range(2)]
        S_AT = [bank[1][:, 384:512], bank[2][:, 0:256], bank[1][:, 0:384], bank[0][:, :]]
        PT_AT = [bank[4][:, :], bank[5][:, 0:384], bank[6][:, 0:256], bank[5][:, 384:512]]
        merged = zr
        msc = [qkv[:, i, 0:512] for i in range(4)]

        first.close()
        PIECES = 4
        raw = keep("raw", [P, PIECES, 4, DE])
        hi = keep("hi", [P, PIECES, 4, DE], f32r)
        lo = keep("lo", [P, PIECES, 4, DE], f32r)
        w2s = keep("w2s", [P, 2, 4, D])
        picked = keep("picked", [P, 2, D])
        xT = keep("xT", [P, 2, KT, P], f32r)
        half_a, half_b, silu_a, hid = (keep(n, [SLOTS, DE]) for n in ("half_a", "half_b", "silu_a", "hid"))
        hidT = keep("hidT", [P, 4, SLOTS])
        ys = keep("ys", [SLOTS, 2, D])
        gather_at = keep("gather_at", [P, NPASS], i32)
        entry = keep("entry", [P, 2 * TT, 4], i32)
        entry_row = keep("entry_row", [P, 2 * TT], i32)
        now = keep("now", [P, 4], i32)
        passes = keep("passes", [1, 1 + MAXOV], i32)
        table = keep("table", [P, NPASS, 4], i32)
        h2 = w2s[:, 0, :, :]
        h2T = w2s[:, 1, :, :].rearrange("p a (b n) -> p (a b) n", b=2)
        h2_hi = hi[:, 0:2, :, :].rearrange("p a b n -> p (a b n)").rearrange("p (t d) -> p t d", t=TT)
        h2_lo = lo[:, 0:2, :, :].rearrange("p a b n -> p (a b n)").rearrange("p (t d) -> p t d", t=TT)
        ln2_bc = picked[:, 0, :]
        rt = picked[:, 1, :]
        rt2 = mod[:, 0:2, :].rearrange("p a n -> p (a n)")
        NR = GROUPS + NEXP
        w_route, b_route = rt[:, 0:KT * NR].rearrange("p (k n) -> p k n", n=NR), rt[:, 288:288 + NR]
        L = rt[:, 324:324 + TT * NR].rearrange("p (t n) -> p t n", n=NR)
        stats = [rt[:, 468 + 4 * i:472 + 4 * i] for i in range(20)]
        ln_stat = rt[:, 548:564]
        gsel, gtmp = (rt[:, 564 + 16 * i:580 + 16 * i].rearrange("p (t n) -> p t n", n=GROUPS) for i in range(2))
        counts, over, over_to, over_from = (rt[:, 596 + 32 * i:628 + 32 * i] for i in range(4))
        ones32 = rt[:, 724:756]
        pass_tmp = rt[0:1, 756:772]
        fresh = table[0:SLOTS, :, :]
        LE, CAND, PICK1, PICK2, PICKS, RANK, PROD = (rt2[:, 128 * i:128 * i + 128].rearrange("p (t n) -> p t n", n=NEXP) for i in range(7))
        ones = rt2[:, 896:1024]
        sum0, sum1 = w2s[:, 0, :, :], w2s[:, 1, :, :]
        h2_table = nc.dram_tensor("h2_table", [2 * SEQ, D], f32).ap()
        slot_table = nc.dram_tensor("slot_table", [SLOTS * NPASS, 4], i32).ap()
        y_rows = nc.dram_tensor("y_rows", [2 * SEQ, D], f32).ap()

        s_const, s_x, s_c, s_cols, s_ln1 = sem("s_const"), sem("s_x"), sem("s_c"), sem("s_cols"), sem("s_ln1")
        s_bias1, s_bias2 = sem("s_bias1"), sem("s_bias2")
        ring_in = [sem(f"ring_in{i}") for i in range(NRING)]
        s_silu, s_cbc, s_prow = sem("s_silu"), sem("s_cbc"), sem("s_prow")
        ada_mm, ada_out = sem("ada_mm"), sem("ada_out")
        s_ssq, s_h, s_xt, s_hT_a, s_hT_v = sem("s_ssq"), sem("s_h"), sem("s_xt"), sem("s_hT_a"), sem("s_hT_v")
        z_mm, z_scaled, z_shifted = sem("z_mm"), sem("z_scaled"), sem("z_shifted")
        att_mm, att_out = sem("att_mm"), sem("att_out")
        s_mu1, s_var1, s_rstd1 = sem("s_mu1"), sem("s_var1"), sem("s_rstd1")
        act_chain, dve_chain, pool_chain = sem("act_chain"), sem("dve_chain"), sem("pool_chain")
        s_done = sem("s_done")
        mg_mm, mg_sig, mg_v, out_mm, x2_done = sem("mg_mm"), sem("mg_sig"), sem("mg_v"), sem("out_mm"), sem("x2_done")
        s_gqk, ssq_qk, sqrt_qk, rstd_qk, rope_done = sem("s_gqk"), sem("ssq_qk"), sem("sqrt_qk"), sem("rstd_qk"), sem("rope_done")
        qk_mm, qk_v, qk_a = sem("qk_mm"), sem("qk_v"), sem("qk_a")
        s_mm, max_v, exp_a, norm_v = sem("s_mm"), sem("max_v"), sem("exp_a"), sem("norm_v")
        pt_mm, pt_v, pt_a, pv_mm, pv_out = sem("pt_mm"), sem("pt_v"), sem("pt_a"), sem("pv_mm"), sem("pv_out")
        s_ln2, s_route_w, ssq2, var2, sqrt2, h2_v, h2_hi_a, h2_lo_v = (sem(n) for n in (
            "s_ln2", "s_route_w", "ssq2", "var2", "sqrt2", "h2_v", "h2_hi_a", "h2_lo_v"))
        h2_stored, h2t_mm, h2t_a, h2t_v, logit_mm, picks_v, rank_mm = (sem(n) for n in (
            "h2_stored", "h2t_mm", "h2t_a", "h2t_v", "logit_mm", "picks_v", "rank_mm"))
        exp_in, exp_out, fresh_v, fresh_in, entry_v, entry_in, table_in, gather_v = (sem(n) for n in (
            "exp_in", "exp_out", "fresh_v", "fresh_in", "entry_v", "entry_in", "table_in", "gather_v"))
        raw_in = [sem(f"raw_in{q}") for q in range(4)]
        w2_in = [sem(f"w2_in{b}") for b in range(2)]
        hi_done, lo_done, piece_mm = sem("hi_done"), sem("lo_done"), sem("piece_mm")
        now_p, rows_in, xt_mm, xt_a, xt_v = sem("now_p"), [sem(f"rows_in{b}") for b in range(2)], sem("xt_mm"), sem("xt_a"), sem("xt_v")
        ab_a, a_v, silu_done, b_v, hid_v, ht_mm, ht_a, w2_mm = (sem(n) for n in (
            "ab_a", "a_v", "silu_done", "b_v", "hid_v", "ht_mm", "ht_a", "w2_mm"))
        y_a, y_v, y_out = sem("y_a"), sem("y_v"), [sem(f"y_out{b}") for b in range(2)]
        ov_ready, ov_in, ov_w2, ov_rows, ov_xt, ov_xe_a, ov_xe_v = (sem(n) for n in (
            "ov_ready", "ov_in", "ov_w2", "ov_rows", "ov_xt", "ov_xe_a", "ov_xe_v"))
        ov_hi, ov_lo, ov_mm, ov_ab, ov_a, ov_silu, ov_hid, ov_ht, ov_hte, ov_y, ov_ya, ov_yv, ov_out = (sem(n) for n in (
            "ov_hi", "ov_lo", "ov_mm", "ov_ab", "ov_a", "ov_silu", "ov_hid", "ov_ht", "ov_hte", "ov_y", "ov_ya", "ov_yv", "ov_out"))
        s_sum, s_final = sem("s_sum"), sem("s_final")
        pe_past, pool_past = sem("pe_past"), sem("pool_past")
        s_lora_w, s_act_in = sem("s_lora_w"), sem("s_act_in")
        lora_mm, lora_act, sq_act, ss_mm, ss_act = sem("lora_mm"), sem("lora_act"), sem("sq_act"), sem("ss_mm"), sem("ss_act")
        scan_done, exp_act, eprev_in = sem("scan_done"), sem("exp_act"), sem("eprev_in")
        bonus_in, bonus_mm, forms_done = sem("bonus_in"), sem("bonus_mm"), sem("forms_done")
        turn_mm, turn_v, turn_a, prep_done = sem("turn_mm"), sem("turn_v"), sem("turn_a"), sem("prep_done")
        solve_mm, solve_v, solve_a = ([sem(f"{n}{g}") for g in range(2)] for n in ("solve_mm", "solve_v", "solve_a"))
        chain_mm, chain_v, s_de8 = sem("chain_mm"), sem("chain_v"), sem("s_de8")
        gn_mm, gn_v, gn_a = sem("gn_mm"), sem("gn_v"), sem("gn_a")

        w_in = A["w_in"].rearrange("(k p) n -> p k n", p=P)
        w_ada = A["w_ada"].rearrange("(k p) n -> p k n", p=P)
        items = [(w_ada[:, :, 512 * j:512 * j + 512], ada_mm, j + 1) for j in range(4)]
        items += [(w_in[:, :, 3 * W:RW_COLS], z_mm, 2)]
        items += [(w_in[:, :, 512 * j:512 * j + 512], z_mm, 4 * j + 6) for j in range(3)]
        items += [(w_in[:, :, RW_COLS + 512 * j:RW_COLS + 512 * j + 512], att_mm, TT * (j + 1)) for j in range(3)]
        items += [(w_ada[:, :, 512 * j:512 * j + 512], ada_mm, j + 1) for j in range(4, 12)]
        w_gate = w_in[:, :, RW_COLS + ATT_COLS:]
        N_BEFORE_MERGE = len(items)
        for b, name in enumerate(("w_br_rwkv", "w_br_moba")):
            items += [(A[name].rearrange("(k p) n -> p k n", p=P), mg_mm, KT * (b + 1))]
            items += [(w_gate[:, :, D * b + 512 * j:D * b + 512 * j + 512], mg_mm, KT * b + 4 * (j + 1)) for j in range(2)]
        items += [(A["w_out"].rearrange("(k p) n -> p k n", p=P)[:, :, 512 * j:512 * j + 512], out_mm, TT * (j + 1)) for j in range(2)]
        Z_TILES = [12, 13] + list(range(12))

        block = ctx.enter_context(nc.Block())

        @block.sync
        def _(sp):
            sp.dma_start(x[:, :, :], A["x"].rearrange("(t p) d -> p t d", p=P)).then_inc(s_x, 16)
            for i, (src, _, _) in enumerate(items):
                slot = i % NRING
                if i >= NRING:
                    sp.wait_ge(items[i - NRING][1], items[i - NRING][2])
                if i == 5:
                    sp.wait_ge(s_prow, 1)
                    sp.dma_start(lora_wa[0:64, :], A["w_lora_up"]).then_inc(s_lora_w, 16)
                    sp.dma_start(lora_wa[64:128, :], A["a_lora_up"]).then_inc(s_lora_w, 16)
                    sp.wait_ge(s_h, TT)
                    sp.dma_start(lora_g, A["g_lora_up"]).then_inc(s_lora_w, 16)
                if i == N_BEFORE_MERGE:
                    sp.wait_ge(gn_v, 4 * CT)
                    sp.wait_ge(rope_done, 2 * TT)
                    sp.dma_start(x[:, :, :], A["x"].rearrange("(t p) d -> p t d", p=P)).then_inc(s_x, 16)
                    sp.wait_ge(pv_out, HEADS)
                k, n = src.shape[1:]
                dst = ring[:, slot, 0:k, 0:n] if n <= 512 else ring[:, slot, :, :].rearrange("p (k a) n -> p k (a n)", k=k)
                sp.dma_start(dst, src).then_inc(ring_in[slot], 16)
            sp.wait_ge(x2_done, 2 * TT)
            sp.dma_start(ln2_bc, A["ln2_g"].partition_broadcast(P)).then_inc(s_ln2, 16)
            sp.dma_start(w_route[:, :, 0:GROUPS], A["w_rg"].rearrange("(k p) n -> p k n", p=P)).then_inc(s_route_w, 16)
            sp.dma_start(w_route[:, :, GROUPS:NR], A["w_re"].rearrange("(k p) n -> p k n", p=P)).then_inc(s_route_w, 16)
            sp.dma_start(b_route[:, 0:GROUPS], A["b_rg"].partition_broadcast(P)).then_inc(s_route_w, 16)
            sp.dma_start(b_route[:, GROUPS:NR], A["b_re"].partition_broadcast(P)).then_inc(s_route_w, 16)
            w13 = [A[n].rearrange("e (p k) n -> e p k n", k=KT)[:, :, 4 * half:4 * half + 4, :] for half in range(2) for n in ("w1", "w3")]
            w2_src = A["w2"].rearrange("e (p k) n -> e p k n", k=4)

            def load_pieces(e):
                for q in range(PIECES):
                    if not (isinstance(e, int) and e == 0):
                        sp.wait_ge(lo_done, PIECES * e + q - 3)
                    src = w13[q][e] if isinstance(e, int) else w13[q][bass.ds(e, 1)].rearrange("e p k n -> (e p) k n")
                    sp.dma_start(raw[:, q, :, :], src).then_inc(raw_in[q], 16)

            def load_w2(e, b):
                if not (isinstance(e, int) and e < 2):
                    sp.wait_ge(w2_mm, e - 1)
                src = w2_src[e] if isinstance(e, int) else w2_src[bass.ds(e, 1)].rearrange("e p k n -> (e p) k n")
                sp.dma_start(w2s[:, b, :, :], src).then_inc(w2_in[b], 16)

            load_pieces(0)
            for t in range(TT):
                sp.wait_ge(h2_hi_a, t + 1)
                sp.dma_start(h2_table[P * t:P * t + P, :], h2_hi[:, t, :].bitcast(f32)).then_inc(h2_stored, 16)
                sp.wait_ge(h2_lo_v, t + 1)
                sp.dma_start(h2_table[SEQ + P * t:SEQ + P * t + P, :], h2_lo[:, t, :].bitcast(f32)).then_inc(h2_stored, 16)
            sp.wait_ge(logit_mm, 1)
            load_w2(0, 0)
            load_pieces(1)
            load_w2(1, 1)
            with sp.Fori(0, (NEXP - 2) // 2) as i:
                for b in range(2):
                    load_pieces(2 * i + 2 + b)
                    load_w2(2 * i + 2 + b, b)
            n_over = sp.value_load(passes[0:1, 0:1], min_val=0, max_val=MAXOV)
            with sp.If(n_over > 0):
                with sp.Fori(0, n_over) as j:
                    sp.wait_ge(ov_ready, j + 1)
                    e = sp.value_load(passes[0:1, bass.ds(j + 1, 1)], min_val=0, max_val=NEXP - 1)
                    for q in range(PIECES):
                        sp.dma_start(raw[:, q, :, :], w13[q][bass.ds(e, 1)].rearrange("e p k n -> (e p) k n")).then_inc(ov_in, 16)
                    sp.dma_start(w2s[:, 0, :, :], w2_src[bass.ds(e, 1)].rearrange("e p k n -> (e p) k n")).then_inc(ov_w2, 16)
            sp.wait_ge(s_sum, 1)
            both = y_rows.rearrange("(k t p) d -> k p t d", k=2, p=P)
            for k in range(2):
                sp.dma_start((sum0, sum1)[k], both[k]).then_inc(s_sum, 16)
            for t in range(TT):
                sp.wait_ge(s_final, t + 1)
                sp.dma_start(out[P * t:P * t + P, :], x[:, t, :]).then_inc(s_done, 16)
            sp.wait_ge(s_done, 16 * TT)

        def ring_wait(eng, i):
            eng.wait_ge(ring_in[i % NRING], 16 * (i // NRING + 1))

        MM_EVENTS = ["ab", "rb", "ak", "rk", "t0"] + [f"{x}{l}" for l in range(1, 6) for x in "pnm" if (x, l) != ("n", 5)]
        MM_EVENTS += ["x", "wu", "q", "gh0", "gh1", "y"]
        V_EVENTS = ["ab", "tt", "rb", "ak", "rk", "n0", "m0"] + [f"p{l}" for l in range(1, 6)] + ["q", "d0", "g0", "d1", "g1", "y"]
        A_EVENTS = [f"{x}{l}" for l in range(1, 6) for x in "nm" if (x, l) != ("n", 5)] + ["x", "wu", "h0", "h1"]
        mm_at = lambda sc, e: len(MM_EVENTS) * sc + MM_EVENTS.index(e) + 1
        v_at = lambda sc, e: len(V_EVENTS) * sc + V_EVENTS.index(e) + 1
        a_at = lambda sc, e: len(A_EVENTS) * sc + A_EVENTS.index(e) + 1

        def weight_of(e):
            w = table[0:SLOTS, :, 2].bitcast(f32)
            return w[:, e:e + 1] if isinstance(e, int) else w[:, bass.ds(e, 1)]

        @block.scalar
        def _(act):
            act.dma_start(ident, A["consts"][:, 0:P]).then_inc(s_c, 16)
            at = 0
            for n, k in [("c", 8), ("mu_shift", 14)] + [(n, CT) for n in ("w0", "a0", "k_k", "k_a", "r_k", "lnx_g", "lnx_b")]:
                src = A[n] if n != "c" else A[n][0]
                act.dma_start(prow[at:at + k, :], src.rearrange("(k p) -> k p", p=P)).then_inc(s_c, 16)
                at += k
            act.dma_start(consts[:, P:], A["consts"][:, P:]).then_inc(s_const, 16)
            act.dma_start(norm_rows[:, 0:2 * D], A["b_ada"][0:2 * D].partition_broadcast(P)).then_inc(s_bias1, 16)
            act.dma_start(mod[:, :, :].rearrange("p a b -> p (a b)"), A["b_ada"][2 * D:6 * D].partition_broadcast(P)).then_inc(s_bias2, 16)
            act.dma_start(ln1_bc, A["ln1_g"].partition_broadcast(P)).then_inc(s_ln1, 16)
            act.wait_ge(s_cols, 1)
            act.activation(small[:, 8:8 + KT], small[:, 0:KT], ACT.Silu).then_inc(s_silu, 1)
            act.wait_ge(s_x, 16)
            for t in range(TT):
                act.activation(h_tok[:, t, :], x[:, t, :], ACT.Square,
                               accum_out=small[:, 16 + t:17 + t]).then_inc(s_ssq, 1)
            act.wait_ge(s_var1, 1)
            act.activation(small[:, 28:32], small[:, 20:24], ACT.Sqrt).then_inc(s_rstd1, 1)
            for k in range(0, KT, 2):
                act.wait_ge(s_xt, k + 1)
                act.activation(hT[:, k, :], bank[2][:, :], ACT.Copy).then_inc(s_hT_a, 1)
            act.wait_ge(s_mu1, 2)
            for j, ct in enumerate(Z_TILES):
                act.wait_ge(z_mm, j + 1)
                act.activation(zr[:, ct, :], bank[4 + j % 4][:, :], ACT.Copy, scale=mu1[:, ct:ct + 1]).then_inc(z_scaled, 1)
                if j == 1:
                    act.wait_ge(z_shifted, 2)
                    act.activation(zr[0:64, 12, :], zr[0:64, 12, :], ACT.Tanh)
                    act.activation(zr[:, 13, :], zr[:, 13, :], ACT.Sigmoid).then_inc(s_act_in, 1)
            for j in range(12):
                act.wait_ge(att_mm, j + 1)
                act.activation(qkv[:, j % TT, 512 * (j // TT):512 * (j // TT) + 512], bank[j % 4][:, :], ACT.Copy).then_inc(att_out, 1)
            for ct in range(CT):
                r_, k_, c1 = zr[:, ct, :], zr[:, 4 + ct, :], slice(ct, ct + 1)
                if ct:
                    act.wait_ge(prep_done, ct)
                act.wait_ge(lora_mm, 2 * ct + 1)
                act.activation(xs[0], bank[0][:, :], ACT.Sigmoid, bias=col["w0"][:, c1]).then_inc(lora_act, 1)
                act.wait_ge(lora_mm, 2 * ct + 2)
                act.activation(xs[1], bank[1][:, :], ACT.Sigmoid, bias=col["a0"][:, c1]).then_inc(lora_act, 1)
                act.activation(xs[2], k_, ACT.Square, scale=col["k_k"][:, c1]).then_inc(sq_act, 1)
                act.wait_ge(scan_done, ct + 1)
                act.activation(xs[6], xs[3], ACT.Exp, scale=-DECAY).then_inc(exp_act, 1)
                act.wait_ge(eprev_in, ct + 1)
                act.activation(xs[0], xs[0], ACT.Exp, scale=-DECAY).then_inc(exp_act, 1)
                act.activation(xs[3], xs[3], ACT.Exp, scale=DECAY).then_inc(exp_act, 1)
                act.wait_ge(ss_mm, ct + 1)
                act.activation(xs[2], bank[2][:, :], ACT.Sqrt).then_inc(ss_act, 1)
                for t in (1, 3):
                    act.wait_ge(turn_mm, TT * ct + t + 1)
                    act.activation(tokm[:, t, ct, :, :].rearrange("p a b -> p (a b)"), bank[5][:, :], ACT.Copy).then_inc(turn_a, 1)
            for sc in range(TT):
                if sc == 2:
                    act.wait_ge(ssq_qk, 1)
                    act.activation(rms_qk, ssq, ACT.Sqrt).then_inc(sqrt_qk, 1)
                for ev in A_EVENTS:
                    for g in range(2):
                        B = bank[4 * g:4 * g + 4]
                        act.wait_ge(solve_mm[g], mm_at(sc, ev if ev[0] != "h" else "gh" + ev[1]))
                        if ev[0] == "h":
                            c = int(ev[1])
                            if c == 1:
                                act.wait_ge(solve_a[g], a_at(sc, "h0"))
                            if sc and c == 0:
                                act.wait_ge(chain_v, 2 * sc)
                            src, dst = B[3 if c == 0 else 0][0:HD, 256:512], HH[c][:, 256 * g:256 * g + 256]
                        else:
                            src, dst = {"n": (B[2], INV), "m": (B[3], INVT), "x": (B[0], XX), "w": (B[2], WU)}[ev[0]]
                            n = 256 if ev == "x" else 512
                            src, dst = src[:, 0:n], dst[g].rearrange("p h n -> p (h n)")
                        act.activation(dst, src, ACT.Copy).then_inc(solve_a[g], 1)
            for ct in range(CT):
                act.wait_ge(gn_mm, 3 * ct + 2)
                act.activation(xs[1], bank[1][:, :], ACT.Identity, bias=eps_x, scale=1.0 / HD).then_inc(gn_a, 1)
                act.wait_ge(gn_a, 2 * ct + 1)
                act.activation(xs[1], xs[1], ACT.Sqrt).then_inc(gn_a, 1)
                act.wait_ge(gn_v, 4 * ct + 4)
            for j in range(0, 8, 2):
                act.wait_ge(qk_mm, j + 1)
                act.activation((qT, kT)[j // 4][:, j % 4, :], bank[4 + j % 4][:, :], ACT.Copy).then_inc(qk_a, 1)

            def exps(h):
                act.wait_ge(max_v, h + 1)
                if h >= 2:
                    act.wait_ge(pt_mm, h - 1)
                for i in range(TT):
                    act.activation(PROB[h % 2][i], S_AT[i], ACT.Exp, bias=stat[:, 4 * (h % 2) + i:4 * (h % 2) + i + 1], scale=HD ** -0.5,
                                   accum_out=stat[:, 8 + 4 * (h % 2) + i:9 + 4 * (h % 2) + i]).then_inc(exp_a, 1)

            exps(0)
            for h in range(HEADS):
                if h + 1 < HEADS:
                    exps(h + 1)
                act.wait_ge(pt_mm, h + 1)
                if h >= 2:
                    act.wait_ge(pv_mm, h - 1)
                for i in (0, 2):
                    act.activation(PROBT[h % 2][i], PT_AT[i], ACT.Copy).then_inc(pt_a, 1)
            for j in range(2 * KT):
                act.wait_ge(mg_mm, j + 1)
                if j >= 2:
                    act.wait_ge(mg_v, j - 1)
                act.activation(msc[j % 2], bank[2 + j % 2][:, :], ACT.Sigmoid).then_inc(mg_sig, 1)
            act.wait_ge(x2_done, 2 * TT)
            for t in range(TT):
                act.activation(h2[:, t, :], x[:, t, :], ACT.Square, accum_out=ln_stat[:, t:t + 1]).then_inc(ssq2, 1)
            act.wait_ge(var2, 1)
            act.activation(ln_stat[:, 8:12], ln_stat[:, 4:8], ACT.Sqrt).then_inc(sqrt2, 1)
            for t in range(TT):
                act.wait_ge(h2_v, t + 1)
                act.activation(h2_hi[:, t, :], h2[:, t, :], ACT.Copy).then_inc(h2_hi_a, 1)
            for k in range(0, KT, 2):
                act.wait_ge(h2t_mm, k + 1)
                act.activation(h2T[:, k, :], bank[6][:, :], ACT.Copy).then_inc(h2t_a, 1)
            for i, n in ((1, 16), (2, 4)):
                act.wait_ge(exp_in, i)
                ap = gtmp if i == 1 else stats[5]
                act.activation(ap, ap, ACT.Exp).then_inc(exp_out, 1)

            def split_hi(q):
                return act.activation(hi[:, q, :, :], raw[:, q, :, :], ACT.Copy)

            def hi_piece(e, q):
                act.wait_ge(raw_in[q], 16 * e + 16)
                if not (isinstance(e, int) and e == 0):
                    act.wait_ge(piece_mm, PIECES * e + q - 3)
                split_hi(q).then_inc(hi_done, 1)

            def y_half(e, b):
                act.wait_ge(w2_mm, e + 1)
                if not (isinstance(e, int) and e < 2):
                    act.wait_ge(y_out[b], 16 * (e // 2))
                act.activation(ys[:, b, 0:512], bank[5][0:SLOTS, :], ACT.Copy, scale=weight_of(e)).then_inc(y_a, 1)

            def turn_x(e, b):
                act.wait_ge(xt_mm, e + 1)
                act.activation(xT[:, b, 0:4, :].rearrange("p k n -> p (k n)"), bank[0][:, :], ACT.Copy).then_inc(xt_a, 1)

            def halves(e):
                act.wait_ge(piece_mm, PIECES * e + 4)
                if not (isinstance(e, int) and e == 0):
                    act.wait_ge(b_v, e)
                act.activation(half_a[:, :], bank[2][SLOTS:P, :], ACT.Copy).then_inc(ab_a, 1)
                act.activation(half_b[:, :], bank[3][SLOTS:P, :], ACT.Copy).then_inc(ab_a, 1)
                act.wait_ge(a_v, e + 1)
                act.activation(silu_a[:, :], half_a[:, :], ACT.Silu).then_inc(silu_done, 1)

            def turn_hid(e):
                act.wait_ge(ht_mm, e + 1)
                act.activation(hidT[:, :, :].rearrange("p k n -> p (k n)"), bank[4][:, 0:4 * SLOTS], ACT.Copy).then_inc(ht_a, 1)

            def act_step(e, b, last=False, head=0):
                if head >= 2:
                    y_half(e - 2, b)
                if not last:
                    hi_piece(e + 1, 0)
                    hi_piece(e + 1, 1)
                if head >= 1:
                    turn_hid(e - 1)
                if not last:
                    hi_piece(e + 1, 2)
                    turn_x(e + 1, 1 - b)
                    hi_piece(e + 1, 3)
                halves(e)

            act.wait_ge(h2_stored, 16 * 2 * TT)
            for q in range(PIECES):
                hi_piece(0, q)
            turn_x(0, 0)
            act_step(0, 0)
            act_step(1, 1, head=1)
            act_step(2, 0, head=2)
            act_step(3, 1, head=2)
            with act.Fori(0, (NEXP - 6) // 2) as i:
                for b in range(2):
                    act_step(2 * i + 4 + b, b, head=2)
            act_step(NEXP - 2, 0, head=2)
            act_step(NEXP - 1, 1, head=2, last=True)
            y_half(NEXP - 2, 0)
            turn_hid(NEXP - 1)
            y_half(NEXP - 1, 1)
            n_over = act.value_load(passes[0:1, 0:1], min_val=0, max_val=MAXOV)
            with act.If(n_over > 0):
                with act.Fori(0, n_over) as j:
                    act.wait_ge(ov_ready, j + 1)
                    act.wait_ge(ov_in, 64 * j + 64)
                    for q in range(PIECES):
                        split_hi(q).then_inc(ov_hi, 1)
                    act.wait_ge(ov_xt, j + 1)
                    act.activation(xT[:, 0, 0:4, :].rearrange("p k n -> p (k n)"), bank[0][:, :], ACT.Copy).then_inc(ov_xe_a, 1)
                    act.wait_ge(ov_mm, j + 1)
                    act.activation(half_a[:, :], bank[2][SLOTS:P, :], ACT.Copy).then_inc(ov_ab, 1)
                    act.activation(half_b[:, :], bank[3][SLOTS:P, :], ACT.Copy).then_inc(ov_ab, 1)
                    act.wait_ge(ov_a, j + 1)
                    act.activation(silu_a[:, :], half_a[:, :], ACT.Silu).then_inc(ov_silu, 1)
                    act.wait_ge(ov_ht, j + 1)
                    act.activation(hidT[:, :, :].rearrange("p k n -> p (k n)"), bank[4][:, 0:4 * SLOTS], ACT.Copy).then_inc(ov_hte, 1)
                    act.wait_ge(ov_y, j + 1)
                    act.activation(ys[:, 0, 0:512], bank[5][0:SLOTS, :], ACT.Copy, scale=weight_of(NEXP + j)).then_inc(ov_ya, 1)


        @block.gpsimd
        def _(pool):
            made = [0]

            def seq(ins):
                made[0] += 1
                ins.then_inc(pool_chain, 1)
                pool.wait_ge(pool_chain, made[0])

            pool.wait_ge(prep_done, CT)
            pool.wait_ge(lora_mm, 2 * CT)
            pool.dma_start(gqk[:, 0, :], A["q_norm_g"].partition_broadcast(P)).then_inc(s_gqk, 16)
            pool.dma_start(gqk[:, 1, :], A["k_norm_g"].partition_broadcast(P)).then_inc(s_gqk, 16)
            pool.wait_ge(att_out, 12)
            heads = lambda ap: ap.rearrange("p (h d) -> p h d", d=HD)
            for i in range(2 * TT):
                t, q = i // 2, heads(qkv[:, i // 2, W * (i % 2):W * (i % 2) + W])
                seq(pool.tensor_tensor(heads(xs[5]), q, q, ALU.mult))
                n = HD // 2
                while n >= 1:
                    a = heads(xs[5])
                    dst = a[:, :, 0:n] if n > 1 else ssq[:, 8 * i:8 * i + 8].unsqueeze(2)
                    seq(pool.tensor_tensor(dst, a[:, :, 0:n], a[:, :, n:2 * n], ALU.add))
                    n //= 2
            pool.tensor_scalar(ssq, ssq, 1.0 / HD, NORM_EPS, ALU.mult, ALU.add).then_inc(ssq_qk, 1)
            pool.wait_ge(rstd_qk, 1)
            pool.wait_ge(s_gqk, 32)
            for i in range(2 * TT):
                t, q = i // 2, heads(qkv[:, i // 2, W * (i % 2):W * (i % 2) + W])
                bc = lambda ap: ap.unsqueeze(1).to_broadcast([P, HEADS, ap.shape[1]])
                cos2, sin2 = (bc(const(n)[:, HD * t:HD * t + HD]) for n in ("cos2", "sin2"))
                seq(pool.tensor_tensor(q, q, ssq[:, 8 * i:8 * i + 8].unsqueeze(2).to_broadcast([P, HEADS, HD]), ALU.mult))
                seq(pool.tensor_tensor(q, q, bc(gqk[:, i % 2, :]), ALU.mult))
                half = HD // 2
                t1 = heads(xs[5])
                pool.tensor_tensor(t1[:, :, 0:half], q[:, :, half:HD], sin2[:, :, 0:half], ALU.mult)
                seq(pool.tensor_tensor(t1[:, :, half:HD], q[:, :, 0:half], sin2[:, :, half:HD], ALU.mult))
                seq(pool.tensor_tensor(q, q, cos2, ALU.mult))
                pool.tensor_tensor(q, q, t1, ALU.add).then_inc(rope_done, 1)
                pool.wait_ge(rope_done, i + 1)

            pool.wait_ge(x2_done, 2 * TT)
            pool.memset(fresh, BIG_INDEX).then_inc(fresh_v, 1)
            pool.wait_ge(fresh_v, 1)
            pool.dma_start(slot_table.rearrange("(p n) c -> p n c", p=SLOTS), fresh).then_inc(fresh_in, 16)
            pool.wait_ge(fresh_in, 16)
            pool.wait_ge(entry_v, 1)
            for j in range(2 * TT):
                pool.indirect_dma_start(slot_table, IOA(entry_row[:, j:j + 1].bitcast(u32), 0), entry[:, j, :], None,
                                        bounds_check=SLOTS * NPASS - 1, oob_is_err=False).then_inc(entry_in, 16)
            pool.wait_ge(entry_in, 16 * 2 * TT)
            for half in range(2):
                pool.dma_start(table[SLOTS * half:SLOTS * half + SLOTS, :, :], slot_table.rearrange("(p n) c -> p n c", p=SLOTS)).then_inc(table_in, 16)
            pool.wait_ge(gather_v, 2)
            pool.wait_ge(h2_stored, 16 * 2 * TT)

            def current(src, at, e):
                n = src.shape[0]
                pool.sem_inc(pool_past, 1)
                pool.tensor_copy(now[0:n, at:at + 1], src[:, e:e + 1] if isinstance(e, int) else src[:, bass.ds(e, 1)]).then_inc(now_p, 1)

            def gather(b, e, sem_):
                current(gather_at[:, :], b, e)
                pool.wait_ge(now_p, now_n(e, 0))
                pool.sem_inc(pool_past, 1)
                pool.indirect_dma_start(picked[:, b, :], None, h2_table, IOA(now[:, b:b + 1].bitcast(u32), 0),
                                        bounds_check=2 * SEQ - 1, oob_is_err=False).then_inc(sem_, 16)

            def scatter(b, e, sem_):
                current(table[0:SLOTS, :, 1], 2 + b, e)
                pool.wait_ge(now_p, now_n(e, 1))
                pool.sem_inc(pool_past, 1)
                pool.indirect_dma_start(y_rows, IOA(now[0:SLOTS, 2 + b:3 + b].bitcast(u32), 0), ys[:, b, :], None,
                                        bounds_check=2 * SEQ - 1, oob_is_err=False).then_inc(sem_, 16)

            def now_n(e, scattering):
                if scattering:
                    return NEXP + e + 1 if isinstance(e, int) else 2 * e + 4
                return e + 1 if isinstance(e, int) else 2 * e - 1

            pool.memset(picked[:, :, :], 0.0).then_inc(gather_v, 1)
            pool.wait_ge(gather_v, 3)
            gather(0, 0, rows_in[0])
            gather(1, 1, rows_in[1])

            def pool_step(e, b, gathers=True):
                if gathers:
                    pool.wait_ge(xt_mm, e + 1)
                    gather(b, e + 2, rows_in[b])
                pool.wait_ge(y_a, e + 1)
                pool.wait_ge(y_v, e + 1)
                scatter(b, e, y_out[b])

            with pool.Fori(0, (NEXP - 2) // 2) as i:
                for b in range(2):
                    pool_step(2 * i + b, b)
            pool_step(NEXP - 2, 0, False)
            pool_step(NEXP - 1, 1, False)
            for b in range(2):
                pool.wait_ge(y_out[b], 16 * NEXP // 2)
            n_over = pool.value_load(passes[0:1, 0:1], min_val=0, max_val=MAXOV)
            with pool.If(n_over > 0):
                with pool.Fori(0, n_over) as j:
                    pool.wait_ge(ov_ready, j + 1)
                    current(gather_at[:, :], 0, j + NEXP)
                    pool.wait_ge(now_p, 2 * j + 2 * NEXP + 1)
                    pool.sem_inc(pool_past, 1)
                    pool.indirect_dma_start(picked[:, 0, :], None, h2_table, IOA(now[:, 0:1].bitcast(u32), 0),
                                            bounds_check=2 * SEQ - 1, oob_is_err=False).then_inc(ov_rows, 16)
                    pool.wait_ge(ov_ya, j + 1)
                    pool.wait_ge(ov_yv, j + 1)
                    current(table[0:SLOTS, :, 1], 2, j + NEXP)
                    pool.wait_ge(now_p, 2 * j + 2 * NEXP + 2)
                    pool.sem_inc(pool_past, 1)
                    pool.indirect_dma_start(y_rows, IOA(now[0:SLOTS, 2:3].bitcast(u32), 0), ys[:, 0, :], None,
                                            bounds_check=2 * SEQ - 1, oob_is_err=False).then_inc(ov_out, 16)
                    pool.wait_ge(ov_out, 16 * j + 16)
                    pool.sem_inc(ov_ready, 1)
            pool.sem_inc(s_sum, 1)

        @block.vector
        def _(dve):
            made = [0]

            def seq(ins):
                made[0] += 1
                ins.then_inc(dve_chain, 1)
                dve.wait_ge(dve_chain, made[0])

            dve.wait_ge(s_prow, 1)
            dve.memset(eps_x, LN_X_EPS)
            dve.tensor_copy(small[:, 0:8], bank[7][:, 0:8])
            dve.tensor_copy(mu, bank[7][:, 8:22])
            dve.tensor_copy(cols[:, 28:56], bank[7][:, 22:50]).then_inc(s_cols, 1)

            def ada_bank(n):
                dve.wait_ge(ada_mm, n + 1)
                dst = (shift1_bc, scale1_bc)[n // 2][:, 512 * (n % 2):512 * (n % 2) + 512] if n < 4 else mod[:, n - 4, :]
                dve.tensor_tensor(dst, bank[n % 2 if n < 4 else 6 + n % 2][:, :], dst, ALU.add).then_inc(ada_out, 1)

            dve.wait_ge(s_bias1, 16)
            for n in range(4):
                ada_bank(n)
            dve.wait_ge(s_ln1, 16)
            dve.wait_ge(ada_out, 4)
            seq(dve.scalar_tensor_tensor(scale1_bc, scale1_bc, 1.0, ln1_bc, ALU.add, ALU.mult))
            dve.wait_ge(s_ssq, TT)
            dve.tensor_scalar(small[:, 20:24], small[:, 16:20], 1.0 / D, NORM_EPS, ALU.mult, ALU.add).then_inc(s_var1, 1)
            dve.wait_ge(s_rstd1, 1)
            seq(dve.reciprocal(small[:, 24:28], small[:, 28:32]))
            for t in range(TT):
                seq(dve.scalar_tensor_tensor(h_tok[:, t, :], x[:, t, :], small[:, 24 + t:25 + t], scale1_bc, ALU.mult, ALU.mult))
                dve.tensor_tensor(h_tok[:, t, :], h_tok[:, t, :], shift1_bc, ALU.add).then_inc(s_h, 1)
            for k in range(1, KT, 2):
                dve.wait_ge(s_xt, k + 1)
                dve.tensor_copy(hT[:, k, :], bank[3][:, :]).then_inc(s_hT_v, 1)
            dve.tensor_scalar(col["k_a1"], col["k_a"], -1.0, 1.0, ALU.mult, ALU.add).then_inc(s_mu1, 1)
            dve.tensor_scalar(mu1, mu, -1.0, 1.0, ALU.mult, ALU.add).then_inc(s_mu1, 1)
            for j, ct in enumerate(Z_TILES):
                dve.wait_ge(z_scaled, j + 1)
                dve.scalar_tensor_tensor(zr[:, ct, 1:SEQ], bank[4 + j % 4][:, 0:SEQ - 1], mu[:, ct:ct + 1], zr[:, ct, 1:SEQ],
                                         ALU.mult, ALU.add).then_inc(z_shifted, 1)
            dve.wait_ge(s_bias2, 16)
            dve.wait_ge(s_const, 16)
            chunks = lambda ap: ap.rearrange("p (c s) -> p c s", s=CH)
            for ct in range(CT):
                r_, k_, v_, c1 = zr[:, ct, :], zr[:, 4 + ct, :], zr[:, 8 + ct, :], slice(ct, ct + 1)
                dve.wait_ge(lora_act, 2 * ct + 1)
                dve.tensor_tensor_scan(xs[3], const("scan_keep"), xs[0], 0.0, ALU.mult, ALU.add).then_inc(scan_done, 1)
                dve.wait_ge(scan_done, ct + 1)
                dve.tensor_tensor(xs[0], xs[3], xs[0], ALU.subtract).then_inc(eprev_in, 1)
                dve.wait_ge(lora_act, 2 * ct + 2)
                seq(dve.tensor_scalar(xs[5], xs[1], col["k_a"][:, c1], col["k_a1"][:, c1], ALU.mult, ALU.add))
                dve.wait_ge(sq_act, ct + 1)
                seq(dve.tensor_scalar(xs[4], k_, col["k_k"][:, c1], None, ALU.mult))
                seq(dve.tensor_tensor(k_, k_, xs[5], ALU.mult))
                dve.scalar_tensor_tensor(xs[5], r_, col["r_k"][:, c1], k_, ALU.mult, ALU.mult).then_inc(bonus_in, 1)
                dve.wait_ge(ss_act, ct + 1)
                seq(dve.tensor_scalar(xs[2], xs[2], 1e-12, None, ALU.max))
                seq(dve.reciprocal(xs[2], xs[2]))
                seq(dve.tensor_tensor(xs[4], xs[4], xs[2], ALU.mult))
                dve.wait_ge(exp_act, 3 * ct + 3)
                dve.tensor_tensor(ahat[:, ct, :], xs[4], xs[0], ALU.mult)
                seq(dve.scalar_tensor_tensor(xs[1], xs[4], -1.0, xs[1], ALU.mult, ALU.mult))
                dve.tensor_copy(decay_end[:, ct, :], chunks(xs[6])[:, :, CH - 1])
                seq(dve.tensor_tensor(bhat[:, ct, :], xs[1], xs[3], ALU.mult))
                seq(dve.tensor_tensor(k_, k_, xs[3], ALU.mult))
                seq(dve.tensor_tensor(r_, r_, xs[6], ALU.mult))
                end = decay_end[:, ct, :].unsqueeze(2).to_broadcast([P, NCH, CH])
                dve.tensor_tensor(chunks(xs[1]), chunks(bhat[:, ct, :]), end, ALU.mult)
                dve.tensor_tensor(chunks(xs[4]), chunks(k_), end, ALU.mult).then_inc(forms_done, 1)
                for t in (0, 2):
                    dve.wait_ge(turn_mm, TT * ct + t + 1)
                    dve.tensor_copy(tokm[:, t, ct, :, :].rearrange("p a b -> p (a b)"), bank[4][:, :]).then_inc(turn_v, 1)
                dve.wait_ge(bonus_mm, ct + 1)
                dve.wait_ge(turn_mm, TT * (ct + 1))
                dve.tensor_tensor(v_, v_, bank[3][:, :], ALU.mult).then_inc(prep_done, 1)
                for n in (4 + 2 * ct, 5 + 2 * ct):
                    ada_bank(n)
            for h in range(HEADS):
                ins = dve.tensor_copy(decay_end8[:, h, :], decay_end[HD * (h % 2):HD * (h % 2) + HD, h // 2, :])
            ins.then_inc(s_de8, 1)
            dve.wait_ge(s_de8, 1)

            def bc4(name, at=0, n=P, parts=P):
                return const(name, parts)[:, at:at + n].unsqueeze(1).to_broadcast([parts, 4, n])

            def f4(ap):
                return ap.rearrange("p (h n) -> p h n", h=4)

            for sc in range(TT):
                toks = slice(P * sc, P * sc + P)
                if sc == 2:
                    dve.wait_ge(sqrt_qk, 1)
                    dve.reciprocal(ssq, rms_qk).then_inc(rstd_qk, 1)
                for ev in V_EVENTS:
                    for g in range(2):
                        B = bank[4 * g:4 * g + 4]
                        if ev in MM_EVENTS and (ev, g) != ("y", 0):
                            dve.wait_ge(solve_mm[g], mm_at(sc, {"ab": "rb", "ak": "rk"}.get(ev, ev)))
                        if ev in ("ab", "rb", "ak", "rk"):
                            strict = ev[0] == "a"
                            dst = {"ab": TT1, "rb": RB, "ak": AK, "rk": RK}[ev][g]
                            mask = const("causal_t")[:, 0 if strict else P:P if strict else 2 * P]
                            for half in range(2):
                                src = f4(B[half + (0 if ev[1] == "b" else 2)])
                                ins = dve.tensor_tensor(dst[:, half::2, :], src[:, 0:2, :] if strict else src[:, 2:4, :],
                                                        mask.unsqueeze(1).to_broadcast([P, 2, P]), ALU.mult)
                        elif ev == "tt":
                            dve.wait_ge(solve_v[g], v_at(sc, "ab"))
                            ins = dve.tensor_tensor(TT1[g], TT1[g], bc4("ident"), ALU.add)
                        elif ev == "n0":
                            dve.wait_ge(solve_mm[g], mm_at(sc, "t0"))
                            ins = dve.tensor_tensor(INV[g], f4(B[0]), bc4("level0"), ALU.mult)
                        elif ev == "m0":
                            dve.wait_ge(solve_v[g], v_at(sc, "tt"))
                            ins = dve.tensor_tensor(INVT[g], TT1[g], bc4("level0_t"), ALU.mult)
                        elif ev[0] == "p":
                            ins = dve.tensor_tensor(PP[g], f4(B[1]), bc4("level" + ev[1]), ALU.mult)
                        elif ev == "q":
                            for half in range(2):
                                ins = dve.tensor_tensor(QQ[g][:, half::2, :], f4(B[1][0:HD, :])[:, half::2, :],
                                                        zr[HD * half:HD * half + HD, 2 * g:2 * g + 2, toks], ALU.add)
                        elif ev[0] == "d":
                            c = int(ev[1])
                            if c == 1:
                                dve.wait_ge(solve_v[g], v_at(sc, "g0"))
                            ins = dve.tensor_tensor(DE_[g], bc4("ident", 0, HD, HD),
                                                    decay_end8[:, 4 * g:4 * g + 4, 2 * sc + c].unsqueeze(2).to_broadcast([HD, 4, HD]), ALU.mult)
                        elif ev[0] == "g":
                            c = int(ev[1])
                            dve.wait_ge(solve_v[g], v_at(sc, f"d{c}"))
                            dve.wait_ge(solve_a[g], a_at(sc, f"h{c}"))
                            ins = dve.tensor_tensor(GG[c][g], f4(B[3 if c == 0 else 0][0:HD, 0:256]), DE_[g], ALU.add)
                        elif ev == "y":
                            if g == 0:
                                for c in range(2):
                                    n = 2 * sc + c
                                    for g2 in range(2):
                                        dve.wait_ge(solve_a[g2], a_at(sc, f"h{c}"))
                                    H = HH[c].rearrange("p (h n) -> p h n", h=HEADS)
                                    if n == 0:
                                        dve.tensor_copy(STATE[1], H).then_inc(chain_v, 1)
                                    else:
                                        dve.wait_ge(chain_mm, n)
                                        dve.tensor_tensor(STATE[(n + 1) % 3], bank[2 if c == 0 else 6][0:HD, :].rearrange("p (h n) -> p h n", h=HEADS),
                                                          H, ALU.add).then_inc(chain_v, 1)
                                dve.wait_ge(solve_mm[g], mm_at(sc, "y"))
                            for half in range(2):
                                ins = dve.tensor_copy(ahat[HD * half:HD * half + HD, 2 * g:2 * g + 2, toks],
                                                      f4(B[1][0:HD, :])[:, half::2, :])
                        ins.then_inc(solve_v[g], 1)
            for ct in range(CT):
                y_, c1 = ahat[:, ct, :], slice(ct, ct + 1)
                if ct == 0:
                    for g in range(2):
                        dve.wait_ge(solve_v[g], v_at(TT - 1, "y"))
                dve.wait_ge(gn_mm, 3 * ct + 1)
                dve.scalar_tensor_tensor(y_, bank[0][:, :], -1.0 / HD, y_, ALU.mult, ALU.add).then_inc(gn_v, 1)
                dve.wait_ge(gn_v, 4 * ct + 1)
                dve.tensor_tensor(xs[0], y_, y_, ALU.mult).then_inc(gn_v, 1)
                dve.wait_ge(gn_a, 2 * ct + 2)
                dve.reciprocal(xs[1], xs[1]).then_inc(gn_v, 1)
                dve.wait_ge(gn_v, 4 * ct + 3)
                seq(dve.tensor_tensor(y_, y_, xs[1], ALU.mult))
                seq(dve.tensor_scalar(y_, y_, col["lnx_g"][:, c1], col["lnx_b"][:, c1], ALU.mult, ALU.add))
                seq(dve.tensor_tensor(y_, y_, zr[:, 8 + ct, :], ALU.add))
                dve.wait_ge(gn_mm, 3 * ct + 3)
                dve.tensor_tensor(y_, y_, bank[2][:, :], ALU.mult).then_inc(gn_v, 1)
            for j in range(1, 8, 2):
                dve.wait_ge(qk_mm, j + 1)
                dve.tensor_copy((qT, kT)[j // 4][:, j % 4, :], bank[4 + j % 4][:, :]).then_inc(qk_v, 1)

            def row_max(h):
                b = 4 * (h % 2)
                dve.wait_ge(s_mm, h + 1)
                if h >= 2:
                    dve.wait_ge(norm_v, 4 * (h - 1))
                for i in range(TT):
                    dg = S_AT[i][:, P * i:P * i + P]
                    ins = dve.tensor_tensor(dg, dg, const("diag_mask"), ALU.add)
                seq(ins)
                for i in range(TT):
                    ins = dve.reduce_max(stat[:, 16 + i:17 + i], S_AT[i], AX.X)
                seq(ins)
                dve.tensor_scalar(stat[:, b:b + 4], stat[:, 16:20], -HD ** -0.5, None, ALU.mult).then_inc(max_v, 1)

            row_max(0)
            for h in range(HEADS):
                b = 8 + 4 * (h % 2)
                dve.wait_ge(exp_a, TT * (h + 1))
                seq(dve.reciprocal(stat[:, 24:28], stat[:, b:b + 4]))
                for i in range(TT):
                    dve.tensor_scalar(PROB[h % 2][i], PROB[h % 2][i], stat[:, 24 + i:25 + i], None, ALU.mult).then_inc(norm_v, 1)
                dve.wait_ge(norm_v, 4 * h + 4)
                if h + 1 < HEADS:
                    row_max(h + 1)
                dve.wait_ge(pt_mm, h + 1)
                if h >= 2:
                    dve.wait_ge(pv_mm, h - 1)
                for i in (1, 3):
                    dve.tensor_copy(PROBT[h % 2][i], PT_AT[i]).then_inc(pt_v, 1)
                dve.wait_ge(pv_mm, h + 1)
                dve.tensor_copy(bhat[HD * (h % 2):HD * (h % 2) + HD, h // 2, :], bank[3 + 4 * (h % 2)][0:HD, :]).then_inc(pv_out, 1)
            for j in range(2 * KT):
                ct = j % KT
                dve.wait_ge(mg_sig, j + 1)
                if j < KT:
                    dve.tensor_tensor(merged[:, ct, :], msc[j % 2], bank[j % 2][:, :], ALU.mult).then_inc(mg_v, 1)
                else:
                    seq(dve.tensor_tensor(msc[j % 2], msc[j % 2], bank[j % 2][:, :], ALU.mult))
                    dve.tensor_tensor(merged[:, ct, :], merged[:, ct, :], msc[j % 2], ALU.add).then_inc(mg_v, 1)
            dve.wait_ge(s_x, 32)
            for j in range(2 * TT):
                n, t = j // TT, j % TT
                dve.wait_ge(out_mm, j + 1)
                if j >= 4:
                    dve.wait_ge(x2_done, j - 3)
                elif j == 0:
                    dve.wait_ge(mg_v, 2 * KT)
                seq(dve.tensor_tensor(msc[j % 4], bank[4 + t][:, :], mod[:, n, :], ALU.mult))
                xx = x[:, t, 512 * n:512 * n + 512]
                dve.tensor_tensor(xx, xx, msc[j % 4], ALU.add).then_inc(x2_done, 1)
            shift2, a2 = (mod[:, i:i + 2, :].rearrange("p a n -> p (a n)") for i in (2, 4))
            dve.wait_ge(s_ln2, 16)
            dve.wait_ge(x2_done, 2 * TT)
            seq(dve.scalar_tensor_tensor(a2, a2, 1.0, ln2_bc, ALU.add, ALU.mult))
            dve.wait_ge(ssq2, TT)
            dve.tensor_scalar(ln_stat[:, 4:8], ln_stat[:, 0:4], 1.0 / D, NORM_EPS, ALU.mult, ALU.add).then_inc(var2, 1)
            dve.wait_ge(sqrt2, 1)
            seq(dve.reciprocal(ln_stat[:, 12:16], ln_stat[:, 8:12]))
            for t in range(TT):
                seq(dve.scalar_tensor_tensor(h2[:, t, :], x[:, t, :], ln_stat[:, 12 + t:13 + t], a2, ALU.mult, ALU.mult))
                dve.tensor_tensor(h2[:, t, :], h2[:, t, :], shift2, ALU.add).then_inc(h2_v, 1)
                dve.wait_ge(h2_hi_a, t + 1)
                dve.tensor_tensor(h2_lo[:, t, :], h2[:, t, :], h2_hi[:, t, :].bitcast(f32), ALU.subtract).then_inc(h2_lo_v, 1)
            for k in range(1, KT, 2):
                dve.wait_ge(h2t_mm, k + 1)
                dve.tensor_copy(h2T[:, k, :], bank[7][:, :]).then_inc(h2t_v, 1)

            def of_token(i):
                return stats[i].unsqueeze(2).to_broadcast([P, TT, NEXP])

            def const4(name, n=NEXP):
                return const(name)[:, 0:n].unsqueeze(1).to_broadcast([P, TT, n])

            def pick(dst, values, top, cand, n):
                t4 = stats[top].unsqueeze(2).to_broadcast([P, TT, n])
                seq(dve.reduce_max(stats[top], values, AX.X))
                seq(dve.tensor_tensor(cand, values, t4, ALU.is_equal))
                seq(dve.tensor_tensor(cand, cand, const4("first_wins", n), ALU.mult))
                seq(dve.reduce_max(stats[19], cand, AX.X))
                seq(dve.tensor_tensor(dst, cand, stats[19].unsqueeze(2).to_broadcast([P, TT, n]), ALU.is_equal))

            dve.wait_ge(s_route_w, 64)
            dve.wait_ge(logit_mm, 1)
            seq(dve.tensor_tensor(L, bank[0][:, 0:TT * NR].rearrange("p (t n) -> p t n", n=NR),
                                  b_route.unsqueeze(1).to_broadcast([P, TT, NR]), ALU.add))
            LG = L[:, :, 0:GROUPS]
            pick(gsel, LG, 0, gtmp, GROUPS)
            dve.tensor_tensor(gtmp, LG, stats[0].unsqueeze(2).to_broadcast([P, TT, GROUPS]), ALU.subtract).then_inc(exp_in, 1)
            dve.wait_ge(exp_out, 1)
            seq(dve.reduce_sum(stats[1], gtmp, AX.X))
            seq(dve.reciprocal(stats[1], stats[1]))
            seq(dve.tensor_scalar(gsel, gsel, -NEG, NEG, ALU.mult, ALU.add))
            for t in range(TT):
                ins = dve.tensor_tensor(LE[:, t, :].rearrange("p (g e) -> p g e", g=GROUPS),
                                        L[:, t, GROUPS:NR].rearrange("p (g e) -> p g e", g=GROUPS),
                                        gsel[:, t, :].unsqueeze(2).to_broadcast([P, GROUPS, EPG]), ALU.add)
            seq(ins)
            pick(PICK1, LE, 2, CAND, NEXP)
            seq(dve.scalar_tensor_tensor(LE, PICK1, 2 * NEG, LE, ALU.mult, ALU.add))
            pick(PICK2, LE, 3, CAND, NEXP)
            dve.memset(ones, 1.0)
            dve.memset(ones32, 1.0)
            dve.tensor_tensor(PICKS, PICK1, PICK2, ALU.add).then_inc(picks_v, 1)
            dve.tensor_tensor(stats[5], stats[3], stats[2], ALU.subtract).then_inc(exp_in, 1)
            dve.wait_ge(exp_out, 2)
            seq(dve.tensor_scalar(stats[4], stats[5], 1.0, None, ALU.add))
            seq(dve.reciprocal(stats[4], stats[4]))
            seq(dve.tensor_tensor(stats[4], stats[4], stats[1], ALU.mult))
            seq(dve.tensor_tensor(stats[5], stats[5], stats[4], ALU.mult))
            dve.wait_ge(rank_mm, 1)
            seq(dve.tensor_copy(RANK, bank[1][:, 0:TT * NEXP].rearrange("p (t n) -> p t n", n=NEXP)))
            seq(dve.tensor_copy(counts, bank[1][:, TT * NEXP:TT * NEXP + NEXP]))
            seq(dve.tensor_scalar(over, counts, float(SLOTS), None, ALU.is_gt))
            for m in range(2, SEQ // SLOTS):
                seq(dve.scalar_tensor_tensor(over, counts, float(SLOTS * m), over, ALU.is_gt, ALU.add))
            seq(dve.tensor_tensor_scan(over_to, ones32, over, 0.0, ALU.mult, ALU.add))
            seq(dve.tensor_tensor(over_from, over_to, over, ALU.subtract))
            seq(dve.tensor_copy(passes[:, 0:1], over_to[0:1, NEXP - 1:NEXP]))
            for j in range(MAXOV):
                seq(dve.tensor_scalar(CAND[0:1, 0, :], over_to[0:1, :], float(j), None, ALU.is_le))
                seq(dve.reduce_sum(pass_tmp[:, j:j + 1], CAND[0:1, 0, :], AX.X))
            seq(dve.tensor_scalar(pass_tmp[:, 0:MAXOV], pass_tmp[:, 0:MAXOV], float(NEXP - 1), None, ALU.min))
            seq(dve.tensor_copy(passes[:, 1:1 + MAXOV], pass_tmp[:, 0:MAXOV]))
            for k, sel in enumerate((PICK1, PICK2)):
                rank, expert, start, full, row = stats[6], stats[7], stats[8], stats[9], stats[10]
                for dst, ap in ((rank, RANK), (expert, const4("expert_id")), (start, over_from.unsqueeze(1).to_broadcast([P, TT, NEXP]))):
                    seq(dve.tensor_tensor(PROD, sel, ap, ALU.mult))
                    seq(dve.reduce_sum(dst, PROD, AX.X))
                seq(dve.tensor_scalar(full, rank, float(SLOTS), None, ALU.is_ge))
                for m in range(2, SEQ // SLOTS):
                    seq(dve.scalar_tensor_tensor(full, rank, float(SLOTS * m), full, ALU.is_ge, ALU.add))
                seq(dve.scalar_tensor_tensor(rank, full, -float(SLOTS), rank, ALU.mult, ALU.add))
                seq(dve.tensor_tensor(start, start, full, ALU.add))
                seq(dve.scalar_tensor_tensor(start, start, float(NEXP - 1), expert, ALU.add, ALU.subtract))
                seq(dve.tensor_scalar(full, full, 1.0, None, ALU.min))
                seq(dve.tensor_tensor(start, start, full, ALU.mult))
                seq(dve.tensor_tensor(start, start, expert, ALU.add))
                seq(dve.scalar_tensor_tensor(row, rank, float(NPASS), start, ALU.mult, ALU.add))
                at = slice(TT * k, TT * k + TT)
                seq(dve.tensor_copy(entry_row[:, at], row))
                seq(dve.tensor_copy(entry[:, at, 0], const("token_id")))
                seq(dve.tensor_scalar(entry[:, at, 1], const("token_id"), float(SEQ * k), None, ALU.add))
                seq(dve.tensor_copy(entry[:, at, 2].bitcast(f32), stats[4 + k]))
                seq(dve.tensor_scalar(entry[:, at, 3], const("token_id"), float(SEQ), None, ALU.add))
            dve.sem_inc(entry_v, 1)
            dve.wait_ge(table_in, 32)
            dve.tensor_copy(gather_at[0:SLOTS, :], table[0:SLOTS, :, 0]).then_inc(gather_v, 1)
            dve.tensor_copy(gather_at[SLOTS:P, :], table[SLOTS:P, :, 3]).then_inc(gather_v, 1)

            def split_lo(q):
                return dve.tensor_tensor(lo[:, q, :, :], raw[:, q, :, :], hi[:, q, :, :].bitcast(f32), ALU.subtract)

            def lo_piece(e, q):
                dve.wait_ge(hi_done, PIECES * e + q + 1)
                split_lo(q).then_inc(lo_done, 1)

            def y_half(e, b):
                dve.wait_ge(w2_mm, e + 1)
                if not (isinstance(e, int) and e < 2):
                    dve.wait_ge(y_out[b], 16 * (e // 2))
                dve.tensor_scalar(ys[:, b, 512:D], bank[6][0:SLOTS, :], weight_of(e), None, ALU.mult).then_inc(y_v, 1)

            def turn_x(e, b):
                dve.wait_ge(xt_mm, e + 1)
                dve.tensor_copy(xT[:, b, 4:8, :].rearrange("p k n -> p (k n)"), bank[1][:, :]).then_inc(xt_v, 1)

            def hidden(e):
                dve.wait_ge(ab_a, 2 * e + 2)
                dve.tensor_tensor(half_a[:, :], bank[2][0:SLOTS, :], half_a[:, :], ALU.add).then_inc(a_v, 1)
                dve.tensor_tensor(half_b[:, :], bank[3][0:SLOTS, :], half_b[:, :], ALU.add).then_inc(b_v, 1)
                dve.wait_ge(silu_done, e + 1)
                dve.wait_ge(b_v, e + 1)
                if not (isinstance(e, int) and e == 0):
                    dve.wait_ge(ht_mm, e)
                dve.tensor_tensor(hid[:, :], silu_a[:, :], half_b[:, :], ALU.mult).then_inc(hid_v, 1)

            def dve_step(e, b, last=False, head=0):
                if head >= 2:
                    y_half(e - 2, b)
                if not last:
                    for q in range(3):
                        lo_piece(e + 1, q)
                    turn_x(e + 1, 1 - b)
                    lo_piece(e + 1, 3)
                hidden(e)

            for q in range(PIECES):
                lo_piece(0, q)
            turn_x(0, 0)
            dve_step(0, 0)
            dve_step(1, 1, head=1)
            dve_step(2, 0, head=2)
            dve_step(3, 1, head=2)
            with dve.Fori(0, (NEXP - 6) // 2) as i:
                for b in range(2):
                    dve_step(2 * i + 4 + b, b, head=2)
            dve_step(NEXP - 2, 0, head=2)
            dve_step(NEXP - 1, 1, head=2, last=True)
            y_half(NEXP - 2, 0)
            y_half(NEXP - 1, 1)
            n_over = dve.value_load(passes[0:1, 0:1], min_val=0, max_val=MAXOV)
            for b in range(2):
                dve.wait_ge(y_out[b], 16 * NEXP // 2)
            dve.wait_ge(y_a, NEXP)
            dve.sem_inc(ov_ready, 1)
            with dve.If(n_over > 0):
                with dve.Fori(0, n_over) as j:
                    for q in range(PIECES):
                        dve.wait_ge(ov_hi, 4 * j + q + 1)
                        split_lo(q).then_inc(ov_lo, 1)
                    dve.wait_ge(ov_xt, j + 1)
                    dve.tensor_copy(xT[:, 0, 4:8, :].rearrange("p k n -> p (k n)"), bank[1][:, :]).then_inc(ov_xe_v, 1)
                    dve.wait_ge(ov_ab, 2 * j + 2)
                    dve.tensor_tensor(half_a[:, :], bank[2][0:SLOTS, :], half_a[:, :], ALU.add).then_inc(ov_a, 1)
                    dve.tensor_tensor(half_b[:, :], bank[3][0:SLOTS, :], half_b[:, :], ALU.add).then_inc(b_v, 1)
                    dve.wait_ge(b_v, j + NEXP + 1)
                    dve.wait_ge(ov_silu, j + 1)
                    dve.tensor_tensor(hid[:, :], silu_a[:, :], half_b[:, :], ALU.mult).then_inc(ov_hid, 1)
                    dve.wait_ge(ov_y, j + 1)
                    dve.tensor_scalar(ys[:, 0, 512:D], bank[6][0:SLOTS, :], weight_of(j + NEXP), None, ALU.mult).then_inc(ov_yv, 1)
            dve.wait_ge(s_sum, 33)
            gate2 = mod[:, 6:8, :].rearrange("p a n -> p (a n)")
            for t in range(TT):
                seq(dve.tensor_tensor(sum0[:, t, :], sum0[:, t, :], sum1[:, t, :], ALU.add))
                seq(dve.tensor_tensor(sum0[:, t, :], sum0[:, t, :], gate2, ALU.mult))
                dve.tensor_tensor(x[:, t, :], x[:, t, :], sum0[:, t, :], ALU.add).then_inc(s_final, 1)

        @block.tensor
        def _(pe):
            taken = [0]

            def take():
                ring_wait(pe, taken[0])
                taken[0] += 1
                return (taken[0] - 1) % NRING

            def ada(n):
                slot = take()
                if n in (2, 3):
                    pe.wait_ge(ada_out, n - 1)
                if n >= 6:
                    pe.wait_ge(ada_out, n - 1)
                for k in range(KT):
                    mm = pe.matmul(bank[n % 2 if n < 4 else 6 + n % 2][:, :], small[:, 8 + k:9 + k].to_broadcast([P, P]), ring[:, slot, k, :], start=(k == 0), stop=(k == KT - 1))
                mm.then_inc(ada_mm, 1)

            pe.wait_ge(s_c, 16 * 10)
            pe.transpose(bank[7][:, 0:50], prow[0:50, :], ident[0:50, 0:50]).then_inc(s_prow, 1)
            pe.wait_ge(s_silu, 1)
            for n in range(4):
                ada(n)
            pe.wait_ge(s_const, 16)
            for k in range(KT):
                if k >= 2:
                    pe.wait_ge((s_hT_a, s_hT_v)[k % 2], k // 2)
                for t in range(TT):
                    if k == 0:
                        pe.wait_ge(s_h, t + 1)
                    mm = pe.transpose(bank[2 + k % 2][:, t * P:t * P + P], h_tok[:, t, k * P:k * P + P], ident)
                mm.then_inc(s_xt, 1)
            pe.wait_ge(s_hT_a, 4)
            pe.wait_ge(s_hT_v, 4)
            for j, ct in enumerate(Z_TILES):
                if j in (0, 2, 6, 10):
                    slot = take()
                if j >= 4:
                    pe.wait_ge(z_shifted, j - 3)
                for k in range(KT):
                    mm = pe.matmul(bank[4 + j % 4][:, :], ring[:, slot, k, (ct % 4) * P:(ct % 4) * P + P], hT[:, k, :], start=(k == 0), stop=(k == KT - 1))
                mm.then_inc(z_mm, 1)
            for j in range(12):
                if j % TT == 0:
                    slot = take()
                if j >= 4:
                    pe.wait_ge(att_out, j - 3)
                for k in range(KT):
                    mm = pe.matmul(bank[j % 4][:, :], hT[:, k, (j % TT) * P:(j % TT) * P + P], ring[:, slot, k, :], start=(k == 0), stop=(k == KT - 1))
                mm.then_inc(att_mm, 1)
            pe.wait_ge(att_out, 12)
            pe.wait_ge(z_shifted, 14)
            pe.wait_ge(s_act_in, 1)
            pe.wait_ge(s_lora_w, 48)

            def lora(ct):
                for i, rows in enumerate((slice(0, 64), slice(64, 128))):
                    if ct:
                        pe.wait_ge(lora_act, 2 * ct - 1 + i)
                    pe.matmul(bank[i][:, :], lora_wa[rows, P * ct:P * ct + P], zr[rows, 12, :], start=True, stop=True).then_inc(lora_mm, 1)

            lora(0)
            for ct in range(CT):
                v_ = zr[:, 8 + ct, :]
                pe.wait_ge(sq_act, ct + 1)
                pe.matmul(bank[2][:, :], const("head_ones"), xs[2], start=True, stop=True).then_inc(ss_mm, 1)
                if ct + 1 < CT:
                    lora(ct + 1)
                pe.wait_ge(bonus_in, ct + 1)
                if ct:
                    pe.wait_ge(prep_done, ct)
                pe.matmul(bank[3][:, :], const("head_ones"), xs[5], start=True, stop=True).then_inc(bonus_mm, 1)
                for n in (4 + 2 * ct, 5 + 2 * ct):
                    ada(n)
                pe.wait_ge(forms_done, ct + 1)
                for t in range(TT):
                    if TT * ct + t >= 2:
                        pe.wait_ge((turn_v, turn_a)[t % 2], (TT * ct + t) // 2)
                    for i, src in enumerate((v_, xs[1], xs[4], ahat[:, ct, :])):
                        mm = pe.transpose(bank[4 + t % 2][:, P * i:P * i + P], src[:, P * t:P * t + P], ident)
                    mm.then_inc(turn_mm, 1)
            pe.wait_ge(prep_done, CT)
            pe.wait_ge(turn_v, 2 * CT)
            pe.wait_ge(turn_a, 2 * CT)
            pe.wait_ge(ada_out, 12)
            for sc in range(TT):
                toks = slice(P * sc, P * sc + P)
                for ev in MM_EVENTS:
                    for g in range(2):
                        B = bank[4 * g:4 * g + 4]
                        if ev == "y" and g == 0:
                            for c in range(2):
                                n = 2 * sc + c
                                if n:
                                    for g2 in range(2):
                                        pe.wait_ge(solve_v[g2], v_at(sc, f"g{c}"))
                                    pe.wait_ge(chain_v, n)
                                    for h in range(HEADS):
                                        mm = pe.matmul(bank[2 if c == 0 else 6][0:HD, HD * h:HD * h + HD], GG[c][h // 4][:, h % 4, :],
                                                       STATE[n % 3][:, h, :], start=True, stop=True)
                                    mm.then_inc(chain_mm, 1)
                            for g2 in range(2):
                                pe.wait_ge(solve_v[g2], v_at(sc, "q"))
                        if ev == "ab":
                            if sc:
                                pe.wait_ge(solve_v[g], v_at(sc - 1, "y"))
                                pe.wait_ge(solve_a[g], a_at(sc - 1, "h1"))
                                pe.wait_ge(chain_v, 2 * sc)
                        need_v = {"t0": "rb", "p1": "n0", "n1": "p1", "m1": "m0", "x": "ak", "q": "rb", "y": "q"}
                        if ev in need_v:
                            pe.wait_ge(solve_v[g], v_at(sc, need_v[ev]))
                        elif ev[0] == "p":
                            pe.wait_ge(solve_a[g], a_at(sc, f"n{int(ev[1]) - 1}"))
                        elif ev[0] == "n" or ev == "m5":
                            pe.wait_ge(solve_v[g], v_at(sc, "p" + ev[1]))
                            pe.wait_ge(solve_a[g], a_at(sc, f"m{int(ev[1]) - 1}"))
                        if ev == "n1":
                            pe.wait_ge(solve_v[g], v_at(sc, "m0"))
                        if ev == "wu":
                            pe.wait_ge(solve_a[g], a_at(sc, "x"))
                        if ev == "q":
                            pe.wait_ge(solve_a[g], a_at(sc, "wu"))
                        for i in range(4):
                            h = 4 * g + i
                            ct, rows = h // 2, slice(HD * (h % 2), HD * (h % 2) + HD)
                            hc = slice(HD * (h % 2), HD * (h % 2) + HD)
                            at = slice(P * i, P * i + P)
                            V_, Bt, Kt_, Ah = (tokm[:, sc, ct, q, hc] for q in range(4))
                            a_, b_ = ahat[rows, ct, toks], bhat[rows, ct, toks]
                            k_, r_ = zr[rows, 4 + ct, toks], zr[rows, ct, toks]
                            if ev == "ab":
                                mm = pe.matmul(B[i % 2][:, P * (i // 2):P * (i // 2) + P], b_, a_, start=True, stop=True)
                            elif ev == "rb":
                                mm = pe.matmul(B[i % 2][:, P * (2 + i // 2):P * (2 + i // 2) + P], b_, r_, start=True, stop=True)
                            elif ev == "ak":
                                mm = pe.matmul(B[2 + i % 2][:, P * (i // 2):P * (i // 2) + P], k_, a_, start=True, stop=True)
                            elif ev == "rk":
                                mm = pe.matmul(B[2 + i % 2][:, P * (2 + i // 2):P * (2 + i // 2) + P], k_, r_, start=True, stop=True)
                            elif ev == "t0":
                                mm = pe.transpose(B[0][:, at], TT1[g][:, i, :], ident)
                            elif ev[0] == "p":
                                mm = pe.matmul(B[1][:, at], TT1[g][:, i, :], INV[g][:, i, :], start=True, stop=True)
                            elif ev[0] == "n":
                                mm = pe.matmul(B[2][:, at], INVT[g][:, i, :], PP[g][:, i, :], start=True, stop=True)
                            elif ev[0] == "m":
                                mm = pe.matmul(B[3][:, at], PP[g][:, i, :], INVT[g][:, i, :], start=True, stop=True)
                            elif ev == "x":
                                mm = pe.matmul(B[0][:, HD * i:HD * i + HD], AK[g][:, i, :], V_, start=True, stop=True)
                            elif ev == "wu":
                                pe.matmul(B[2][:, P * i:P * i + HD], INVT[g][:, i, :], Ah, start=True, stop=True)
                                mm = pe.matmul(B[2][:, P * i + HD:P * i + P], INVT[g][:, i, :], XX[g][:, i, :], start=True, stop=True)
                            elif ev == "q":
                                mm = pe.matmul(B[1][0:HD, at], WU[g][:, i, 0:HD], RB[g][:, i, :], start=True, stop=True)
                            elif ev[:2] == "gh":
                                c = int(ev[2])
                                cr = slice(CH * c, CH * c + CH)
                                dst = B[3 if c == 0 else 0]
                                if i == 0 and c == 0:
                                    pe.wait_ge(solve_a[g], a_at(sc, "m5"))
                                pe.matmul(dst[0:HD, HD * i:HD * i + HD], WU[g][cr, i, 0:HD], Bt[cr, :], start=True, stop=True)
                                pe.matmul(dst[0:HD, 256 + HD * i:256 + HD * i + HD], Bt[cr, :], WU[g][cr, i, HD:P], start=True, stop=False)
                                mm = pe.matmul(dst[0:HD, 256 + HD * i:256 + HD * i + HD], Kt_[cr, :], V_[cr, :], start=False, stop=True)
                            elif ev == "y":
                                pe.matmul(B[1][0:HD, at], WU[g][:, i, HD:P], RB[g][:, i, :], start=True, stop=False)
                                mm = pe.matmul(B[1][0:HD, at], V_, RK[g][:, i, :], start=False, stop=False)
                                for c in range(2):
                                    n = 2 * sc + c
                                    if n:
                                        if i == 0:
                                            pe.wait_ge(chain_v, n)
                                        mm = pe.matmul(B[1][0:HD, P * i + CH * c:P * i + CH * c + CH], STATE[n % 3][:, h, :],
                                                       QQ[g][:, i, CH * c:CH * c + CH], start=False, stop=(c == 1))
                        mm.then_inc(solve_mm[g], 1)
            for ct in range(CT):
                if ct:
                    pe.wait_ge(gn_v, 4 * ct)
                else:
                    for g in range(2):
                        pe.wait_ge(solve_v[g], v_at(TT - 1, "y"))
                pe.matmul(bank[0][:, :], const("head_ones"), ahat[:, ct, :], start=True, stop=True).then_inc(gn_mm, 1)
                pe.wait_ge(gn_v, 4 * ct + 2)
                pe.matmul(bank[1][:, :], const("head_ones"), xs[0], start=True, stop=True).then_inc(gn_mm, 1)
                pe.matmul(bank[2][:, :], lora_g[:, P * ct:P * ct + P], zr[:, 13, :], start=True, stop=True).then_inc(gn_mm, 1)
            pe.wait_ge(gn_v, 4 * CT)
            for j in range(8):
                if j >= 4:
                    pe.wait_ge((qk_a, qk_v)[j % 2], (j - 4) // 2 + 1)
                for t in range(TT):
                    pe.wait_ge(rope_done, 2 * t + 2)
                    c0 = W * (j // 4) + P * (j % 4)
                    mm = pe.transpose(bank[4 + j % 4][:, P * t:P * t + P], qkv[:, t, c0:c0 + P], ident)
                mm.then_inc(qk_mm, 1)
            pe.wait_ge(qk_a, 4)
            pe.wait_ge(qk_v, 4)

            def scores(h):
                rows = slice(HD * (h % 2), HD * (h % 2) + HD)
                if h:
                    pe.wait_ge(exp_a, TT * h)
                for i in range(TT):
                    mm = pe.matmul(S_AT[i], qT[rows, h // 2, P * i:P * i + P], kT[rows, h // 2, 0:P * (i + 1)], start=True, stop=True)
                mm.then_inc(s_mm, 1)

            scores(0)
            for h in range(HEADS):
                if h + 1 < HEADS:
                    scores(h + 1)
                pe.wait_ge(norm_v, 4 * h + 4)
                if h:
                    pe.wait_ge(pt_a, 2 * h)
                    pe.wait_ge(pt_v, 2 * h)
                for kt in range(TT):
                    for i in range(kt, TT):
                        mm = pe.transpose(PT_AT[kt][:, P * (i - kt):P * (i - kt) + P], PROB[h % 2][i][:, P * kt:P * kt + P], ident)
                mm.then_inc(pt_mm, 1)
                pe.wait_ge(pt_a, 2 * h + 2)
                pe.wait_ge(pt_v, 2 * h + 2)
                if h >= 2:
                    pe.wait_ge(pv_out, h - 1)
                for kt in range(TT):
                    mm = pe.matmul(bank[3 + 4 * (h % 2)][0:HD, P * kt:SEQ], qkv[:, kt, 2 * W + HD * h:2 * W + HD * h + HD], PROBT[h % 2][kt],
                                   start=(kt == 0), stop=(kt == TT - 1))
                mm.then_inc(pv_mm, 1)
            pe.wait_ge(pv_out, HEADS)
            for b in range(2):
                proj = ring[:, take(), :, :].rearrange("p (k a) n -> p k (a n)", k=CT)
                y_ = (ahat, bhat)[b]
                for ct in range(KT):
                    j = KT * b + ct
                    if ct % 4 == 0:
                        slot = take()
                    if j >= 2:
                        pe.wait_ge(mg_v, j - 1)
                    for k in range(CT):
                        pe.matmul(bank[j % 2][:, :], proj[:, k, P * ct:P * ct + P], y_[:, k, :], start=(k == 0), stop=(k == CT - 1))
                    for k in range(KT):
                        mm = pe.matmul(bank[2 + j % 2][:, :], ring[:, slot, k, P * (ct % 4):P * (ct % 4) + P], hT[:, k, :], start=(k == 0), stop=(k == KT - 1))
                    mm.then_inc(mg_mm, 1)
            pe.wait_ge(mg_v, 2 * KT)
            for j in range(2 * TT):
                if j % TT == 0:
                    slot = take()
                if j >= TT:
                    pe.wait_ge(x2_done, j - TT + 1)
                for k in range(KT):
                    mm = pe.matmul(bank[4 + j % TT][:, :], merged[:, k, P * (j % TT):P * (j % TT) + P], ring[:, slot, k, :], start=(k == 0), stop=(k == KT - 1))
                mm.then_inc(out_mm, 1)
            for k in range(KT):
                if k >= 2:
                    pe.wait_ge((h2t_a, h2t_v)[k % 2], k // 2)
                for t in range(TT):
                    if k == 0:
                        pe.wait_ge(h2_v, t + 1)
                    mm = pe.transpose(bank[6 + k % 2][:, t * P:t * P + P], h2[:, t, k * P:k * P + P], ident)
                mm.then_inc(h2t_mm, 1)
            pe.wait_ge(h2t_a, 4)
            pe.wait_ge(h2t_v, 4)
            pe.wait_ge(s_route_w, 64)
            for t in range(TT):
                for k in range(KT):
                    mm = pe.matmul(bank[0][:, NR * t:NR * t + NR], h2T[:, k, P * t:P * t + P], w_route[:, k, :], start=(k == 0), stop=(k == KT - 1))
            mm.then_inc(logit_mm, 1)
            pe.wait_ge(picks_v, 1)
            for t in range(TT):
                at = slice(NEXP * t, NEXP * t + NEXP)
                for t2 in range(t):
                    pe.matmul(bank[1][:, at], ones, PICKS[:, t2, :], start=(t2 == 0), stop=False)
                pe.matmul(bank[1][:, at], const("before"), PICKS[:, t, :], start=(t == 0), stop=True)
            for t in range(TT):
                mm = pe.matmul(bank[1][:, TT * NEXP:TT * NEXP + NEXP], ones, PICKS[:, t, :], start=(t == 0), stop=(t == TT - 1))
            mm.then_inc(rank_mm, 1)

            def turn_rows(b):
                for k in range(KT):
                    mm = pe.transpose(bank[k // 4][:, P * (k % 4):P * (k % 4) + P], picked[:, b, k:D:KT], ident)
                return mm

            def piece(q, b):
                for k in range(4):
                    for part in (hi, lo):
                        mm = pe.matmul(bank[2 + q % 2][:, :], xT[:, b, 4 * (q // 2) + k, :], part[:, q, k, :],
                                       start=(q < 2 and k == 0 and part is hi), stop=(q >= 2 and k == 3 and part is lo))
                return mm

            def turn_hid():
                for k in range(4):
                    mm = pe.transpose(bank[4][:, SLOTS * k:SLOTS * k + SLOTS], hid[:, k:DE:4], ident[0:SLOTS, 0:SLOTS])
                return mm

            def down(b):
                for k in range(4):
                    for n in range(2):
                        mm = pe.matmul(bank[5 + n][0:SLOTS, :], hidT[:, k, :], w2s[:, b, k, 512 * n:512 * n + 512], start=(k == 0), stop=(k == 3))
                return mm

            def do_rows(e, b):
                first_one = isinstance(e, int) and e == 0
                pe.wait_ge(rows_in[b], 16 * (e // 2 + 1) if isinstance(e, int) else 16 * (e // 2) + 16)
                if not first_one:
                    pe.wait_ge(xt_a, e)
                    pe.wait_ge(xt_v, e)
                turn_rows(b).then_inc(xt_mm, 1)

            def do_piece(e, q, b):
                if q == 0:
                    pe.wait_ge(xt_a, e + 1)
                    pe.wait_ge(xt_v, e + 1)
                    if not (isinstance(e, int) and e == 0):
                        pe.wait_ge(b_v, e)
                pe.wait_ge(lo_done, PIECES * e + q + 1)
                piece(q, b).then_inc(piece_mm, 1)

            def do_turn_hid(e):
                pe.wait_ge(hid_v, e + 1)
                pe.sem_inc(pe_past, 1)
                turn_hid().then_inc(ht_mm, 1)

            def do_down(e, b):
                pe.wait_ge(ht_a, e + 1)
                pe.wait_ge(w2_in[b], 16 * (e // 2 + 1) if isinstance(e, int) else 16 * (e // 2) + 16)
                if not (isinstance(e, int) and e == 0):
                    pe.wait_ge(y_a, e)
                    pe.wait_ge(y_v, e)
                down(b).then_inc(w2_mm, 1)

            def pe_step(e, b, last=False):
                for q in range(3):
                    do_piece(e, q, b)
                do_turn_hid(e - 1)
                do_piece(e, 3, b)
                if not last:
                    do_rows(e + 1, 1 - b)
                do_down(e - 1, 1 - b)

            do_rows(0, 0)
            for q in range(PIECES):
                do_piece(0, q, 0)
            do_rows(1, 1)
            pe_step(1, 1)
            with pe.Fori(0, (NEXP - 4) // 2) as i:
                for b in range(2):
                    pe_step(2 * i + 2 + b, b)
            pe_step(NEXP - 2, 0)
            pe_step(NEXP - 1, 1, last=True)
            do_turn_hid(NEXP - 1)
            do_down(NEXP - 1, 1)
            n_over = pe.value_load(passes[0:1, 0:1], min_val=0, max_val=MAXOV)
            with pe.If(n_over > 0):
                with pe.Fori(0, n_over) as j:
                    pe.wait_ge(ov_rows, 16 * j + 16)
                    turn_rows(0).then_inc(ov_xt, 1)
                    pe.wait_ge(ov_xe_a, j + 1)
                    pe.wait_ge(ov_xe_v, j + 1)
                    pe.wait_ge(ov_lo, 4 * j + 4)
                    for q in range(PIECES):
                        mm = piece(q, 0)
                    mm.then_inc(ov_mm, 1)
                    pe.wait_ge(ov_hid, j + 1)
                    pe.sem_inc(pe_past, 1)
                    turn_hid().then_inc(ov_ht, 1)
                    pe.wait_ge(ov_hte, j + 1)
                    pe.wait_ge(ov_w2, 16 * j + 16)
                    down(0).then_inc(ov_y, 1)


_INS = ["x", "c", "w_ada", "b_ada", "ln1_g", "ln2_g", "w_in", "mu_shift", "w0", "w_lora_up", "a0", "a_lora_up",
        "g_lora_up", "k_k", "k_a", "r_k", "lnx_g", "lnx_b", "q_norm_g", "k_norm_g", "w_br_rwkv", "w_br_moba",
        "w_out", "w_rg", "b_rg", "w_re", "b_re", "w1", "w3", "w2"]


def kernel(**inputs):
    import numpy as _np
    import concourse.bacc as _bacc
    from concourse import mybir as _mybir
    from concourse.bass_utils import run_bass_kernel_spmd as _run

    nc = _bacc.Bacc("TRN2", target_bir_lowering=False, num_devices=1)
    arrays, A = {}, {}
    for name in _INS:
        a = _np.ascontiguousarray(inputs[name])
        if name not in ("c",):
            a = a.reshape(a.shape[1:])
        if name == "r_k":
            a = a.reshape(-1)
        arrays[f"in_{name}"] = a
        A[name] = nc.dram_tensor(f"in_{name}", a.shape, _mybir.dt.from_np(a.dtype), kind="ExternalInput").ap()
    arrays["in_consts"] = CONSTS
    A["consts"] = nc.dram_tensor("in_consts", CONSTS.shape, _mybir.dt.float32, kind="ExternalInput").ap()
    out = nc.dram_tensor("out", (SEQ, D), _mybir.dt.float32, kind="ExternalOutput").ap()
    hybrid_layer(nc, A, out)
    r = _run(nc, [arrays], core_ids=[0])
    return r.results[0]["out"].reshape(1, SEQ, D)
```

```python
import numpy as np
import concourse.bass as bass
from concourse import mybir
from contextlib import ExitStack

P = 128
SEQ, D = 512, 1024
TT = SEQ // P
KT = D // P
HD = 64
HEADS = 8
W = HEADS * HD
CT = W // P
RW_COLS, ATT_COLS = 3 * W + 256, 3 * W
CH = 64
NCH = SEQ // CH
DECAY = 0.606531
LN_X_EPS, NORM_EPS = 64e-5, 1e-6
NEXP, GROUPS, EPG = 32, 4, 8
DE = D // 2
SLOTS = 64
MAXOV = 15
NPASS = NEXP + MAXOV
NEG = -1e30
BIG_INDEX = 1 << 20


def shape_constants():
    i = np.arange(P)
    r, c = i[:, None], i[None, :]
    same = (r // CH) == (c // CH)
    eye = np.eye(P)
    parts = {"ident": eye,
             "before": (r < c) * 1.0,
             "causal_t": np.concatenate([same & (r < c), same & (r <= c)], 1) * 1.0}
    for n, m in enumerate([1, 2, 4, 8, 16, 32]):
        low = (r // (2 * m) == c // (2 * m)) & (r // m % 2 == 1) & (c // m % 2 == 0)
        parts[f"level{n}"] = low + eye
        if n == 0:
            parts["level0_t"] = low.T + eye
    parts["head_ones"] = same * 1.0
    parts["scan_keep"] = np.broadcast_to((np.arange(SEQ) % CH != 0) * 1.0, (P, SEQ))
    parts["diag_mask"] = np.where(c <= r, 0.0, NEG)
    half = HD // 2
    inv_freq = 10000.0 ** (-np.arange(half, dtype=np.float32) / half)
    ang = np.arange(SEQ, dtype=np.float32)[:, None] * inv_freq[None, :].astype(np.float32)
    cos, sin = np.cos(ang), np.sin(ang)
    tiles = lambda a: a.reshape(TT, P, HD).transpose(1, 0, 2).reshape(P, TT * HD)
    parts["cos2"] = tiles(np.concatenate([cos, cos], 1))
    parts["sin2"] = tiles(np.concatenate([-sin, sin], 1))
    parts["expert_id"] = np.broadcast_to(np.arange(NEXP), (P, NEXP))
    parts["first_wins"] = np.broadcast_to(NEXP - np.arange(NEXP), (P, NEXP))
    parts["token_id"] = i[:, None] + P * np.arange(TT)[None, :]
    at, cols = {}, 0
    for k, v in parts.items():
        at[k] = (cols, v.shape[1])
        cols += v.shape[1]
    return np.ascontiguousarray(np.concatenate([np.asarray(v, np.float32) for v in parts.values()], 1)), at


CONSTS, CONST_AT = shape_constants()


def hybrid_layer(nc, A, out):
    f32, f32r, i32, u32 = mybir.dt.float32, mybir.dt.float32r, mybir.dt.int32, mybir.dt.uint32
    ALU, ACT, AX = mybir.AluOpType, mybir.ActivationFunctionType, mybir.AxisListType
    IOA = bass.IndirectOffsetOnAxis

    ctx = ExitStack()
    with ctx:
        def sem(name):
            return ctx.enter_context(nc.semaphore(name))

        def pool_of(stack):
            return lambda name, shape, dt=f32: stack.enter_context(nc.sbuf_tensor(name, shape, dt))

        keep = pool_of(ctx)
        consts = keep("consts", [P, CONSTS.shape[1]])
        x = keep("x", [P, TT, D])
        mod = keep("mod", [P, 8, 512])
        bank = [ctx.enter_context(nc.psum_tensor(f"bank{i}", [P, 512], f32)) for i in range(8)]

        def const(name, parts=P):
            at, n = CONST_AT[name]
            return consts[0:parts, at:at + n]

        ident = const("ident")

        first = ExitStack()
        sb = pool_of(first)
        NRING = 3
        ring = sb("ring", [P, NRING, KT, 512])
        hT = sb("hT", [P, KT, SEQ])
        zr = sb("zr", [P, 14, SEQ])
        ahat = sb("ahat", [P, CT, SEQ])
        bhat = sb("bhat", [P, CT, SEQ])
        qkv = sb("qkv", [P, TT, 3 * W])
        tokm = sb("tokm", [P, TT, CT, 4, P])
        cols = sb("cols", [P, 14 + 14 + 4 * 8 + 16 + 8 + 16])
        small = sb("small", [P, 64])
        eps_x = small[:, 60:61]
        prow = tokm[:, 3, 2, 0, :]
        mu, mu1 = cols[:, 0:14], cols[:, 14:28]
        col = {n: cols[:, 28 + 4 * i:32 + 4 * i] for i, n in
               enumerate(["w0", "a0", "k_k", "k_a", "r_k", "lnx_g", "lnx_b", "k_a1"])}
        bias1, ln1 = cols[:, 60:76], cols[:, 76:84]
        shift1, scale1 = cols[:, 84:92], cols[:, 92:100]
        one = small[:, 59:60]
        x_n = qkv[:, :, 0:D]
        def ada_acc(n):
            tiles_of = ((2, 2), (2, 3)) if n % 2 == 0 else ((3, 2), (3, 1)) if n < 11 else ((3, 2), (1, 3))
            return [tokm[:, t, i, :, :].rearrange("p a b -> p (a b)") for t, i in tiles_of]


        xs = [x[:, i // 2, 512 * (i % 2):512 * (i % 2) + 512] for i in range(8)]
        lora_wa = tokm[:, 3, 3, :, :].rearrange("p a b -> p (a b)")
        lora_g = xs[7]
        decay_end = sb("decay_end", [P, CT, NCH])
        decay_end8 = sb("decay_end8", [HD, HEADS, NCH])
        flat = ring[:, :, :, :].rearrange("p s k n -> p (s k n)")

        def pair(i, parts=P, n=512, off=0):
            return [flat[0:parts, 512 * (i + 12 * g) + off:512 * (i + 12 * g) + off + n].rearrange("p (h n) -> p h n", h=4)
                    for g in range(2)]

        TT1, RB, AK, RK, INV, INVT, PP, WU = (pair(i) for i in range(8))
        QQ = pair(8, HD)
        GG = [pair(9, HD, 256), pair(9, HD, 256, 256)]
        HH = [xs[3][0:HD, :], xs[4][0:HD, :]]
        XX, DE_ = pair(11, P, 256), pair(11, HD, 256, 256)
        STATE = [xs[i][0:HD, :].rearrange("p (h n) -> p h n", h=HEADS) for i in range(3)]

        gqk = zr[:, 12, 0:2 * HD].rearrange("p (a d) -> p a d", a=2)
        ssq = zr[:, 12, 128:192]
        rms_qk = zr[:, 12, 192:256]
        stat = zr[:, 12, 256:320]
        qT, kT = (tokm[:, i, :, :, :].rearrange("p c a b -> p c (a b)") for i in range(2))
        PROB = [[flat[:, 512 * (4 * b + i):512 * (4 * b + i) + P * (i + 1)] for i in range(TT)] for b in range(2)]
        PROBT = [[flat[:, 512 * (8 + 4 * b + i):512 * (8 + 4 * b + i) + P * (TT - i)] for i in range(TT)] for b in range(2)]
        S_AT = [bank[1][:, 384:512], bank[2][:, 0:256], bank[1][:, 0:384], bank[0][:, :]]
        PT_AT = [bank[4][:, :], bank[5][:, 0:384], bank[6][:, 0:256], bank[5][:, 384:512]]
        UNITS = ((3,), (2, 0), (1,))
        y_tok = qkv[:, :, 0:W]
        merged = zr
        msc = [qkv[:, i, 512:1024] for i in range(4)]

        first.close()
        PIECES = 4
        raw = keep("raw", [P, PIECES, 4, DE])
        hi = keep("hi", [P, PIECES, 4, DE], f32r)
        lo = keep("lo", [P, PIECES, 4, DE], f32r)
        w2s = keep("w2s", [P, 2, 4, D])
        picked = keep("picked", [P, 2, D])
        xT = keep("xT", [P, 2, KT, P], f32r)
        half_a, half_b, silu_a, hid = (keep(n, [SLOTS, DE]) for n in ("half_a", "half_b", "silu_a", "hid"))
        hidT = keep("hidT", [P, 4, SLOTS])
        ys = keep("ys", [SLOTS, 2, D])
        gather_at = keep("gather_at", [SLOTS, NPASS], i32)
        entry = keep("entry", [P, 2 * TT, 4], i32)
        entry_row = keep("entry_row", [P, 2 * TT], i32)
        now = keep("now", [P, 4], i32)
        passes = keep("passes", [1, 1 + MAXOV], i32)
        table = keep("table", [SLOTS, NPASS, 4], i32)
        h2 = w2s[:, 0, :, :]
        h2T = w2s[:, 1, :, :].rearrange("p a (b n) -> p (a b) n", b=2)
        ln2_bc = picked[:, 0, :]
        rt = picked[:, 1, :]
        rt2 = mod[:, 0:2, :].rearrange("p a n -> p (a n)")
        NR = GROUPS + NEXP
        w_route, b_route = rt[:, 0:KT * NR].rearrange("p (k n) -> p k n", n=NR), rt[:, 288:288 + NR]
        L = rt[:, 324:324 + TT * NR].rearrange("p (t n) -> p t n", n=NR)
        stats = [rt[:, 468 + 4 * i:472 + 4 * i] for i in range(20)]
        ln_stat = rt[:, 548:564]
        gsel, gtmp = (rt[:, 564 + 16 * i:580 + 16 * i].rearrange("p (t n) -> p t n", n=GROUPS) for i in range(2))
        counts, over, over_to, over_from = (rt[:, 596 + 32 * i:628 + 32 * i] for i in range(4))
        ones32 = rt[:, 724:756]
        pass_tmp = rt[0:1, 756:772]
        fresh = table[:, :, :]
        LE, CAND, PICK1, PICK2, PICKS, RANK, PROD = (rt2[:, 128 * i:128 * i + 128].rearrange("p (t n) -> p t n", n=NEXP) for i in range(7))
        ones = rt2[:, 896:1024]
        sum0, sum1 = w2s[:, 0, :, :], w2s[:, 1, :, :]
        h2_table = nc.dram_tensor("h2_table", [SEQ, D], f32).ap()
        slot_table = nc.dram_tensor("slot_table", [SLOTS * NPASS, 4], i32).ap()
        y_rows = nc.dram_tensor("y_rows", [2 * SEQ, D], f32).ap()

        s_const, s_x, s_c, s_cols = sem("s_const"), sem("s_x"), sem("s_c"), sem("s_cols")
        s_bias2 = sem("s_bias2")
        ring_in = [sem(f"ring_in{i}") for i in range(NRING + 2)]
        s_silu, s_prow = sem("s_silu"), sem("s_prow")
        ada_chain, ada_in, ada_mm, ada_out = sem("ada_chain"), sem("ada_in"), sem("ada_mm"), sem("ada_out")
        s_rstd, s_xn, s_xT, s_mod1 = sem("s_rstd"), sem("s_xn"), sem("s_xT"), sem("s_mod1")
        s_ssq, s_xt, s_hT = sem("s_ssq"), sem("s_xt"), sem("s_hT")
        z_mm, z_scaled, z_shifted = sem("z_mm"), sem("z_scaled"), sem("z_shifted")
        att_mm, att_out = sem("att_mm"), sem("att_out")
        s_mu1, s_var1, s_rstd1 = sem("s_mu1"), sem("s_var1"), sem("s_rstd1")
        dve_chain, pool_chain = sem("dve_chain"), sem("pool_chain")
        s_done = sem("s_done")
        mg_mm, mg_sig, mg_v, out_mm, x2_done = sem("mg_mm"), sem("mg_sig"), sem("mg_v"), sem("out_mm"), sem("x2_done")
        s_gqk, ssq_qk, sqrt_qk, rstd_qk, rope_done = sem("s_gqk"), sem("ssq_qk"), sem("sqrt_qk"), sem("rstd_qk"), sem("rope_done")
        qk_mm, qk_a = sem("qk_mm"), sem("qk_a")
        s_mm, max_v, exp_a = sem("s_mm"), sem("max_v"), sem("exp_a")
        yt_mm, yt_v = sem("yt_mm"), sem("yt_v")
        pt_mm, pt_v, pt_a, pv_mm, pv_out = sem("pt_mm"), sem("pt_v"), sem("pt_a"), sem("pv_mm"), sem("pv_out")
        s_ln2, s_route_w, ssq2, var2, sqrt2, h2_v = (sem(n) for n in (
            "s_ln2", "s_route_w", "ssq2", "var2", "sqrt2", "h2_v"))
        h2_stored, h2t_mm, h2t_a, h2t_v, logit_mm, picks_v, rank_mm = (sem(n) for n in (
            "h2_stored", "h2t_mm", "h2t_a", "h2t_v", "logit_mm", "picks_v", "rank_mm"))
        exp_in, exp_out, fresh_v, fresh_in, entry_v, entry_in, table_in, gather_v = (sem(n) for n in (
            "exp_in", "exp_out", "fresh_v", "fresh_in", "entry_v", "entry_in", "table_in", "gather_v"))
        raw_in = [sem(f"raw_in{q}") for q in range(4)]
        w2_in = [sem(f"w2_in{b}") for b in range(2)]
        hi_done, lo_done, piece_mm = sem("hi_done"), sem("lo_done"), sem("piece_mm")
        now_p, rows_in, xt_mm, xt_a, xt_v = sem("now_p"), [sem(f"rows_in{b}") for b in range(2)], sem("xt_mm"), sem("xt_a"), sem("xt_v")
        ab_a, a_v, silu_done, b_v, hid_v, ht_mm, ht_a, w2_mm = (sem(n) for n in (
            "ab_a", "a_v", "silu_done", "b_v", "hid_v", "ht_mm", "ht_a", "w2_mm"))
        y_a, y_v, y_out = sem("y_a"), sem("y_v"), [sem(f"y_out{b}") for b in range(2)]
        ov_ready, ov_in, ov_w2, ov_rows, ov_xt, ov_xe_a, ov_xe_v = (sem(n) for n in (
            "ov_ready", "ov_in", "ov_w2", "ov_rows", "ov_xt", "ov_xe_a", "ov_xe_v"))
        ov_hi, ov_lo, ov_mm, ov_ab, ov_a, ov_silu, ov_hid, ov_ht, ov_hte, ov_y, ov_ys, ov_out = (sem(n) for n in (
            "ov_hi", "ov_lo", "ov_mm", "ov_ab", "ov_a", "ov_silu", "ov_hid", "ov_ht", "ov_hte", "ov_y", "ov_ys", "ov_out"))
        s_sum, s_final = sem("s_sum"), sem("s_final")
        past = sem("past")
        s_lora_w, s_act_in = sem("s_lora_w"), sem("s_act_in")
        lora_mm, lora_act, sq_act, ss_mm, ss_act = sem("lora_mm"), sem("lora_act"), sem("sq_act"), sem("ss_mm"), sem("ss_act")
        scan_done, exp_act, eprev_in = sem("scan_done"), sem("exp_act"), sem("eprev_in")
        bonus_in, bonus_mm, forms_done = sem("bonus_in"), sem("bonus_mm"), sem("forms_done")
        turn_mm, turn_v, turn_a, prep_done = sem("turn_mm"), sem("turn_v"), sem("turn_a"), sem("prep_done")
        solve_mm, solve_v, solve_a = ([sem(f"{n}{g}") for g in range(2)] for n in ("solve_mm", "solve_v", "solve_a"))
        chain_mm, chain_v, s_de8 = sem("chain_mm"), sem("chain_v"), sem("s_de8")
        gn_mm, gn_v, gn_a = sem("gn_mm"), sem("gn_v"), sem("gn_a")

        w_in = A["w_in"].rearrange("(k p) n -> p k n", p=P)
        w_ada = A["w_ada"].rearrange("(k p) n -> p k n", p=P)
        ada_items = [(w_ada[:, :, 512 * j:512 * j + 512], ada_in, 2 * j + 2) for j in range(12)]
        z_items = [(w_in[:, :, 3 * W:RW_COLS], z_mm, 2)]
        z_items += [(w_in[:, :, 512 * j:512 * j + 512], z_mm, 4 * j + 6) for j in range(3)]
        att_items = [(w_in[:, :, RW_COLS + 512 * j:RW_COLS + 512 * j + 512], att_mm, TT * (j + 1)) for j in range(3)]
        items, first_slots, at_of = [], [], {"ada": [], "z": [], "att": []}
        of = {"ada": ada_items, "z": z_items, "att": att_items}
        for kind, slot in [("ada", 0), ("ada", 1), ("ada", 2), ("ada", 3), ("z", 0), ("z", 1), ("ada", 2), ("ada", 3), ("z", 0), ("ada", 2),
                           ("ada", 3), ("z", 1), ("ada", 2), ("ada", 3), ("att", 0), ("ada", 2), ("att", 1), ("ada", 2), ("att", 0)]:
            items.append(of[kind][len(at_of[kind])])
            at_of[kind].append(len(items) - 1)
            first_slots.append(slot)
        ADA_AT, Z_AT, ATT_AT = at_of["ada"], at_of["z"], at_of["att"]
        w_gate = w_in[:, :, RW_COLS + ATT_COLS:]
        N_BEFORE_MERGE = len(items)
        for b, name in enumerate(("w_br_rwkv", "w_br_moba")):
            items += [(A[name].rearrange("(k p) n -> p k n", p=P), mg_mm, KT * (b + 1))]
            items += [(w_gate[:, :, D * b + 512 * j:D * b + 512 * j + 512], mg_mm, KT * b + 4 * (j + 1)) for j in range(2)]
        items += [(A["w_out"].rearrange("(k p) n -> p k n", p=P)[:, :, 512 * j:512 * j + 512], out_mm, TT * (j + 1)) for j in range(2)]
        slot_of = first_slots + [2, 4, 0, 1, 3, 4, 0, 2]
        nth_in_slot = [slot_of[:i].count(v) + 1 for i, v in enumerate(slot_of)]
        last_in_slot = [max([j for j in range(i) if slot_of[j] == v], default=None) for i, v in enumerate(slot_of)]

        def slot_view(i, k=KT):
            v = slot_of[i]
            flat_slot = (ring[:, v, :, :].rearrange("p k n -> p (k n)") if v < NRING else
                         tokm[:, (0, 2)[v - NRING]:(2, 4)[v - NRING], :, :, :].rearrange("p t c a b -> p (t c a b)"))
            return flat_slot.rearrange("p (k n) -> p k n", k=k)

        Z_TILES = [12, 13] + list(range(12))

        block = ctx.enter_context(nc.Block())

        @block.sync
        def _(sp):
            sp.dma_start(x[:, :, :], A["x"].rearrange("(t p) d -> p t d", p=P)).then_inc(s_x, 16)
            sp.wait_ge(s_c, 16 * 12)
            for i, (src, _, _) in enumerate(items):
                before = last_in_slot[i]
                if before is not None:
                    sp.wait_ge(items[before][1], items[before][2])
                if i == Z_AT[1]:
                    sp.wait_ge(s_prow, 1)
                    sp.dma_start(lora_wa[0:64, :], A["w_lora_up"]).then_inc(s_lora_w, 16)
                    sp.dma_start(lora_wa[64:128, :], A["a_lora_up"]).then_inc(s_lora_w, 16)
                    sp.wait_ge(s_xn, TT)
                    sp.dma_start(lora_g, A["g_lora_up"]).then_inc(s_lora_w, 16)
                if i == N_BEFORE_MERGE:
                    sp.wait_ge(gn_v, 3 * CT)
                if i == N_BEFORE_MERGE + 2:
                    sp.wait_ge(rope_done, 2 * TT)
                    sp.dma_start(x[:, :, :], A["x"].rearrange("(t p) d -> p t d", p=P)).then_inc(s_x, 16)
                    sp.wait_ge(pv_out, HEADS)
                k, n = src.shape[1:]
                dst = slot_view(i)[:, 0:k, 0:n] if n <= 512 else slot_view(i, k)
                sp.dma_start(dst, src).then_inc(ring_in[slot_of[i]], 16)
            sp.wait_ge(x2_done, 2 * TT)
            sp.dma_start(ln2_bc, A["ln2_g"].partition_broadcast(P)).then_inc(s_ln2, 16)
            sp.dma_start(w_route[:, :, 0:GROUPS], A["w_rg"].rearrange("(k p) n -> p k n", p=P)).then_inc(s_route_w, 16)
            sp.dma_start(w_route[:, :, GROUPS:NR], A["w_re"].rearrange("(k p) n -> p k n", p=P)).then_inc(s_route_w, 16)
            sp.dma_start(b_route[:, 0:GROUPS], A["b_rg"].partition_broadcast(P)).then_inc(s_route_w, 16)
            sp.dma_start(b_route[:, GROUPS:NR], A["b_re"].partition_broadcast(P)).then_inc(s_route_w, 16)
            w13 = [A[n].rearrange("e (p k) n -> e p k n", k=KT)[:, :, 4 * half:4 * half + 4, :] for half in range(2) for n in ("w1", "w3")]
            w2_src = A["w2"].rearrange("e (p k) n -> e p k n", k=4)

            def load_pieces(e, pieces=range(PIECES)):
                for q in pieces:
                    if not (isinstance(e, int) and e == 0):
                        sp.wait_ge(lo_done, PIECES * e + q - 3)
                    src = w13[q][e] if isinstance(e, int) else w13[q][bass.ds(e, 1)].rearrange("e p k n -> (e p) k n")
                    sp.dma_start(raw[:, q, :, :], src).then_inc(raw_in[q], 16)

            def load_w2(e, b):
                if not (isinstance(e, int) and e < 2):
                    sp.wait_ge(w2_mm, e - 1)
                src = w2_src[e] if isinstance(e, int) else w2_src[bass.ds(e, 1)].rearrange("e p k n -> (e p) k n")
                sp.dma_start(w2s[:, b, :, :], src).then_inc(w2_in[b], 16)

            load_pieces(0)
            for t in range(TT):
                sp.wait_ge(h2_v, t + 1)
                sp.dma_start(h2_table[P * t:P * t + P, :], h2[:, t, :]).then_inc(h2_stored, 16)
            sp.wait_ge(h2_stored, 16 * TT)
            sp.wait_ge(logit_mm, 1)

            def load_step(e, b):
                load_pieces(e, range(3))
                load_w2(e - 1, 1 - b)
                load_pieces(e, (3,))

            load_step(1, 1)
            load_step(2, 0)
            with sp.Fori(0, (NEXP - 4) // 2) as i:
                for b in range(2):
                    load_step(2 * i + 3 + b, 1 - b)
            load_step(NEXP - 1, 1)
            load_w2(NEXP - 1, 1)
            n_over = sp.value_load(passes[0:1, 0:1], min_val=0, max_val=MAXOV)
            with sp.If(n_over > 0):
                with sp.Fori(0, n_over) as j:
                    sp.wait_ge(ov_ready, j + 1)
                    e = sp.value_load(passes[0:1, bass.ds(j + 1, 1)], min_val=0, max_val=NEXP - 1)
                    for q in range(PIECES):
                        sp.dma_start(raw[:, q, :, :], w13[q][bass.ds(e, 1)].rearrange("e p k n -> (e p) k n")).then_inc(ov_in, 16)
                    sp.dma_start(w2s[:, 0, :, :], w2_src[bass.ds(e, 1)].rearrange("e p k n -> (e p) k n")).then_inc(ov_w2, 16)
            sp.wait_ge(s_sum, 1)
            both = y_rows.rearrange("(k t p) d -> k p t d", k=2, p=P)
            for k in range(2):
                sp.dma_start((sum0, sum1)[k], both[k]).then_inc(s_sum, 16)
            for t in range(TT):
                sp.wait_ge(s_final, t + 1)
                sp.dma_start(out[P * t:P * t + P, :], x[:, t, :]).then_inc(s_done, 16)
            sp.wait_ge(s_done, 16 * TT)

        def sum_bank(n):
            return bank[2 if n >= 10 else n % 2][:, :]

        ADA_AFTER = (2, 4, 6, 8, 10, 12)

        def ring_wait(eng, i):
            eng.wait_ge(ring_in[slot_of[i]], 16 * nth_in_slot[i])

        MM_EVENTS = ["ab", "rb", "ak", "rk", "t0"] + [f"{x}{l}" for l in range(1, 6) for x in "pnm" if (x, l) != ("n", 5)]
        MM_EVENTS += ["x", "wu", "q", "gh0", "gh1", "y"]
        V_EVENTS = ["ab", "tt", "rb", "ak", "rk", "n0", "m0"] + [f"p{l}" for l in range(1, 6)] + ["q", "d0", "g0", "d1", "g1", "y"]
        A_EVENTS = [f"{x}{l}" for l in range(1, 6) for x in "nm" if (x, l) != ("n", 5)] + ["x", "wu", "h0", "h1"]
        mm_at = lambda sc, e: len(MM_EVENTS) * sc + MM_EVENTS.index(e) + 1
        v_at = lambda sc, e: len(V_EVENTS) * sc + V_EVENTS.index(e) + 1
        a_at = lambda sc, e: len(A_EVENTS) * sc + A_EVENTS.index(e) + 1

        def weight_of(e):
            w = table[0:SLOTS, :, 2].bitcast(f32)
            return w[:, e:e + 1] if isinstance(e, int) else w[:, bass.ds(e, 1)]

        def turned(b):
            return bank[b][:, :].rearrange("p (k n) -> p k n", k=KT)

        @block.scalar
        def _(act):
            act.dma_start(ident, A["consts"][:, 0:P]).then_inc(s_c, 16)
            at = 0
            rows_of = [(A["c"][0], 8), (A["mu_shift"], 14)] + [(A[n], CT) for n in ("w0", "a0", "k_k", "k_a", "r_k", "lnx_g", "lnx_b")]
            rows_of += [(A["b_ada"][0:2 * D], 2 * KT), (A["ln1_g"], KT)]
            for src, k in rows_of:
                act.dma_start(prow[at:at + k, :], src.rearrange("(k p) -> k p", p=P)).then_inc(s_c, 16)
                at += k
            act.dma_start(mod[0:1, :, :].rearrange("p a b -> p (a b)"), A["b_ada"][2 * D:6 * D].rearrange("(a n) -> a n", a=1)).then_inc(s_bias2, 16)
            act.wait_ge(s_cols, 1)
            act.activation(small[:, 8:8 + KT], small[:, 0:KT], ACT.Silu).then_inc(s_silu, 1)
            act.wait_ge(s_x, 16)
            for t in range(TT):
                act.activation(x_n[:, t, :], x[:, t, :], ACT.Square,
                               accum_out=small[:, 16 + t:17 + t]).then_inc(s_ssq, 1)
            act.wait_ge(s_var1, 1)
            act.activation(small[:, 28:32], small[:, 20:24], ACT.Sqrt).then_inc(s_rstd1, 1)
            act.wait_ge(s_rstd, 1)
            for t in range(TT):
                act.activation(x_n[:, t, :], x[:, t, :], ACT.Copy, scale=small[:, 24 + t:25 + t]).then_inc(s_xn, 1)
            act.dma_start(consts[:, P:], A["consts"][:, P:]).then_inc(s_const, 16)
            for k in range(KT):
                act.wait_ge(s_xt, k + 1)
                act.activation(hT[:, k, :], bank[2 + k % 2][:, :], ACT.Copy).then_inc(s_xT, 1)
            act.wait_ge(s_mod1, 1)
            act.wait_ge(s_xT, KT)
            for k in range(0, KT, 2):
                act.activation(hT[:, k, :], hT[:, k, :], ACT.Identity, scale=scale1[:, k:k + 1], bias=shift1[:, k:k + 1]).then_inc(s_hT, 1)
            act.wait_ge(s_mu1, 2)
            for j, ct in enumerate(Z_TILES):
                act.wait_ge(z_mm, j + 1)
                act.activation(zr[:, ct, :], bank[4 + j % 4][:, :], ACT.Copy, scale=mu1[:, ct:ct + 1]).then_inc(z_scaled, 1)
                if j == 1:
                    act.wait_ge(z_shifted, 2)
                    act.activation(zr[0:64, 12, :], zr[0:64, 12, :], ACT.Tanh)
                    act.activation(zr[:, 13, :], zr[:, 13, :], ACT.Sigmoid).then_inc(s_act_in, 1)

            def att_copy(j):
                act.wait_ge(att_mm, j + 1)
                act.activation(qkv[:, j % TT, 512 * (j // TT):512 * (j // TT) + 512], bank[6 + j % 2][:, :], ACT.Copy).then_inc(att_out, 1)

            for ct in range(CT):
                r_, k_, c1 = zr[:, ct, :], zr[:, 4 + ct, :], slice(ct, ct + 1)
                if ct:
                    act.wait_ge(prep_done, ct)
                act.wait_ge(lora_mm, 2 * ct + 1)
                act.activation(xs[0], bank[0][:, :], ACT.Sigmoid, bias=col["w0"][:, c1]).then_inc(lora_act, 1)
                act.wait_ge(lora_mm, 2 * ct + 2)
                act.activation(xs[1], bank[1][:, :], ACT.Sigmoid, bias=col["a0"][:, c1]).then_inc(lora_act, 1)
                act.activation(xs[2], k_, ACT.Square, scale=col["k_k"][:, c1]).then_inc(sq_act, 1)
                act.wait_ge(scan_done, ct + 1)
                act.activation(xs[6], xs[3], ACT.Exp, scale=-DECAY).then_inc(exp_act, 1)
                act.wait_ge(eprev_in, ct + 1)
                act.activation(xs[0], xs[0], ACT.Exp, scale=-DECAY).then_inc(exp_act, 1)
                act.activation(xs[3], xs[3], ACT.Exp, scale=DECAY).then_inc(exp_act, 1)
                act.wait_ge(ss_mm, ct + 1)
                act.activation(xs[2], bank[2][:, :], ACT.Sqrt).then_inc(ss_act, 1)
                att_copy(3 * ct)
                att_copy(3 * ct + 1)
                for t in (1, 3):
                    act.wait_ge(turn_mm, TT * ct + t + 1)
                    act.activation(tokm[:, t, ct, :, :].rearrange("p a b -> p (a b)"), bank[5][:, :], ACT.Copy).then_inc(turn_a, 1)
                att_copy(3 * ct + 2)
            for sc in range(TT):
                if sc == 2:
                    act.wait_ge(ssq_qk, 1)
                    act.activation(rms_qk, ssq, ACT.Sqrt).then_inc(sqrt_qk, 1)
                for ev in A_EVENTS:
                    for g in range(2):
                        B = bank[4 * g:4 * g + 4]
                        act.wait_ge(solve_mm[g], mm_at(sc, ev if ev[0] != "h" else "gh" + ev[1]))
                        if ev[0] == "h":
                            c = int(ev[1])
                            if c == 1:
                                act.wait_ge(solve_a[g], a_at(sc, "h0"))
                            if sc and c == 0:
                                act.wait_ge(chain_v, 2 * sc)
                            src, dst = B[3 if c == 0 else 0][0:HD, 256:512], HH[c][:, 256 * g:256 * g + 256]
                        else:
                            src, dst = {"n": (B[2], INV), "m": (B[3], INVT), "x": (B[0], XX), "w": (B[2], WU)}[ev[0]]
                            n = 256 if ev == "x" else 512
                            src, dst = src[:, 0:n], dst[g].rearrange("p h n -> p (h n)")
                        act.activation(dst, src, ACT.Copy).then_inc(solve_a[g], 1)
            for ct in range(CT):
                act.wait_ge(gn_mm, CT + ct + 1)
                act.activation(xs[ct], bank[ct][:, :], ACT.Sqrt, bias=eps_x, scale=1.0 / HD).then_inc(gn_a, 1)
            for j in range(8):
                act.wait_ge(qk_mm, j + 1)
                act.activation((qT, kT)[j // 4][:, j % 4, :], bank[4 + j % 4][:, :], ACT.Copy).then_inc(qk_a, 1)

            def exps(h):
                if h >= 2:
                    act.wait_ge(pt_mm, h - 1)
                act.wait_ge(max_v, h + 1)
                for unit in UNITS:
                    for i in unit:
                        act.activation(PROB[h % 2][i], S_AT[i], ACT.Exp, bias=stat[:, 4 * (h % 2) + i:4 * (h % 2) + i + 1], scale=HD ** -0.5,
                                       accum_out=stat[:, 8 + 4 * (h % 4) + i:9 + 4 * (h % 4) + i]).then_inc(exp_a, 1)

            exps(0)
            for h in range(HEADS):
                if h + 1 < HEADS:
                    exps(h + 1)
                act.wait_ge(pt_mm, h + 1)
                if h >= 2:
                    act.wait_ge(pv_mm, h - 1)
                for i in (0, 2):
                    act.activation(PROBT[h % 2][i], PT_AT[i], ACT.Copy).then_inc(pt_a, 1)
            for j in range(2 * KT):
                act.wait_ge(mg_mm, j + 1)
                if j >= 2:
                    act.wait_ge(mg_v, j - 1)
                act.activation(msc[j % 2], bank[2 + j % 2][:, :], ACT.Sigmoid).then_inc(mg_sig, 1)
            act.wait_ge(x2_done, 2 * TT)
            for t in range(TT):
                act.activation(h2[:, t, :], x[:, t, :], ACT.Square, accum_out=ln_stat[:, t:t + 1]).then_inc(ssq2, 1)
            act.wait_ge(var2, 1)
            act.activation(ln_stat[:, 8:12], ln_stat[:, 4:8], ACT.Sqrt).then_inc(sqrt2, 1)
            for k in range(0, KT, 2):
                act.wait_ge(h2t_mm, k + 1)
                act.activation(h2T[:, k, :], bank[6][:, :], ACT.Copy).then_inc(h2t_a, 1)
            for i, n in ((1, 16), (2, 4)):
                act.wait_ge(exp_in, i)
                ap = gtmp if i == 1 else stats[5]
                act.activation(ap, ap, ACT.Exp).then_inc(exp_out, 1)

            def split_hi(q):
                return act.activation(hi[:, q, :, :], raw[:, q, :, :], ACT.Copy)

            def hi_piece(e, q):
                act.wait_ge(raw_in[q], 16 * e + 16)
                if not (isinstance(e, int) and e == 0):
                    act.wait_ge(piece_mm, PIECES * e + q - 3)
                split_hi(q).then_inc(hi_done, 1)

            def y_half(e, b):
                act.wait_ge(w2_mm, e + 1)
                if not (isinstance(e, int) and e < 2):
                    act.wait_ge(y_out[b], 16 * (e // 2))
                act.activation(ys[:, b, 0:512], bank[5][0:SLOTS, :], ACT.Copy, scale=weight_of(e)).then_inc(y_a, 1)

            def turn_x(e, b):
                act.wait_ge(xt_mm, e + 1)
                act.activation(xT[:, b, :, 0:SLOTS], turned(b), ACT.Copy).then_inc(xt_a, 1)

            def halves(e):
                act.wait_ge(piece_mm, PIECES * e + 4)
                if not (isinstance(e, int) and e == 0):
                    act.wait_ge(b_v, e)
                act.activation(half_a[:, :], bank[2][SLOTS:P, :], ACT.Copy).then_inc(ab_a, 1)
                act.activation(half_b[:, :], bank[3][SLOTS:P, :], ACT.Copy).then_inc(ab_a, 1)
                act.wait_ge(a_v, e + 1)
                act.activation(silu_a[:, :], half_a[:, :], ACT.Silu).then_inc(silu_done, 1)

            def turn_hid(e):
                act.wait_ge(ht_mm, e + 1)
                act.activation(hidT[:, :, :].rearrange("p k n -> p (k n)"), bank[4][:, 0:4 * SLOTS], ACT.Copy).then_inc(ht_a, 1)

            def act_step(e, b, last=False, head=0):
                if head >= 2:
                    y_half(e - 2, b)
                if not last:
                    hi_piece(e + 1, 0)
                    hi_piece(e + 1, 1)
                if head >= 1:
                    turn_hid(e - 1)
                if not last:
                    hi_piece(e + 1, 2)
                    turn_x(e + 1, 1 - b)
                    hi_piece(e + 1, 3)
                halves(e)

            for q in range(PIECES):
                hi_piece(0, q)
            turn_x(0, 0)
            act_step(0, 0)
            act_step(1, 1, head=1)
            act_step(2, 0, head=2)
            act_step(3, 1, head=2)
            with act.Fori(0, (NEXP - 6) // 2) as i:
                for b in range(2):
                    act_step(2 * i + 4 + b, b, head=2)
            act_step(NEXP - 2, 0, head=2)
            act_step(NEXP - 1, 1, head=2, last=True)
            y_half(NEXP - 2, 0)
            turn_hid(NEXP - 1)
            y_half(NEXP - 1, 1)
            n_over = act.value_load(passes[0:1, 0:1], min_val=0, max_val=MAXOV)
            with act.If(n_over > 0):
                with act.Fori(0, n_over) as j:
                    act.wait_ge(ov_ready, j + 1)
                    act.wait_ge(ov_in, 64 * j + 64)
                    for q in range(PIECES):
                        split_hi(q).then_inc(ov_hi, 1)
                    act.wait_ge(ov_xt, j + 1)
                    act.activation(xT[:, 0, :, 0:SLOTS], turned(0), ACT.Copy).then_inc(ov_xe_a, 1)
                    act.wait_ge(ov_mm, j + 1)
                    act.activation(half_a[:, :], bank[2][SLOTS:P, :], ACT.Copy).then_inc(ov_ab, 1)
                    act.activation(half_b[:, :], bank[3][SLOTS:P, :], ACT.Copy).then_inc(ov_ab, 1)
                    act.wait_ge(ov_a, j + 1)
                    act.activation(silu_a[:, :], half_a[:, :], ACT.Silu).then_inc(ov_silu, 1)
                    act.wait_ge(ov_ht, j + 1)
                    act.activation(hidT[:, :, :].rearrange("p k n -> p (k n)"), bank[4][:, 0:4 * SLOTS], ACT.Copy).then_inc(ov_hte, 1)
                    act.wait_ge(ov_y, j + 1)
                    act.activation(ys[:, 0, 0:512], bank[5][0:SLOTS, :], ACT.Copy, scale=weight_of(NEXP + j)).then_inc(ov_ys, 1)


        @block.gpsimd
        def _(pool):
            made = [0]

            def seq(ins):
                made[0] += 1
                ins.then_inc(pool_chain, 1)
                pool.wait_ge(pool_chain, made[0])

            pool.wait_ge(prep_done, CT)
            pool.wait_ge(lora_mm, 2 * CT)
            pool.dma_start(gqk[:, 0, :], A["q_norm_g"].partition_broadcast(P)).then_inc(s_gqk, 16)
            pool.dma_start(gqk[:, 1, :], A["k_norm_g"].partition_broadcast(P)).then_inc(s_gqk, 16)
            pool.wait_ge(att_out, 12)
            heads = lambda ap: ap.rearrange("p (h d) -> p h d", d=HD)
            for i in range(2 * TT):
                t, q = i // 2, heads(qkv[:, i // 2, W * (i % 2):W * (i % 2) + W])
                seq(pool.tensor_tensor(heads(xs[5]), q, q, ALU.mult))
                n = HD // 2
                while n >= 1:
                    a = heads(xs[5])
                    dst = a[:, :, 0:n] if n > 1 else ssq[:, 8 * i:8 * i + 8].unsqueeze(2)
                    seq(pool.tensor_tensor(dst, a[:, :, 0:n], a[:, :, n:2 * n], ALU.add))
                    n //= 2
            pool.tensor_scalar(ssq, ssq, 1.0 / HD, NORM_EPS, ALU.mult, ALU.add).then_inc(ssq_qk, 1)
            pool.wait_ge(rstd_qk, 1)
            pool.wait_ge(s_gqk, 32)
            for i in range(2 * TT):
                t, q = i // 2, heads(qkv[:, i // 2, W * (i % 2):W * (i % 2) + W])
                bc = lambda ap: ap.unsqueeze(1).to_broadcast([P, HEADS, ap.shape[1]])
                cos2, sin2 = (bc(const(n)[:, HD * t:HD * t + HD]) for n in ("cos2", "sin2"))
                seq(pool.tensor_tensor(q, q, ssq[:, 8 * i:8 * i + 8].unsqueeze(2).to_broadcast([P, HEADS, HD]), ALU.mult))
                seq(pool.tensor_tensor(q, q, bc(gqk[:, i % 2, :]), ALU.mult))
                half = HD // 2
                t1 = heads(xs[5])
                pool.tensor_tensor(t1[:, :, 0:half], q[:, :, half:HD], sin2[:, :, 0:half], ALU.mult)
                seq(pool.tensor_tensor(t1[:, :, half:HD], q[:, :, 0:half], sin2[:, :, half:HD], ALU.mult))
                seq(pool.tensor_tensor(q, q, cos2, ALU.mult))
                pool.tensor_tensor(q, q, t1, ALU.add).then_inc(rope_done, 1)
                pool.wait_ge(rope_done, i + 1)

            pool.wait_ge(x2_done, 2 * TT)
            pool.memset(fresh, BIG_INDEX).then_inc(fresh_v, 1)
            pool.wait_ge(fresh_v, 1)
            pool.dma_start(slot_table.rearrange("(p n) c -> p n c", p=SLOTS), fresh).then_inc(fresh_in, 16)
            pool.wait_ge(fresh_in, 16)
            pool.wait_ge(entry_v, 1)
            for j in range(2 * TT):
                pool.indirect_dma_start(slot_table, IOA(entry_row[:, j:j + 1].bitcast(u32), 0), entry[:, j, :], None,
                                        bounds_check=SLOTS * NPASS - 1, oob_is_err=False).then_inc(entry_in, 16)
            pool.wait_ge(entry_in, 16 * 2 * TT)
            pool.dma_start(table[:, :, :], slot_table.rearrange("(p n) c -> p n c", p=SLOTS)).then_inc(table_in, 16)
            pool.wait_ge(gather_v, 1)
            pool.wait_ge(h2_stored, 16 * TT)

            def current(src, at, e):
                n = src.shape[0]
                pool.sem_inc(past, 1)
                pool.tensor_copy(now[0:n, at:at + 1], src[:, e:e + 1] if isinstance(e, int) else src[:, bass.ds(e, 1)]).then_inc(now_p, 1)

            def gather(b, e, sem_):
                current(gather_at[:, :], b, e)
                pool.wait_ge(now_p, now_n(e, 0))
                pool.sem_inc(past, 1)
                pool.indirect_dma_start(picked[0:SLOTS, b, :], None, h2_table, IOA(now[0:SLOTS, b:b + 1].bitcast(u32), 0),
                                        bounds_check=SEQ - 1, oob_is_err=False).then_inc(sem_, 16)

            def scatter(b, e, sem_):
                current(table[0:SLOTS, :, 1], 2 + b, e)
                pool.wait_ge(now_p, now_n(e, 1))
                pool.sem_inc(past, 1)
                pool.indirect_dma_start(y_rows, IOA(now[0:SLOTS, 2 + b:3 + b].bitcast(u32), 0), ys[:, b, :], None,
                                        bounds_check=2 * SEQ - 1, oob_is_err=False).then_inc(sem_, 16)

            def now_n(e, scattering):
                if scattering:
                    return 2 * e + 6 if not isinstance(e, int) or e < NEXP - 4 else NEXP + e + 1
                return e + 1 if isinstance(e, int) and e < 4 else 2 * e - 3

            pool.memset(picked[:, :, :], 0.0).then_inc(gather_v, 1)
            pool.wait_ge(gather_v, 2)
            gather(0, 0, rows_in[0])
            gather(1, 1, rows_in[1])

            def gather_next(e, b):
                pool.wait_ge(xt_mm, e + 1)
                gather(b, e + 2, rows_in[b])

            def scatter_last(e, b):
                pool.wait_ge(y_a, e + 1)
                pool.wait_ge(y_v, e + 1)
                scatter(b, e, y_out[b])

            gather_next(0, 0)
            gather_next(1, 1)
            with pool.Fori(0, (NEXP - 4) // 2) as i:
                for b in range(2):
                    gather_next(2 * i + 2 + b, b)
                    scatter_last(2 * i + b, b)
            for e in range(NEXP - 4, NEXP):
                scatter_last(e, e % 2)
            for b in range(2):
                pool.wait_ge(y_out[b], 16 * NEXP // 2)
            n_over = pool.value_load(passes[0:1, 0:1], min_val=0, max_val=MAXOV)
            with pool.If(n_over > 0):
                with pool.Fori(0, n_over) as j:
                    pool.wait_ge(ov_ready, j + 1)
                    current(gather_at[:, :], 0, j + NEXP)
                    pool.wait_ge(now_p, 2 * j + 2 * NEXP + 1)
                    pool.sem_inc(past, 1)
                    pool.indirect_dma_start(picked[0:SLOTS, 0, :], None, h2_table, IOA(now[0:SLOTS, 0:1].bitcast(u32), 0),
                                            bounds_check=SEQ - 1, oob_is_err=False).then_inc(ov_rows, 16)
                    pool.wait_ge(ov_ys, 2 * j + 2)
                    current(table[0:SLOTS, :, 1], 2, j + NEXP)
                    pool.wait_ge(now_p, 2 * j + 2 * NEXP + 2)
                    pool.sem_inc(past, 1)
                    pool.indirect_dma_start(y_rows, IOA(now[0:SLOTS, 2:3].bitcast(u32), 0), ys[:, 0, :], None,
                                            bounds_check=2 * SEQ - 1, oob_is_err=False).then_inc(ov_out, 16)
                    pool.wait_ge(ov_out, 16 * j + 16)
                    pool.sem_inc(ov_ready, 1)
            pool.sem_inc(s_sum, 1)

        @block.vector
        def _(dve):
            made = [0]

            def seq(ins):
                made[0] += 1
                ins.then_inc(dve_chain, 1)
                dve.wait_ge(dve_chain, made[0])

            dve.wait_ge(s_prow, 1)
            dve.memset(eps_x, LN_X_EPS)
            dve.memset(one, 1.0)
            dve.tensor_copy(small[:, 0:8], bank[7][:, 0:8])
            dve.tensor_copy(mu, bank[7][:, 8:22])
            dve.tensor_copy(cols[:, 28:56], bank[7][:, 22:50])
            dve.tensor_copy(cols[:, 60:84], bank[7][:, 50:74]).then_inc(s_cols, 1)

            def ada_item(n):
                ring_wait(dve, ADA_AT[n])
                if n >= 2:
                    dve.wait_ge(ada_mm, n - 1)
                w = slot_view(ADA_AT[n])
                for k in range(KT):
                    acc, c_ = ada_acc(n)[k % 2], small[:, 8 + k:9 + k]
                    if k < 2:
                        ins = dve.tensor_scalar(acc, w[:, k, :], c_, None, ALU.mult)
                    else:
                        dve.wait_ge(ada_chain, (KT - 2) * n + k - 1)
                        ins = dve.scalar_tensor_tensor(acc, w[:, k, :], c_, acc, ALU.mult, ALU.add)
                    ins.then_inc(ada_chain if k < KT - 2 else ada_in, 1)

            def ada_bank(n):
                dve.wait_ge(ada_mm, n + 1)
                dve.tensor_copy(mod[:, n - 4, :], sum_bank(n)).then_inc(ada_out, 1)

            dve.wait_ge(s_silu, 1)
            dve.wait_ge(s_ssq, TT)
            dve.tensor_scalar(small[:, 20:24], small[:, 16:20], 1.0 / D, NORM_EPS, ALU.mult, ALU.add).then_inc(s_var1, 1)
            dve.wait_ge(s_rstd1, 1)
            dve.reciprocal(small[:, 24:28], small[:, 28:32]).then_inc(s_rstd, 1)
            for n in range(4):
                ada_item(n)
            dve.wait_ge(ada_mm, 4)
            seq(dve.tensor_tensor(cols[:, 84:100], bank[0][:, 0:16], bias1, ALU.add))
            dve.scalar_tensor_tensor(scale1, scale1, 1.0, ln1, ALU.add, ALU.mult).then_inc(s_mod1, 1)
            dve.wait_ge(s_mod1, 1)
            dve.wait_ge(s_xT, KT)
            for k in range(1, KT, 2):
                dve.tensor_scalar(hT[:, k, :], hT[:, k, :], scale1[:, k:k + 1], shift1[:, k:k + 1], ALU.mult, ALU.add).then_inc(s_hT, 1)
            dve.tensor_scalar(col["k_a1"], col["k_a"], -1.0, 1.0, ALU.mult, ALU.add).then_inc(s_mu1, 1)
            dve.tensor_scalar(mu1, mu, -1.0, 1.0, ALU.mult, ALU.add).then_inc(s_mu1, 1)
            for j, ct in enumerate(Z_TILES):
                dve.wait_ge(z_scaled, j + 1)
                dve.scalar_tensor_tensor(zr[:, ct, 1:SEQ], bank[4 + j % 4][:, 0:SEQ - 1], mu[:, ct:ct + 1], zr[:, ct, 1:SEQ],
                                         ALU.mult, ALU.add).then_inc(z_shifted, 1)
                if j in ADA_AFTER:
                    n = 4 + ADA_AFTER.index(j)
                    ada_item(n)
                    if n > 4:
                        ada_bank(n - 1)
            ada_bank(9)
            dve.wait_ge(s_const, 16)
            chunks = lambda ap: ap.rearrange("p (c s) -> p c s", s=CH)
            for ct in range(CT):
                r_, k_, v_, c1 = zr[:, ct, :], zr[:, 4 + ct, :], zr[:, 8 + ct, :], slice(ct, ct + 1)
                dve.wait_ge(lora_act, 2 * ct + 1)
                dve.tensor_tensor_scan(xs[3], const("scan_keep"), xs[0], 0.0, ALU.mult, ALU.add).then_inc(scan_done, 1)
                dve.wait_ge(scan_done, ct + 1)
                dve.tensor_tensor(xs[0], xs[3], xs[0], ALU.subtract).then_inc(eprev_in, 1)
                dve.wait_ge(lora_act, 2 * ct + 2)
                seq(dve.tensor_scalar(xs[5], xs[1], col["k_a"][:, c1], col["k_a1"][:, c1], ALU.mult, ALU.add))
                dve.wait_ge(sq_act, ct + 1)
                seq(dve.tensor_scalar(xs[4], k_, col["k_k"][:, c1], None, ALU.mult))
                seq(dve.tensor_tensor(k_, k_, xs[5], ALU.mult))
                dve.scalar_tensor_tensor(xs[5], r_, col["r_k"][:, c1], k_, ALU.mult, ALU.mult).then_inc(bonus_in, 1)
                dve.wait_ge(ss_act, ct + 1)
                seq(dve.tensor_scalar(xs[2], xs[2], 1e-12, None, ALU.max))
                seq(dve.reciprocal(xs[2], xs[2]))
                seq(dve.tensor_tensor(xs[4], xs[4], xs[2], ALU.mult))
                dve.wait_ge(exp_act, 3 * ct + 3)
                dve.tensor_tensor(ahat[:, ct, :], xs[4], xs[0], ALU.mult)
                seq(dve.scalar_tensor_tensor(xs[1], xs[4], -1.0, xs[1], ALU.mult, ALU.mult))
                dve.tensor_copy(decay_end[:, ct, :], chunks(xs[6])[:, :, CH - 1])
                seq(dve.tensor_tensor(bhat[:, ct, :], xs[1], xs[3], ALU.mult))
                seq(dve.tensor_tensor(k_, k_, xs[3], ALU.mult))
                seq(dve.tensor_tensor(r_, r_, xs[6], ALU.mult))
                end = decay_end[:, ct, :].unsqueeze(2).to_broadcast([P, NCH, CH])
                dve.tensor_tensor(chunks(xs[1]), chunks(bhat[:, ct, :]), end, ALU.mult)
                dve.tensor_tensor(chunks(xs[4]), chunks(k_), end, ALU.mult).then_inc(forms_done, 1)
                for t in (0, 2):
                    dve.wait_ge(turn_mm, TT * ct + t + 1)
                    dve.tensor_copy(tokm[:, t, ct, :, :].rearrange("p a b -> p (a b)"), bank[4][:, :]).then_inc(turn_v, 1)
                dve.wait_ge(bonus_mm, ct + 1)
                dve.wait_ge(turn_mm, TT * (ct + 1))
                dve.tensor_tensor(v_, v_, bank[3][:, :], ALU.mult).then_inc(prep_done, 1)
                if ct in (1, 2):
                    ada_bank(9 + ct)
                if ct in (0, 1):
                    ada_item(10 + ct)
            for h in range(HEADS):
                ins = dve.tensor_copy(decay_end8[:, h, :], decay_end[HD * (h % 2):HD * (h % 2) + HD, h // 2, :])
            ins.then_inc(s_de8, 1)
            dve.wait_ge(s_de8, 1)

            def bc4(name, at=0, n=P, parts=P):
                return const(name, parts)[:, at:at + n].unsqueeze(1).to_broadcast([parts, 4, n])

            def f4(ap):
                return ap.rearrange("p (h n) -> p h n", h=4)

            for sc in range(TT):
                toks = slice(P * sc, P * sc + P)
                if sc == 2:
                    dve.wait_ge(sqrt_qk, 1)
                    dve.reciprocal(ssq, rms_qk).then_inc(rstd_qk, 1)
                for ev in V_EVENTS:
                    for g in range(2):
                        B = bank[4 * g:4 * g + 4]
                        if ev in MM_EVENTS and (ev, g) != ("y", 0):
                            dve.wait_ge(solve_mm[g], mm_at(sc, {"ab": "rb", "ak": "rk"}.get(ev, ev)))
                        if ev in ("ab", "rb", "ak", "rk"):
                            strict = ev[0] == "a"
                            dst = {"ab": TT1, "rb": RB, "ak": AK, "rk": RK}[ev][g]
                            mask = const("causal_t")[:, 0 if strict else P:P if strict else 2 * P]
                            for half in range(2):
                                src = f4(B[half + (0 if ev[1] == "b" else 2)])
                                ins = dve.tensor_tensor(dst[:, half::2, :], src[:, 0:2, :] if strict else src[:, 2:4, :],
                                                        mask.unsqueeze(1).to_broadcast([P, 2, P]), ALU.mult)
                        elif ev == "tt":
                            dve.wait_ge(solve_v[g], v_at(sc, "ab"))
                            ins = dve.tensor_tensor(TT1[g], TT1[g], bc4("ident"), ALU.add)
                        elif ev == "n0":
                            dve.wait_ge(solve_mm[g], mm_at(sc, "t0"))
                            ins = dve.tensor_tensor(INV[g], f4(B[0]), bc4("level0"), ALU.mult)
                        elif ev == "m0":
                            dve.wait_ge(solve_v[g], v_at(sc, "tt"))
                            ins = dve.tensor_tensor(INVT[g], TT1[g], bc4("level0_t"), ALU.mult)
                        elif ev[0] == "p":
                            ins = dve.tensor_tensor(PP[g], f4(B[1]), bc4("level" + ev[1]), ALU.mult)
                        elif ev == "q":
                            for half in range(2):
                                ins = dve.tensor_tensor(QQ[g][:, half::2, :], f4(B[1][0:HD, :])[:, half::2, :],
                                                        zr[HD * half:HD * half + HD, 2 * g:2 * g + 2, toks], ALU.add)
                        elif ev[0] == "d":
                            c = int(ev[1])
                            if c == 1:
                                dve.wait_ge(solve_v[g], v_at(sc, "g0"))
                            ins = dve.tensor_tensor(DE_[g], bc4("ident", 0, HD, HD),
                                                    decay_end8[:, 4 * g:4 * g + 4, 2 * sc + c].unsqueeze(2).to_broadcast([HD, 4, HD]), ALU.mult)
                        elif ev[0] == "g":
                            c = int(ev[1])
                            dve.wait_ge(solve_v[g], v_at(sc, f"d{c}"))
                            dve.wait_ge(solve_a[g], a_at(sc, f"h{c}"))
                            ins = dve.tensor_tensor(GG[c][g], f4(B[3 if c == 0 else 0][0:HD, 0:256]), DE_[g], ALU.add)
                        elif ev == "y":
                            if g == 0:
                                for c in range(2):
                                    n = 2 * sc + c
                                    for g2 in range(2):
                                        dve.wait_ge(solve_a[g2], a_at(sc, f"h{c}"))
                                    H = HH[c].rearrange("p (h n) -> p h n", h=HEADS)
                                    if n == 0:
                                        dve.tensor_copy(STATE[1], H).then_inc(chain_v, 1)
                                    else:
                                        dve.wait_ge(chain_mm, n)
                                        dve.tensor_tensor(STATE[(n + 1) % 3], bank[2 if c == 0 else 6][0:HD, :].rearrange("p (h n) -> p h n", h=HEADS),
                                                          H, ALU.add).then_inc(chain_v, 1)
                                dve.wait_ge(solve_mm[g], mm_at(sc, "y"))
                            for half in range(2):
                                ins = dve.tensor_copy(ahat[HD * half:HD * half + HD, 2 * g:2 * g + 2, toks],
                                                      f4(B[1][0:HD, :])[:, half::2, :])
                        ins.then_inc(solve_v[g], 1)
            for g in range(2):
                dve.wait_ge(solve_v[g], v_at(TT - 1, "y"))
            for ct in range(CT):
                dve.wait_ge(gn_mm, ct + 1)
                y_ = ahat[:, ct, :]
                dve.scalar_tensor_tensor(y_, bank[ct][:, :], -1.0 / HD, y_, ALU.mult, ALU.add).then_inc(gn_v, 1)
            for ct in range(CT):
                dve.wait_ge(gn_v, ct + 1)
                dve.tensor_tensor(xs[ct], ahat[:, ct, :], ahat[:, ct, :], ALU.mult).then_inc(gn_v, 1)
            for ct in range(CT):
                y_, c1 = ahat[:, ct, :], slice(ct, ct + 1)
                dve.wait_ge(gn_a, ct + 1)
                seq(dve.reciprocal(xs[ct], xs[ct]))
                seq(dve.tensor_tensor(y_, y_, xs[ct], ALU.mult))
                seq(dve.tensor_scalar(y_, y_, col["lnx_g"][:, c1], col["lnx_b"][:, c1], ALU.mult, ALU.add))
                seq(dve.tensor_tensor(y_, y_, zr[:, 8 + ct, :], ALU.add))
                dve.wait_ge(gn_mm, 2 * CT + ct + 1)
                dve.tensor_tensor(y_, y_, bank[ct][:, :], ALU.mult).then_inc(gn_v, 1)

            def row_max(h):
                b = 4 * (h % 2)
                for u, unit in enumerate(UNITS):
                    dve.wait_ge(s_mm, len(UNITS) * h + u + 1)
                    for i in unit:
                        ins = dve.reduce_max(stat[:, 24 + i:25 + i], S_AT[i], AX.X)
                seq(ins)
                dve.tensor_scalar(stat[:, b:b + 4], stat[:, 24:28], -HD ** -0.5, None, ALU.mult).then_inc(max_v, 1)

            def y_att(h):
                b, r = 8 + 4 * (h % 4), 28 + 4 * (h % 2)
                seq(dve.reciprocal(stat[:, r:r + 4], stat[:, b:b + 4]))
                dve.wait_ge(pv_mm, h + 1)
                dve.tensor_tensor(y_tok[:, :, HD * h:HD * h + HD], bank[3 + 4 * (h % 2)][:, 0:TT * HD].rearrange("p (t n) -> p t n", t=TT),
                                  stat[:, r:r + 4].unsqueeze(2).to_broadcast([P, TT, HD]), ALU.mult).then_inc(pv_out, 1)

            row_max(0)
            for h in range(HEADS):
                if h + 1 < HEADS:
                    dve.wait_ge(exp_a, TT * h + TT)
                    row_max(h + 1)
                dve.wait_ge(pt_mm, h + 1)
                if h >= 2:
                    dve.wait_ge(pv_mm, h - 1)
                for i in (1, 3):
                    dve.tensor_copy(PROBT[h % 2][i], PT_AT[i]).then_inc(pt_v, 1)
                if h:
                    y_att(h - 1)
            y_att(HEADS - 1)
            for ct in range(CT):
                dve.wait_ge(yt_mm, ct + 1)
                dve.tensor_copy(bhat[:, ct, :], bank[4 + ct][:, :]).then_inc(yt_v, 1)
            for j in range(2 * KT):
                ct = j % KT
                dve.wait_ge(mg_sig, j + 1)
                if j < KT:
                    dve.tensor_tensor(merged[:, ct, :], msc[j % 2], bank[j % 2][:, :], ALU.mult).then_inc(mg_v, 1)
                else:
                    seq(dve.tensor_tensor(msc[j % 2], msc[j % 2], bank[j % 2][:, :], ALU.mult))
                    dve.tensor_tensor(merged[:, ct, :], merged[:, ct, :], msc[j % 2], ALU.add).then_inc(mg_v, 1)
            dve.wait_ge(s_x, 32)
            for j in range(2 * TT):
                n, t = j // TT, j % TT
                dve.wait_ge(out_mm, j + 1)
                if j >= 4:
                    dve.wait_ge(x2_done, j - 3)
                elif j == 0:
                    dve.wait_ge(mg_v, 2 * KT)
                seq(dve.tensor_tensor(msc[j % 4], bank[4 + t][:, :], mod[:, n, :], ALU.mult))
                xx = x[:, t, 512 * n:512 * n + 512]
                dve.tensor_tensor(xx, xx, msc[j % 4], ALU.add).then_inc(x2_done, 1)
            shift2, a2 = (mod[:, i:i + 2, :].rearrange("p a n -> p (a n)") for i in (2, 4))
            dve.wait_ge(s_ln2, 16)
            dve.wait_ge(x2_done, 2 * TT)
            seq(dve.scalar_tensor_tensor(a2, a2, 1.0, ln2_bc, ALU.add, ALU.mult))
            dve.wait_ge(ssq2, TT)
            dve.tensor_scalar(ln_stat[:, 4:8], ln_stat[:, 0:4], 1.0 / D, NORM_EPS, ALU.mult, ALU.add).then_inc(var2, 1)
            dve.wait_ge(sqrt2, 1)
            seq(dve.reciprocal(ln_stat[:, 12:16], ln_stat[:, 8:12]))
            for t in range(TT):
                seq(dve.scalar_tensor_tensor(h2[:, t, :], x[:, t, :], ln_stat[:, 12 + t:13 + t], a2, ALU.mult, ALU.mult))
                dve.tensor_tensor(h2[:, t, :], h2[:, t, :], shift2, ALU.add).then_inc(h2_v, 1)
            for k in range(1, KT, 2):
                dve.wait_ge(h2t_mm, k + 1)
                dve.tensor_copy(h2T[:, k, :], bank[7][:, :]).then_inc(h2t_v, 1)

            def of_token(i):
                return stats[i].unsqueeze(2).to_broadcast([P, TT, NEXP])

            def const4(name, n=NEXP):
                return const(name)[:, 0:n].unsqueeze(1).to_broadcast([P, TT, n])

            def pick(dst, values, top, cand, n):
                t4 = stats[top].unsqueeze(2).to_broadcast([P, TT, n])
                seq(dve.reduce_max(stats[top], values, AX.X))
                seq(dve.tensor_tensor(cand, values, t4, ALU.is_equal))
                seq(dve.tensor_tensor(cand, cand, const4("first_wins", n), ALU.mult))
                seq(dve.reduce_max(stats[19], cand, AX.X))
                seq(dve.tensor_tensor(dst, cand, stats[19].unsqueeze(2).to_broadcast([P, TT, n]), ALU.is_equal))

            dve.wait_ge(s_route_w, 64)
            dve.wait_ge(logit_mm, 1)
            seq(dve.tensor_tensor(L, bank[0][:, 0:TT * NR].rearrange("p (t n) -> p t n", n=NR),
                                  b_route.unsqueeze(1).to_broadcast([P, TT, NR]), ALU.add))
            LG = L[:, :, 0:GROUPS]
            pick(gsel, LG, 0, gtmp, GROUPS)
            dve.tensor_tensor(gtmp, LG, stats[0].unsqueeze(2).to_broadcast([P, TT, GROUPS]), ALU.subtract).then_inc(exp_in, 1)
            dve.wait_ge(exp_out, 1)
            seq(dve.reduce_sum(stats[1], gtmp, AX.X))
            seq(dve.reciprocal(stats[1], stats[1]))
            seq(dve.tensor_scalar(gsel, gsel, -NEG, NEG, ALU.mult, ALU.add))
            for t in range(TT):
                ins = dve.tensor_tensor(LE[:, t, :].rearrange("p (g e) -> p g e", g=GROUPS),
                                        L[:, t, GROUPS:NR].rearrange("p (g e) -> p g e", g=GROUPS),
                                        gsel[:, t, :].unsqueeze(2).to_broadcast([P, GROUPS, EPG]), ALU.add)
            seq(ins)
            pick(PICK1, LE, 2, CAND, NEXP)
            seq(dve.scalar_tensor_tensor(LE, PICK1, 2 * NEG, LE, ALU.mult, ALU.add))
            pick(PICK2, LE, 3, CAND, NEXP)
            dve.memset(ones, 1.0)
            dve.memset(ones32, 1.0)
            dve.tensor_tensor(PICKS, PICK1, PICK2, ALU.add).then_inc(picks_v, 1)
            dve.tensor_tensor(stats[5], stats[3], stats[2], ALU.subtract).then_inc(exp_in, 1)
            dve.wait_ge(exp_out, 2)
            seq(dve.tensor_scalar(stats[4], stats[5], 1.0, None, ALU.add))
            seq(dve.reciprocal(stats[4], stats[4]))
            seq(dve.tensor_tensor(stats[4], stats[4], stats[1], ALU.mult))
            seq(dve.tensor_tensor(stats[5], stats[5], stats[4], ALU.mult))
            dve.wait_ge(rank_mm, 1)
            seq(dve.tensor_copy(RANK, bank[1][:, 0:TT * NEXP].rearrange("p (t n) -> p t n", n=NEXP)))
            seq(dve.tensor_copy(counts, bank[1][:, TT * NEXP:TT * NEXP + NEXP]))
            seq(dve.tensor_scalar(over, counts, float(SLOTS), None, ALU.is_gt))
            for m in range(2, SEQ // SLOTS):
                seq(dve.scalar_tensor_tensor(over, counts, float(SLOTS * m), over, ALU.is_gt, ALU.add))
            seq(dve.tensor_tensor_scan(over_to, ones32, over, 0.0, ALU.mult, ALU.add))
            seq(dve.tensor_tensor(over_from, over_to, over, ALU.subtract))
            seq(dve.tensor_copy(passes[:, 0:1], over_to[0:1, NEXP - 1:NEXP]))
            for j in range(MAXOV):
                seq(dve.tensor_scalar(CAND[0:1, 0, :], over_to[0:1, :], float(j), None, ALU.is_le))
                seq(dve.reduce_sum(pass_tmp[:, j:j + 1], CAND[0:1, 0, :], AX.X))
            seq(dve.tensor_scalar(pass_tmp[:, 0:MAXOV], pass_tmp[:, 0:MAXOV], float(NEXP - 1), None, ALU.min))
            seq(dve.tensor_copy(passes[:, 1:1 + MAXOV], pass_tmp[:, 0:MAXOV]))
            for k, sel in enumerate((PICK1, PICK2)):
                rank, expert, start, full, row = stats[6], stats[7], stats[8], stats[9], stats[10]
                for dst, ap in ((rank, RANK), (expert, const4("expert_id")), (start, over_from.unsqueeze(1).to_broadcast([P, TT, NEXP]))):
                    seq(dve.tensor_tensor(PROD, sel, ap, ALU.mult))
                    seq(dve.reduce_sum(dst, PROD, AX.X))
                seq(dve.tensor_scalar(full, rank, float(SLOTS), None, ALU.is_ge))
                for m in range(2, SEQ // SLOTS):
                    seq(dve.scalar_tensor_tensor(full, rank, float(SLOTS * m), full, ALU.is_ge, ALU.add))
                seq(dve.scalar_tensor_tensor(rank, full, -float(SLOTS), rank, ALU.mult, ALU.add))
                seq(dve.tensor_tensor(start, start, full, ALU.add))
                seq(dve.scalar_tensor_tensor(start, start, float(NEXP - 1), expert, ALU.add, ALU.subtract))
                seq(dve.tensor_scalar(full, full, 1.0, None, ALU.min))
                seq(dve.tensor_tensor(start, start, full, ALU.mult))
                seq(dve.tensor_tensor(start, start, expert, ALU.add))
                seq(dve.scalar_tensor_tensor(row, rank, float(NPASS), start, ALU.mult, ALU.add))
                at = slice(TT * k, TT * k + TT)
                seq(dve.tensor_copy(entry_row[:, at], row))
                seq(dve.tensor_copy(entry[:, at, 0], const("token_id")))
                seq(dve.tensor_scalar(entry[:, at, 1], const("token_id"), float(SEQ * k), None, ALU.add))
                seq(dve.tensor_copy(entry[:, at, 2].bitcast(f32), stats[4 + k]))
                seq(dve.tensor_scalar(entry[:, at, 3], const("token_id"), float(SEQ), None, ALU.add))
            dve.sem_inc(entry_v, 1)
            dve.wait_ge(table_in, 16)
            dve.tensor_copy(gather_at[0:SLOTS, :], table[0:SLOTS, :, 0]).then_inc(gather_v, 1)

            def split_lo(q):
                return dve.tensor_tensor(lo[:, q, :, :], raw[:, q, :, :], hi[:, q, :, :].bitcast(f32), ALU.subtract)

            def lo_piece(e, q):
                dve.wait_ge(hi_done, PIECES * e + q + 1)
                split_lo(q).then_inc(lo_done, 1)

            def y_half(e, b):
                dve.wait_ge(w2_mm, e + 1)
                if not (isinstance(e, int) and e < 2):
                    dve.wait_ge(y_out[b], 16 * (e // 2))
                dve.tensor_scalar(ys[:, b, 512:D], bank[6][0:SLOTS, :], weight_of(e), None, ALU.mult).then_inc(y_v, 1)

            def turn_x(e, b):
                dve.wait_ge(xt_a, e + 1)
                dve.tensor_tensor(xT[:, b, :, SLOTS:P], turned(b), xT[:, b, :, 0:SLOTS].bitcast(f32), ALU.subtract).then_inc(xt_v, 1)

            def hidden(e):
                dve.wait_ge(ab_a, 2 * e + 2)
                dve.tensor_tensor(half_a[:, :], bank[2][0:SLOTS, :], half_a[:, :], ALU.add).then_inc(a_v, 1)
                dve.tensor_tensor(half_b[:, :], bank[3][0:SLOTS, :], half_b[:, :], ALU.add).then_inc(b_v, 1)
                dve.wait_ge(silu_done, e + 1)
                dve.wait_ge(b_v, e + 1)
                if not (isinstance(e, int) and e == 0):
                    dve.wait_ge(ht_mm, e)
                dve.tensor_tensor(hid[:, :], silu_a[:, :], half_b[:, :], ALU.mult).then_inc(hid_v, 1)

            def dve_step(e, b, last=False, head=0):
                if head >= 2:
                    y_half(e - 2, b)
                if not last:
                    for q in range(3):
                        lo_piece(e + 1, q)
                    turn_x(e + 1, 1 - b)
                    lo_piece(e + 1, 3)
                hidden(e)

            for q in range(PIECES):
                lo_piece(0, q)
            turn_x(0, 0)
            dve_step(0, 0)
            dve_step(1, 1, head=1)
            dve_step(2, 0, head=2)
            dve_step(3, 1, head=2)
            with dve.Fori(0, (NEXP - 6) // 2) as i:
                for b in range(2):
                    dve_step(2 * i + 4 + b, b, head=2)
            dve_step(NEXP - 2, 0, head=2)
            dve_step(NEXP - 1, 1, head=2, last=True)
            y_half(NEXP - 2, 0)
            y_half(NEXP - 1, 1)
            n_over = dve.value_load(passes[0:1, 0:1], min_val=0, max_val=MAXOV)
            for b in range(2):
                dve.wait_ge(y_out[b], 16 * NEXP // 2)
            dve.wait_ge(y_a, NEXP)
            dve.sem_inc(ov_ready, 1)
            with dve.If(n_over > 0):
                with dve.Fori(0, n_over) as j:
                    for q in range(PIECES):
                        dve.wait_ge(ov_hi, 4 * j + q + 1)
                        split_lo(q).then_inc(ov_lo, 1)
                    dve.wait_ge(ov_xe_a, j + 1)
                    dve.tensor_tensor(xT[:, 0, :, SLOTS:P], turned(0), xT[:, 0, :, 0:SLOTS].bitcast(f32), ALU.subtract).then_inc(ov_xe_v, 1)
                    dve.wait_ge(ov_ab, 2 * j + 2)
                    dve.tensor_tensor(half_a[:, :], bank[2][0:SLOTS, :], half_a[:, :], ALU.add).then_inc(ov_a, 1)
                    dve.tensor_tensor(half_b[:, :], bank[3][0:SLOTS, :], half_b[:, :], ALU.add).then_inc(b_v, 1)
                    dve.wait_ge(b_v, j + NEXP + 1)
                    dve.wait_ge(ov_silu, j + 1)
                    dve.tensor_tensor(hid[:, :], silu_a[:, :], half_b[:, :], ALU.mult).then_inc(ov_hid, 1)
                    dve.wait_ge(ov_y, j + 1)
                    dve.tensor_scalar(ys[:, 0, 512:D], bank[6][0:SLOTS, :], weight_of(j + NEXP), None, ALU.mult).then_inc(ov_ys, 1)
            dve.wait_ge(s_sum, 33)
            gate2 = mod[:, 6:8, :].rearrange("p a n -> p (a n)")
            for t in range(TT):
                seq(dve.tensor_tensor(sum0[:, t, :], sum0[:, t, :], sum1[:, t, :], ALU.add))
                seq(dve.tensor_tensor(sum0[:, t, :], sum0[:, t, :], gate2, ALU.mult))
                dve.tensor_tensor(x[:, t, :], x[:, t, :], sum0[:, t, :], ALU.add).then_inc(s_final, 1)

        @block.tensor
        def _(pe):
            def ada(n):
                pe.wait_ge(ada_in, 2 * n + 2)
                even, odd = ada_acc(n)
                if n < 4:
                    for i in range(4):
                        dst = bank[0][:, 4 * n + i:4 * n + i + 1]
                        pe.matmul(dst, even[:, P * i:P * i + P], one, start=True, stop=False)
                        mm = pe.matmul(dst, odd[:, P * i:P * i + P], one, start=False, stop=True)
                    mm.then_inc(ada_mm, 1)
                    return
                if 6 <= n < 10:
                    pe.wait_ge(ada_out, n - 5)
                dst, ones_ = sum_bank(n), one.to_broadcast([P, P])
                pe.matmul(dst, ones_, even, start=True, stop=False)
                pe.matmul(dst, ones_, odd, start=False, stop=False)
                pe.matmul(dst, one[0:1, :].to_broadcast([1, P]), mod[0:1, n - 4, :], start=False, stop=True).then_inc(ada_mm, 1)

            pe.wait_ge(s_c, 16 * 12)
            pe.transpose(bank[7][:, 0:74], prow[0:74, :], ident[0:74, 0:74]).then_inc(s_prow, 1)
            pe.wait_ge(s_cols, 1)
            for k in range(KT):
                if k >= 2:
                    pe.wait_ge(s_xT, k - 1)
                for t in range(TT):
                    if k == 0:
                        pe.wait_ge(s_xn, t + 1)
                    mm = pe.transpose(bank[2 + k % 2][:, t * P:t * P + P], x_n[:, t, k * P:k * P + P], ident)
                mm.then_inc(s_xt, 1)
            for n in range(4):
                ada(n)
            pe.wait_ge(s_hT, KT)
            pe.wait_ge(s_bias2, 16)
            for j, ct in enumerate(Z_TILES):
                if j in (0, 2, 6, 10):
                    ring_wait(pe, Z_AT[(j + 2) // 4])
                    w = slot_view(Z_AT[(j + 2) // 4])
                if j >= 4:
                    pe.wait_ge(z_shifted, j - 3)
                for k in range(KT):
                    mm = pe.matmul(bank[4 + j % 4][:, :], w[:, k, (ct % 4) * P:(ct % 4) * P + P], hT[:, k, :], start=(k == 0), stop=(k == KT - 1))
                mm.then_inc(z_mm, 1)
                if j - 2 in ADA_AFTER:
                    ada(4 + ADA_AFTER.index(j - 2))
            def att_tile(j):
                if j % TT == 0:
                    ring_wait(pe, ATT_AT[j // TT])
                w = slot_view(ATT_AT[j // TT])
                if j == 0:
                    pe.wait_ge(z_shifted, 14)
                if j >= 2:
                    pe.wait_ge(att_out, j - 1)
                for k in range(KT):
                    mm = pe.matmul(bank[6 + j % 2][:, :], hT[:, k, (j % TT) * P:(j % TT) * P + P], w[:, k, :], start=(k == 0), stop=(k == KT - 1))
                mm.then_inc(att_mm, 1)

            def lora(ct):
                for i, rows in enumerate((slice(0, 64), slice(64, 128))):
                    if ct:
                        pe.wait_ge(lora_act, 2 * ct - 1 + i)
                    pe.matmul(bank[i][:, :], lora_wa[rows, P * ct:P * ct + P], zr[rows, 12, :], start=True, stop=True).then_inc(lora_mm, 1)

            ada(9)
            pe.wait_ge(ada_out, 6)
            pe.wait_ge(s_const, 16)
            pe.wait_ge(s_act_in, 1)
            pe.wait_ge(s_lora_w, 48)
            lora(0)
            for ct in range(CT):
                v_ = zr[:, 8 + ct, :]
                att_tile(3 * ct)
                pe.wait_ge(sq_act, ct + 1)
                if ct == 2:
                    pe.wait_ge(ada_out, 7)
                elif ct == 3:
                    pe.wait_ge(ada_out, 8)
                pe.matmul(bank[2][:, :], const("head_ones"), xs[2], start=True, stop=True).then_inc(ss_mm, 1)
                if ct + 1 < CT:
                    lora(ct + 1)
                att_tile(3 * ct + 1)
                pe.wait_ge(bonus_in, ct + 1)
                if ct:
                    pe.wait_ge(prep_done, ct)
                pe.matmul(bank[3][:, :], const("head_ones"), xs[5], start=True, stop=True).then_inc(bonus_mm, 1)
                if ct in (1, 2):
                    pe.wait_ge(ss_act, ct + 1)
                    ada(9 + ct)
                att_tile(3 * ct + 2)
                pe.wait_ge(forms_done, ct + 1)
                for t in range(TT):
                    if TT * ct + t >= 2:
                        pe.wait_ge((turn_v, turn_a)[t % 2], (TT * ct + t) // 2)
                    for i, src in enumerate((v_, xs[1], xs[4], ahat[:, ct, :])):
                        mm = pe.transpose(bank[4 + t % 2][:, P * i:P * i + P], src[:, P * t:P * t + P], ident)
                    mm.then_inc(turn_mm, 1)
            pe.wait_ge(att_out, 12)
            pe.wait_ge(prep_done, CT)
            pe.wait_ge(turn_v, 2 * CT)
            pe.wait_ge(turn_a, 2 * CT)
            pe.wait_ge(ada_out, 8)
            for sc in range(TT):
                toks = slice(P * sc, P * sc + P)
                for ev in MM_EVENTS:
                    for g in range(2):
                        B = bank[4 * g:4 * g + 4]
                        if ev == "y" and g == 0:
                            for c in range(2):
                                n = 2 * sc + c
                                if n:
                                    for g2 in range(2):
                                        pe.wait_ge(solve_v[g2], v_at(sc, f"g{c}"))
                                    pe.wait_ge(chain_v, n)
                                    for h in range(HEADS):
                                        mm = pe.matmul(bank[2 if c == 0 else 6][0:HD, HD * h:HD * h + HD], GG[c][h // 4][:, h % 4, :],
                                                       STATE[n % 3][:, h, :], start=True, stop=True)
                                    mm.then_inc(chain_mm, 1)
                            for g2 in range(2):
                                pe.wait_ge(solve_v[g2], v_at(sc, "q"))
                        if ev == "ab":
                            if sc:
                                pe.wait_ge(solve_v[g], v_at(sc - 1, "y"))
                                pe.wait_ge(solve_a[g], a_at(sc - 1, "h1"))
                                pe.wait_ge(chain_v, 2 * sc)
                        need_v = {"t0": "rb", "p1": "n0", "n1": "p1", "m1": "m0", "x": "ak", "q": "rb", "y": "q"}
                        if ev in need_v:
                            pe.wait_ge(solve_v[g], v_at(sc, need_v[ev]))
                        elif ev[0] == "p":
                            pe.wait_ge(solve_a[g], a_at(sc, f"n{int(ev[1]) - 1}"))
                        elif ev[0] == "n" or ev == "m5":
                            pe.wait_ge(solve_v[g], v_at(sc, "p" + ev[1]))
                            pe.wait_ge(solve_a[g], a_at(sc, f"m{int(ev[1]) - 1}"))
                        if ev == "n1":
                            pe.wait_ge(solve_v[g], v_at(sc, "m0"))
                        if ev == "wu":
                            pe.wait_ge(solve_a[g], a_at(sc, "x"))
                        if ev == "q":
                            pe.wait_ge(solve_a[g], a_at(sc, "wu"))
                        for i in range(4):
                            h = 4 * g + i
                            ct, rows = h // 2, slice(HD * (h % 2), HD * (h % 2) + HD)
                            hc = slice(HD * (h % 2), HD * (h % 2) + HD)
                            at = slice(P * i, P * i + P)
                            V_, Bt, Kt_, Ah = (tokm[:, sc, ct, q, hc] for q in range(4))
                            a_, b_ = ahat[rows, ct, toks], bhat[rows, ct, toks]
                            k_, r_ = zr[rows, 4 + ct, toks], zr[rows, ct, toks]
                            if ev == "ab":
                                mm = pe.matmul(B[i % 2][:, P * (i // 2):P * (i // 2) + P], b_, a_, start=True, stop=True)
                            elif ev == "rb":
                                mm = pe.matmul(B[i % 2][:, P * (2 + i // 2):P * (2 + i // 2) + P], b_, r_, start=True, stop=True)
                            elif ev == "ak":
                                mm = pe.matmul(B[2 + i % 2][:, P * (i // 2):P * (i // 2) + P], k_, a_, start=True, stop=True)
                            elif ev == "rk":
                                mm = pe.matmul(B[2 + i % 2][:, P * (2 + i // 2):P * (2 + i // 2) + P], k_, r_, start=True, stop=True)
                            elif ev == "t0":
                                mm = pe.transpose(B[0][:, at], TT1[g][:, i, :], ident)
                            elif ev[0] == "p":
                                mm = pe.matmul(B[1][:, at], TT1[g][:, i, :], INV[g][:, i, :], start=True, stop=True)
                            elif ev[0] == "n":
                                mm = pe.matmul(B[2][:, at], INVT[g][:, i, :], PP[g][:, i, :], start=True, stop=True)
                            elif ev[0] == "m":
                                mm = pe.matmul(B[3][:, at], PP[g][:, i, :], INVT[g][:, i, :], start=True, stop=True)
                            elif ev == "x":
                                mm = pe.matmul(B[0][:, HD * i:HD * i + HD], AK[g][:, i, :], V_, start=True, stop=True)
                            elif ev == "wu":
                                pe.matmul(B[2][:, P * i:P * i + HD], INVT[g][:, i, :], Ah, start=True, stop=True)
                                mm = pe.matmul(B[2][:, P * i + HD:P * i + P], INVT[g][:, i, :], XX[g][:, i, :], start=True, stop=True)
                            elif ev == "q":
                                mm = pe.matmul(B[1][0:HD, at], WU[g][:, i, 0:HD], RB[g][:, i, :], start=True, stop=True)
                            elif ev[:2] == "gh":
                                c = int(ev[2])
                                cr = slice(CH * c, CH * c + CH)
                                dst = B[3 if c == 0 else 0]
                                if i == 0 and c == 0:
                                    pe.wait_ge(solve_a[g], a_at(sc, "m5"))
                                pe.matmul(dst[0:HD, HD * i:HD * i + HD], WU[g][cr, i, 0:HD], Bt[cr, :], start=True, stop=True)
                                pe.matmul(dst[0:HD, 256 + HD * i:256 + HD * i + HD], Bt[cr, :], WU[g][cr, i, HD:P], start=True, stop=False)
                                mm = pe.matmul(dst[0:HD, 256 + HD * i:256 + HD * i + HD], Kt_[cr, :], V_[cr, :], start=False, stop=True)
                            elif ev == "y":
                                pe.matmul(B[1][0:HD, at], WU[g][:, i, HD:P], RB[g][:, i, :], start=True, stop=False)
                                mm = pe.matmul(B[1][0:HD, at], V_, RK[g][:, i, :], start=False, stop=False)
                                for c in range(2):
                                    n = 2 * sc + c
                                    if n:
                                        if i == 0:
                                            pe.wait_ge(chain_v, n)
                                        mm = pe.matmul(B[1][0:HD, P * i + CH * c:P * i + CH * c + CH], STATE[n % 3][:, h, :],
                                                       QQ[g][:, i, CH * c:CH * c + CH], start=False, stop=(c == 1))
                        mm.then_inc(solve_mm[g], 1)
            for g in range(2):
                pe.wait_ge(solve_v[g], v_at(TT - 1, "y"))
            for ct in range(CT):
                pe.matmul(bank[ct][:, :], const("head_ones"), ahat[:, ct, :], start=True, stop=True).then_inc(gn_mm, 1)
            for ct in range(CT):
                pe.wait_ge(gn_v, CT + ct + 1)
                pe.matmul(bank[ct][:, :], const("head_ones"), xs[ct], start=True, stop=True).then_inc(gn_mm, 1)
            for j in range(8):
                if j >= 4:
                    pe.wait_ge(qk_a, j - 3)
                for t in range(TT):
                    if j in (0, 4):
                        pe.wait_ge(rope_done, 2 * t + 1 + j // 4)
                    c0 = W * (j // 4) + P * (j % 4)
                    mm = pe.transpose(bank[4 + j % 4][:, P * t:P * t + P], qkv[:, t, c0:c0 + P], ident)
                mm.then_inc(qk_mm, 1)
            for ct in range(CT):
                pe.wait_ge(gn_a, ct + 1)
                pe.matmul(bank[ct][:, :], lora_g[:, P * ct:P * ct + P], zr[:, 13, :], start=True, stop=True).then_inc(gn_mm, 1)
            pe.wait_ge(gn_v, 3 * CT)
            pe.wait_ge(qk_a, 8)

            def scores(h):
                rows, ct = slice(HD * (h % 2), HD * (h % 2) + HD), h // 2
                done = 0
                for unit in UNITS:
                    done += len(unit)
                    if h:
                        pe.wait_ge(exp_a, TT * (h - 1) + done)
                    for i in unit:
                        q_ = qT[rows, ct, P * i:P * i + P]
                        if i:
                            pe.matmul(S_AT[i][:, 0:P * i], q_, kT[rows, ct, 0:P * i], start=True, stop=True)
                        pe.matmul(S_AT[i][:, P * i:P * i + P], q_, kT[rows, ct, P * i:P * i + P], start=True, stop=False)
                        mm = pe.matmul(S_AT[i][:, P * i:P * i + P], ident, const("diag_mask"), start=False, stop=True)
                    mm.then_inc(s_mm, 1)

            def weighted(h):
                pe.wait_ge(pt_a, 2 * h + 2)
                pe.wait_ge(pt_v, 2 * h + 2)
                if h >= 2:
                    pe.wait_ge(pv_out, h - 1)
                for i in range(TT):
                    for kt in range(i + 1):
                        mm = pe.matmul(bank[3 + 4 * (h % 2)][:, HD * i:HD * i + HD], PROBT[h % 2][kt][:, P * (i - kt):P * (i - kt) + P],
                                       qkv[:, kt, 2 * W + HD * h:2 * W + HD * h + HD], start=(kt == 0), stop=(kt == i))
                mm.then_inc(pv_mm, 1)

            scores(0)
            for h in range(HEADS):
                if h + 1 < HEADS:
                    scores(h + 1)
                if h:
                    weighted(h - 1)
                pe.wait_ge(exp_a, TT * h + TT)
                for kt in range(TT):
                    for i in range(kt, TT):
                        mm = pe.transpose(PT_AT[kt][:, P * (i - kt):P * (i - kt) + P], PROB[h % 2][i][:, P * kt:P * kt + P], ident)
                mm.then_inc(pt_mm, 1)
            weighted(HEADS - 1)
            for b in range(2):
                at = N_BEFORE_MERGE + 3 * b
                ring_wait(pe, at)
                proj = slot_view(at, CT)
                y_ = (ahat, bhat)[b]
                for ct in range(KT):
                    j = KT * b + ct
                    if ct % 4 == 0:
                        ring_wait(pe, at + 1 + ct // 4)
                        w = slot_view(at + 1 + ct // 4)
                    if j >= 2:
                        pe.wait_ge(mg_v, j - 1)
                    if j == 1:
                        pe.wait_ge(pv_out, HEADS - 1)
                    if j == KT:
                        pe.wait_ge(yt_v, CT)
                    for k in range(CT):
                        pe.matmul(bank[j % 2][:, :], proj[:, k, P * ct:P * ct + P], y_[:, k, :], start=(k == 0), stop=(k == CT - 1))
                    for k in range(KT):
                        mm = pe.matmul(bank[2 + j % 2][:, :], w[:, k, P * (ct % 4):P * (ct % 4) + P], hT[:, k, :], start=(k == 0), stop=(k == KT - 1))
                    mm.then_inc(mg_mm, 1)
                    if j == 1:
                        pe.wait_ge(pv_out, HEADS)
                        for c in range(CT):
                            for t in range(TT):
                                mm = pe.transpose(bank[4 + c][:, P * t:P * t + P], y_tok[:, t, P * c:P * c + P], ident)
                            mm.then_inc(yt_mm, 1)
            pe.wait_ge(mg_v, 2 * KT)
            for j in range(2 * TT):
                if j % TT == 0:
                    ring_wait(pe, len(items) - 2 + j // TT)
                    w = slot_view(len(items) - 2 + j // TT)
                if j >= TT:
                    pe.wait_ge(x2_done, j - TT + 1)
                for k in range(KT):
                    mm = pe.matmul(bank[4 + j % TT][:, :], merged[:, k, P * (j % TT):P * (j % TT) + P], w[:, k, :], start=(k == 0), stop=(k == KT - 1))
                mm.then_inc(out_mm, 1)
            for k in range(KT):
                if k >= 2:
                    pe.wait_ge((h2t_a, h2t_v)[k % 2], k // 2)
                for t in range(TT):
                    if k == 0:
                        pe.wait_ge(h2_v, t + 1)
                    mm = pe.transpose(bank[6 + k % 2][:, t * P:t * P + P], h2[:, t, k * P:k * P + P], ident)
                mm.then_inc(h2t_mm, 1)
            pe.wait_ge(h2t_a, 4)
            pe.wait_ge(h2t_v, 4)
            pe.wait_ge(s_route_w, 64)
            for t in range(TT):
                for k in range(KT):
                    mm = pe.matmul(bank[0][:, NR * t:NR * t + NR], h2T[:, k, P * t:P * t + P], w_route[:, k, :], start=(k == 0), stop=(k == KT - 1))
            mm.then_inc(logit_mm, 1)
            pe.wait_ge(picks_v, 1)
            for t in range(TT):
                at = slice(NEXP * t, NEXP * t + NEXP)
                for t2 in range(t):
                    pe.matmul(bank[1][:, at], ones, PICKS[:, t2, :], start=(t2 == 0), stop=False)
                pe.matmul(bank[1][:, at], const("before"), PICKS[:, t, :], start=(t == 0), stop=True)
            for t in range(TT):
                mm = pe.matmul(bank[1][:, TT * NEXP:TT * NEXP + NEXP], ones, PICKS[:, t, :], start=(t == 0), stop=(t == TT - 1))
            mm.then_inc(rank_mm, 1)

            def turn_rows(b):
                for k in range(KT):
                    mm = pe.transpose(turned(b)[:, k, :], picked[0:SLOTS, b, k:D:KT], ident[0:SLOTS, 0:SLOTS])
                return mm

            def piece(q, b):
                for k in range(4):
                    for part in (hi, lo):
                        mm = pe.matmul(bank[2 + q % 2][:, :], xT[:, b, 4 * (q // 2) + k, :], part[:, q, k, :],
                                       start=(q < 2 and k == 0 and part is hi), stop=(q >= 2 and k == 3 and part is lo))
                return mm

            def turn_hid():
                for k in range(4):
                    mm = pe.transpose(bank[4][:, SLOTS * k:SLOTS * k + SLOTS], hid[:, k:DE:4], ident[0:SLOTS, 0:SLOTS])
                return mm

            def down(b):
                for k in range(4):
                    for n in range(2):
                        mm = pe.matmul(bank[5 + n][0:SLOTS, :], hidT[:, k, :], w2s[:, b, k, 512 * n:512 * n + 512], start=(k == 0), stop=(k == 3))
                return mm

            def do_rows(e, b):
                first_one = isinstance(e, int) and e == 0
                pe.wait_ge(rows_in[b], 16 * (e // 2 + 1) if isinstance(e, int) else 16 * (e // 2) + 16)
                if not first_one:
                    pe.wait_ge(xt_v, e)
                    pe.sem_inc(past, 1)
                turn_rows(b).then_inc(xt_mm, 1)

            def do_piece(e, q, b):
                if q == 0:
                    pe.wait_ge(xt_v, e + 1)
                    if not (isinstance(e, int) and e == 0):
                        pe.wait_ge(b_v, e)
                pe.wait_ge(lo_done, PIECES * e + q + 1)
                piece(q, b).then_inc(piece_mm, 1)

            def do_turn_hid(e):
                pe.wait_ge(hid_v, e + 1)
                pe.sem_inc(past, 1)
                turn_hid().then_inc(ht_mm, 1)

            def do_down(e, b):
                pe.wait_ge(ht_a, e + 1)
                pe.wait_ge(w2_in[b], 16 * (e // 2 + 1) if isinstance(e, int) else 16 * (e // 2) + 16)
                if not (isinstance(e, int) and e == 0):
                    pe.wait_ge(y_a, e)
                    pe.wait_ge(y_v, e)
                down(b).then_inc(w2_mm, 1)

            def pe_step(e, b, last=False):
                for q in range(3):
                    do_piece(e, q, b)
                do_turn_hid(e - 1)
                do_piece(e, 3, b)
                if not last:
                    do_rows(e + 1, 1 - b)
                do_down(e - 1, 1 - b)

            do_rows(0, 0)
            for q in range(PIECES):
                do_piece(0, q, 0)
            do_rows(1, 1)
            pe_step(1, 1)
            with pe.Fori(0, (NEXP - 4) // 2) as i:
                for b in range(2):
                    pe_step(2 * i + 2 + b, b)
            pe_step(NEXP - 2, 0)
            pe_step(NEXP - 1, 1, last=True)
            do_turn_hid(NEXP - 1)
            do_down(NEXP - 1, 1)
            n_over = pe.value_load(passes[0:1, 0:1], min_val=0, max_val=MAXOV)
            with pe.If(n_over > 0):
                with pe.Fori(0, n_over) as j:
                    pe.wait_ge(ov_rows, 16 * j + 16)
                    pe.sem_inc(past, 1)
                    turn_rows(0).then_inc(ov_xt, 1)
                    pe.wait_ge(ov_xe_v, j + 1)
                    pe.wait_ge(ov_lo, 4 * j + 4)
                    for q in range(PIECES):
                        mm = piece(q, 0)
                    mm.then_inc(ov_mm, 1)
                    pe.wait_ge(ov_hid, j + 1)
                    pe.sem_inc(past, 1)
                    turn_hid().then_inc(ov_ht, 1)
                    pe.wait_ge(ov_hte, j + 1)
                    pe.wait_ge(ov_w2, 16 * j + 16)
                    down(0).then_inc(ov_y, 1)


_INS = ["x", "c", "w_ada", "b_ada", "ln1_g", "ln2_g", "w_in", "mu_shift", "w0", "w_lora_up", "a0", "a_lora_up",
        "g_lora_up", "k_k", "k_a", "r_k", "lnx_g", "lnx_b", "q_norm_g", "k_norm_g", "w_br_rwkv", "w_br_moba",
        "w_out", "w_rg", "b_rg", "w_re", "b_re", "w1", "w3", "w2"]


def kernel(**inputs):
    import numpy as _np
    import concourse.bacc as _bacc
    from concourse import mybir as _mybir
    from concourse.bass_utils import run_bass_kernel_spmd as _run

    nc = _bacc.Bacc("TRN2", target_bir_lowering=False, num_devices=1)
    arrays, A = {}, {}
    for name in _INS:
        a = _np.ascontiguousarray(inputs[name])
        if name not in ("c",):
            a = a.reshape(a.shape[1:])
        if name == "r_k":
            a = a.reshape(-1)
        arrays[f"in_{name}"] = a
        A[name] = nc.dram_tensor(f"in_{name}", a.shape, _mybir.dt.from_np(a.dtype), kind="ExternalInput").ap()
    arrays["in_consts"] = CONSTS
    A["consts"] = nc.dram_tensor("in_consts", CONSTS.shape, _mybir.dt.float32, kind="ExternalInput").ap()
    out = nc.dram_tensor("out", (SEQ, D), _mybir.dt.float32, kind="ExternalOutput").ap()
    hybrid_layer(nc, A, out)
    r = _run(nc, [arrays], core_ids=[0])
    return r.results[0]["out"].reshape(1, SEQ, D)
```

```python
import numpy as np
import concourse.bass as bass
from concourse import mybir
from contextlib import ExitStack

P = 128
SEQ, D = 512, 1024
TT = SEQ // P
KT = D // P
HD = 64
HEADS = 8
W = HEADS * HD
CT = W // P
RW_COLS, ATT_COLS = 3 * W + 256, 3 * W
CH = 64
NCH = SEQ // CH
DECAY = 0.606531
LN_X_EPS, NORM_EPS = 64e-5, 1e-6
NEXP, GROUPS, EPG = 32, 4, 8
DE = D // 2
SLOTS = 64
MAXOV = 15
NPASS = NEXP + MAXOV
NEG = -1e30
BIG_INDEX = 1 << 20


def shape_constants():
    i = np.arange(P)
    r, c = i[:, None], i[None, :]
    same = (r // CH) == (c // CH)
    eye = np.eye(P)
    parts = {"ident": eye,
             "before": (r < c) * 1.0,
             "causal_t": np.concatenate([same & (r < c), same & (r <= c)], 1) * 1.0}
    for n, m in enumerate([1, 2, 4, 8, 16, 32]):
        low = (r // (2 * m) == c // (2 * m)) & (r // m % 2 == 1) & (c // m % 2 == 0)
        parts[f"level{n}"] = low + eye
        if n == 0:
            parts["level0_t"] = low.T + eye
    parts["head_ones"] = same * 1.0
    parts["scan_keep"] = np.broadcast_to((np.arange(SEQ) % CH != 0) * 1.0, (P, SEQ))
    parts["diag_mask"] = np.where(c <= r, 0.0, NEG)
    half = HD // 2
    inv_freq = 10000.0 ** (-np.arange(half, dtype=np.float32) / half)
    ang = np.arange(SEQ, dtype=np.float32)[:, None] * inv_freq[None, :].astype(np.float32)
    cos, sin = np.cos(ang), np.sin(ang)
    tiles = lambda a: a.reshape(TT, P, HD).transpose(1, 0, 2).reshape(P, TT * HD)
    parts["cos2"] = tiles(np.concatenate([cos, cos], 1))
    parts["sin2"] = tiles(np.concatenate([-sin, sin], 1))
    parts["expert_id"] = np.broadcast_to(np.arange(NEXP), (P, NEXP))
    parts["first_wins"] = np.broadcast_to(NEXP - np.arange(NEXP), (P, NEXP))
    parts["pass_starts"] = np.broadcast_to(SLOTS * np.arange(1, SEQ // SLOTS), (P, SEQ // SLOTS - 1))
    parts["token_id"] = i[:, None] + P * np.arange(TT)[None, :]
    at, cols = {}, 0
    for k, v in parts.items():
        at[k] = (cols, v.shape[1])
        cols += v.shape[1]
    return np.ascontiguousarray(np.concatenate([np.asarray(v, np.float32) for v in parts.values()], 1)), at


CONSTS, CONST_AT = shape_constants()


def hybrid_layer(nc, A, out):
    f32, f32r, i32, u32 = mybir.dt.float32, mybir.dt.float32r, mybir.dt.int32, mybir.dt.uint32
    ALU, ACT, AX = mybir.AluOpType, mybir.ActivationFunctionType, mybir.AxisListType
    IOA = bass.IndirectOffsetOnAxis

    ctx = ExitStack()
    with ctx:
        def sem(name):
            return ctx.enter_context(nc.semaphore(name))

        def pool_of(stack):
            return lambda name, shape, dt=f32: stack.enter_context(nc.sbuf_tensor(name, shape, dt))

        keep = pool_of(ctx)
        consts = keep("consts", [P, CONSTS.shape[1]])
        mod = keep("mod", [P, 8, 512])
        NRING = 3
        parts_stack = ExitStack()
        sbr = pool_of(parts_stack)
        x_r, ring_r, hT_r, zr_r = (sbr(n, shape, f32r) for n, shape in (
            ("x_r", [P, KT, 512]), ("ring_r", [P, NRING, KT, 512]), ("hT_r", [P, KT, SEQ]), ("zr_r", [P, 14, SEQ])))
        mid_r = sbr("mid_r", [P, 2 * CT * SEQ + TT * 3 * W], f32r)
        tokm_r = sbr("tokm_r", [P, TT, CT, 4, P], f32r)
        parts_stack.close()
        x = keep("x", [P, TT, D])
        bank = [ctx.enter_context(nc.psum_tensor(f"bank{i}", [P, 512], f32)) for i in range(8)]

        def const(name, parts=P):
            at, n = CONST_AT[name]
            return consts[0:parts, at:at + n]

        ident = const("ident")

        first = ExitStack()
        sb = pool_of(first)
        ring = sb("ring", [P, NRING, KT, 512])
        hT = sb("hT", [P, KT, SEQ])
        zr = sb("zr", [P, 14, SEQ])
        ahat = sb("ahat", [P, CT, SEQ])
        bhat = sb("bhat", [P, CT, SEQ])
        qkv = sb("qkv", [P, TT, 3 * W])
        tokm = sb("tokm", [P, TT, CT, 4, P])
        cols = sb("cols", [P, 14 + 14 + 4 * 8 + 16 + 8 + 16])
        small = sb("small", [P, 64])
        eps_x = small[:, 60:61]
        prow = tokm[:, 3, 2, 0, :]
        mu, mu1 = cols[:, 0:14], cols[:, 14:28]
        col = {n: cols[:, 28 + 4 * i:32 + 4 * i] for i, n in
               enumerate(["w0", "a0", "k_k", "k_a", "r_k", "lnx_g", "lnx_b", "k_a1"])}
        bias1, ln1 = cols[:, 60:76], cols[:, 76:84]
        shift1, scale1 = cols[:, 84:92], cols[:, 92:100]
        one = small[:, 59:60]
        x_n = qkv[:, :, 0:D]
        def ada_acc(n):
            tiles_of = ((2, 2), (2, 3)) if n % 2 == 0 else ((3, 2), (3, 1)) if n < 11 else ((3, 2), (1, 3))
            return [tokm[:, t, i, :, :].rearrange("p a b -> p (a b)") for t, i in tiles_of]


        xs = [x[:, i // 2, 512 * (i % 2):512 * (i % 2) + 512] for i in range(8)]
        lora_wa = tokm[:, 3, 3, :, :].rearrange("p a b -> p (a b)")
        lora_g = xs[7]
        decay_end = sb("decay_end", [P, CT, NCH])
        decay_end8 = sb("decay_end8", [HD, HEADS, NCH])
        flat = ring[:, :, :, :].rearrange("p s k n -> p (s k n)")

        def pair(i, parts=P, n=512, off=0):
            return [flat[0:parts, 512 * (i + 12 * g) + off:512 * (i + 12 * g) + off + n].rearrange("p (h n) -> p h n", h=4)
                    for g in range(2)]

        TT1, RB, AK, RK, INV, INVT, PP, WU = (pair(i) for i in range(8))
        QQ = pair(8, HD)
        GG = [pair(9, HD, 256), pair(9, HD, 256, 256)]
        HH = [xs[3][0:HD, :], xs[4][0:HD, :]]
        XX, DE_ = pair(11, P, 256), pair(11, HD, 256, 256)
        STATE = [xs[i][0:HD, :].rearrange("p (h n) -> p h n", h=HEADS) for i in range(3)]

        gqk = zr[:, 12, 0:2 * HD].rearrange("p (a d) -> p a d", a=2)
        ssq = zr[:, 12, 128:192]
        rms_qk = zr[:, 12, 192:256]
        stat = zr[:, 12, 256:320]
        qT, kT = (tokm[:, i, :, :, :].rearrange("p c a b -> p c (a b)") for i in range(2))
        PROB = [[flat[:, 512 * (4 * b + i):512 * (4 * b + i) + P * (i + 1)] for i in range(TT)] for b in range(2)]
        PROBT = [[flat[:, 512 * (8 + 4 * b + i):512 * (8 + 4 * b + i) + P * (TT - i)] for i in range(TT)] for b in range(2)]
        S_AT = [bank[1][:, 384:512], bank[2][:, 0:256], bank[1][:, 0:384], bank[0][:, :]]
        PT_AT = [bank[4][:, :], bank[5][:, 0:384], bank[6][:, 0:256], bank[5][:, 384:512]]
        UNITS = ((3,), (2, 0), (1,))
        y_tok = qkv[:, :, 0:W]
        ln2_bc = zr[:, 8:10, :].rearrange("p a n -> p (a n)")
        merged = zr
        msc = [qkv[:, i, 512:1024] for i in range(4)]

        first.close()
        PIECES = 4
        raw = keep("raw", [P, PIECES, 4, DE])
        hi = keep("hi", [P, PIECES, 4, DE], f32r)
        lo = keep("lo", [P, PIECES, 4, DE], f32r)
        w2s = keep("w2s", [P, 2, 4, D])
        picked = keep("picked", [P, 2, D])
        xT = keep("xT", [P, 2, KT, P], f32r)
        half_a, half_b, silu_a, hid = (keep(n, [SLOTS, DE]) for n in ("half_a", "half_b", "silu_a", "hid"))
        hidT = keep("hidT", [P, 4, SLOTS])
        ys = keep("ys", [SLOTS, 2, D])
        gather_at = keep("gather_at", [SLOTS, NPASS], i32)
        entry = keep("entry", [P, 2 * TT, 4], i32)
        entry_row = keep("entry_row", [P, 2 * TT], i32)
        now = keep("now", [P, 4], i32)
        passes = keep("passes", [1, 1 + MAXOV], i32)
        table = keep("table", [SLOTS, NPASS, 4], i32)
        h2 = w2s[:, 0, :, :]
        h2T = w2s[:, 1, :, :].rearrange("p a (b n) -> p (a b) n", b=2)
        rt = picked[:, 1, :]
        rt2 = mod[:, 0:2, :].rearrange("p a n -> p (a n)")
        NR = GROUPS + NEXP
        w_route, b_route = rt[:, 0:KT * NR].rearrange("p (k n) -> p k n", n=NR), rt[:, 288:288 + NR]
        L = rt[:, 324:324 + TT * NR].rearrange("p (t n) -> p t n", n=NR)
        stats = [rt[:, 468 + 4 * i:472 + 4 * i] for i in range(20)]
        ln_stat = rt[:, 548:564]
        gsel, gtmp = (rt[:, 564 + 16 * i:580 + 16 * i].rearrange("p (t n) -> p t n", n=GROUPS) for i in range(2))
        counts, over, over_to, over_from = (rt[:, 596 + 32 * i:628 + 32 * i] for i in range(4))
        ones32 = rt[:, 724:756]
        spare = rt[:, 996:1000]
        steps = rt[:, 772:772 + NEXP * (SEQ // SLOTS - 1)].rearrange("p (n s) -> p n s", s=SEQ // SLOTS - 1)
        pass_tmp = rt[0:1, 756:772]
        fresh = table[:, :, :]
        LE, CAND, PICK1, PICK2, PICKS, RANK = (rt2[:, 128 * i:128 * i + 128].rearrange("p (t n) -> p t n", n=NEXP) for i in range(6))
        ones = rt2[:, 896:1024]
        picked_to = LE
        sum0, sum1 = w2s[:, 0, :, :], w2s[:, 1, :, :]
        h2_table = nc.dram_tensor("h2_table", [SEQ, D], f32).ap()
        slot_table = nc.dram_tensor("slot_table", [SLOTS * NPASS, 4], i32).ap()
        y_rows = nc.dram_tensor("y_rows", [2 * SEQ, D], f32).ap()

        s_const, s_x, s_c, s_cols = sem("s_const"), sem("s_x"), sem("s_c"), sem("s_cols")
        s_bias2 = sem("s_bias2")
        ring_in = [sem(f"ring_in{i}") for i in range(NRING + 2)]
        ada_chain, ada_in, ada_mm, ada_out = sem("ada_chain"), sem("ada_in"), sem("ada_mm"), sem("ada_out")
        s_xn, s_xT, s_mod1 = sem("s_xn"), sem("s_xT"), sem("s_mod1")
        first_turned = sem("first_turned")
        silu_ssq, s_hT = sem("silu_ssq"), sem("s_hT")
        z_mm, z_scaled, z_shifted = sem("z_mm"), sem("z_scaled"), sem("z_shifted")
        att_mm, att_out = sem("att_mm"), sem("att_out")
        s_stat1, s_rstd1 = sem("s_stat1"), sem("s_rstd1")
        dve_chain, pool_chain = sem("dve_chain"), sem("pool_chain")
        s_done = sem("s_done")
        mg_mm, mg_sig, mg_v, out_mm, x2_done = sem("mg_mm"), sem("mg_sig"), sem("mg_v"), sem("out_mm"), sem("x2_done")
        s_gqk, ssq_qk, sqrt_qk, rstd_qk, rope_done = sem("s_gqk"), sem("ssq_qk"), sem("sqrt_qk"), sem("rstd_qk"), sem("rope_done")
        qk_mm, qk_a = sem("qk_mm"), sem("qk_a")
        s_mm, max_v, exp_a = sem("s_mm"), sem("max_v"), sem("exp_a")
        yt_mm, yt_v, h_whole = sem("yt_mm"), sem("yt_v"), sem("h_whole")
        cut_a, cut_v = sem("cut_a"), sem("cut_v")
        pt_mm, pt_v, pt_a, pv_mm, pv_out = sem("pt_mm"), sem("pt_v"), sem("pt_a"), sem("pv_mm"), sem("pv_out")
        s_ln2, s_route_w, ssq2, var2, sqrt2, h2_v = (sem(n) for n in (
            "s_ln2", "s_route_w", "ssq2", "var2", "sqrt2", "h2_v"))
        h2_stored, h2t_mm, h2t_a, h2t_v, logit_mm, picks_v, rank_mm = (sem(n) for n in (
            "h2_stored", "h2t_mm", "h2t_a", "h2t_v", "logit_mm", "picks_v", "rank_mm"))
        exp_in, exp_out, fresh_v, fresh_in, entry_v, entry_in, table_in, gather_v = (sem(n) for n in (
            "exp_in", "exp_out", "fresh_v", "fresh_in", "entry_v", "entry_in", "table_in", "gather_v"))
        raw_in = [sem(f"raw_in{q}") for q in range(4)]
        w2_in = [sem(f"w2_in{b}") for b in range(2)]
        hi_done, lo_done, piece_mm = sem("hi_done"), sem("lo_done"), sem("piece_mm")
        now_p, rows_in, xt_mm, xt_a, xt_v = sem("now_p"), [sem(f"rows_in{b}") for b in range(2)], sem("xt_mm"), sem("xt_a"), sem("xt_v")
        ab_a, a_v, silu_done, b_v, hid_v, ht_mm, ht_a, w2_mm = (sem(n) for n in (
            "ab_a", "a_v", "silu_done", "b_v", "hid_v", "ht_mm", "ht_a", "w2_mm"))
        y_a, y_v, y_out = sem("y_a"), sem("y_v"), [sem(f"y_out{b}") for b in range(2)]
        ov_ready, ov_in, ov_w2, ov_rows, ov_xt, ov_xe_a, ov_xe_v = (sem(n) for n in (
            "ov_ready", "ov_in", "ov_w2", "ov_rows", "ov_xt", "ov_xe_a", "ov_xe_v"))
        ov_hi, ov_lo, ov_mm, ov_half, ov_hid, ov_ht, ov_hte, ov_y, ov_ys, ov_out = (sem(n) for n in (
            "ov_hi", "ov_lo", "ov_mm", "ov_half", "ov_hid", "ov_ht", "ov_hte", "ov_y", "ov_ys", "ov_out"))
        s_sum, s_added, y_stored, s_final = [sem(f"s_sum{t}") for t in range(TT)], sem("s_added"), sem("y_stored"), sem("s_final")
        past = sem("past")
        s_lora_w, s_act_in = sem("s_lora_w"), sem("s_act_in")
        lora_mm, lora_act, sq_act, ss_mm, ss_act = sem("lora_mm"), sem("lora_act"), sem("sq_act"), sem("ss_mm"), sem("ss_act")
        scan_done, exp_act, eprev_in = sem("scan_done"), sem("exp_act"), sem("eprev_in")
        bonus_in, bonus_mm, forms_done = sem("bonus_in"), sem("bonus_mm"), sem("forms_done")
        turn_mm, turn_v, turn_a, prep_done = sem("turn_mm"), sem("turn_v"), sem("turn_a"), sem("prep_done")
        solve_mm, solve_v, solve_a = ([sem(f"{n}{g}") for g in range(2)] for n in ("solve_mm", "solve_v", "solve_a"))
        chain_mm, chain_v, s_de8 = sem("chain_mm"), sem("chain_v"), sem("s_de8")
        gn_mm, gn_v, gn_a = sem("gn_mm"), sem("gn_v"), sem("gn_a")

        w_in = A["w_in"].rearrange("(k p) n -> p k n", p=P)
        w_ada = A["w_ada"].rearrange("(k p) n -> p k n", p=P)
        ada_items = [(w_ada[:, :, 512 * j:512 * j + 512], ada_in, 2 * j + 2) for j in range(12)]
        z_items = [(w_in[:, :, 3 * W:RW_COLS], z_mm, 2)]
        z_items += [(w_in[:, :, 512 * j:512 * j + 512], z_mm, 4 * j + 6) for j in range(3)]
        att_items = [(w_in[:, :, RW_COLS + 512 * j:RW_COLS + 512 * j + 512], att_mm, TT * (j + 1)) for j in range(3)]
        items, first_slots, at_of = [], [], {"ada": [], "z": [], "att": []}
        of = {"ada": ada_items, "z": z_items, "att": att_items}
        for kind, slot in [("ada", 0), ("ada", 1), ("ada", 2), ("ada", 3), ("z", 0), ("z", 1), ("ada", 2), ("ada", 3), ("z", 0), ("ada", 2),
                           ("z", 1), ("ada", 3), ("ada", 2), ("ada", 3), ("att", 0), ("ada", 2), ("att", 1), ("ada", 2), ("att", 0)]:
            items.append(of[kind][len(at_of[kind])])
            at_of[kind].append(len(items) - 1)
            first_slots.append(slot)
        ADA_AT, Z_AT, ATT_AT = at_of["ada"], at_of["z"], at_of["att"]
        w_gate = w_in[:, :, RW_COLS + ATT_COLS:]
        N_BEFORE_MERGE = len(items)
        for b, name in enumerate(("w_br_rwkv", "w_br_moba")):
            items += [(A[name].rearrange("(k p) n -> p k n", p=P), mg_mm, KT * (b + 1))]
            items += [(w_gate[:, :, D * b + 512 * j:D * b + 512 * j + 512], mg_mm, KT * b + 4 * (j + 1)) for j in range(2)]
        items += [(A["w_out"].rearrange("(k p) n -> p k n", p=P)[:, :, 512 * j:512 * j + 512], out_mm, TT * (j + 1)) for j in range(2)]
        slot_of = first_slots + [2, 4, 3, 0, 4, 1, 4, 0]
        nth_in_slot = [slot_of[:i].count(v) + 1 for i, v in enumerate(slot_of)]
        last_in_slot = [max([j for j in range(i) if slot_of[j] == v], default=None) for i, v in enumerate(slot_of)]

        def slot_view(i, k=KT):
            return slot_flat(slot_of[i]).rearrange("p (k n) -> p k n", k=k)

        def slot_flat(v, ring=ring, tokm=tokm):
            return (ring[:, v, :, :].rearrange("p k n -> p (k n)") if v < NRING else
                    tokm[:, (0, 2)[v - NRING]:(2, 4)[v - NRING], :, :, :].rearrange("p t c a b -> p (t c a b)"))

        CUT = [(N_BEFORE_MERGE + i, slot, free) for i, slot, free in ((1, 0, 0), (2, 1, 0), (4, 2, KT), (5, 3, KT), (6, 2, KT + 4), (7, 1, 2 * KT))]
        CUT_H_AT = (5, 6)
        CUT_OF = {c[0]: n for n, c in enumerate(CUT)}
        CUT_AFTER = {0: 1, KT - 1: 2, KT + 1: 3, KT + 5: 4}
        Z_CUTS = 2 * 4 + KT
        Z_CUT_FREE = (0, 0, 2, 6)
        Z_CUT_AFTER = {3: 2, 7: 3}
        z_cut_count = lambda n: 2 * n + (KT if n else 0)
        cut_count = lambda n: Z_CUTS + 2 + 2 * n + (KT if n == 5 else 0)

        def z_cut_views(n):
            return (mid_r[:, KT * 512 * (n % 2):KT * 512 * (n % 2) + KT * 512].rearrange("p (k n) -> p k n", k=KT), ring_r[:, slot_of[Z_AT[n]], :, :])

        def cut_views(i):
            return tuple(slot_flat(v, ring_r, tokm_r).rearrange("p (k n) -> p k n", k=KT) for v in (CUT[CUT_OF[i]][1], slot_of[i]))

        h_hi, h_lo = x_r[:, :, :], hT_r[:, :, :]
        m_hi, m_lo = hT_r[:, :, :], zr_r[:, 0:KT, :]

        Z_TILES = [12, 13] + list(range(12))

        block = ctx.enter_context(nc.Block())

        @block.sync
        def _(sp):
            sp.dma_start(x[:, :, :], A["x"].rearrange("(t p) d -> p t d", p=P)).then_inc(s_x, 16)
            sp.wait_ge(s_c, 16 * 12)
            for i, (src, _, _) in enumerate(items):
                before = last_in_slot[i]
                if before is not None:
                    sp.wait_ge(items[before][1], items[before][2])
                if i == Z_AT[1]:
                    sp.wait_ge(first_turned, 1)
                    sp.dma_start(lora_wa[0:64, :], A["w_lora_up"]).then_inc(s_lora_w, 16)
                    sp.dma_start(lora_wa[64:128, :], A["a_lora_up"]).then_inc(s_lora_w, 16)
                if i == ATT_AT[1]:
                    sp.wait_ge(h_whole, KT)
                    sp.dma_start(lora_g, A["g_lora_up"]).then_inc(s_lora_w, 16)
                if i == N_BEFORE_MERGE:
                    sp.wait_ge(gn_mm, 1)
                if i == N_BEFORE_MERGE + 2:
                    sp.wait_ge(gn_v, 3 * CT)
                    sp.dma_start(ln2_bc, A["ln2_g"].partition_broadcast(P)).then_inc(s_ln2, 16)
                    sp.wait_ge(pv_out, HEADS)
                if i in (N_BEFORE_MERGE + 3, N_BEFORE_MERGE + 5):
                    sp.wait_ge(mg_mm, 4 if i == N_BEFORE_MERGE + 3 else KT)
                if i == N_BEFORE_MERGE + 7:
                    sp.wait_ge(mg_mm, 2 * KT)
                    sp.dma_start(x[:, :, :], A["x"].rearrange("(t p) d -> p t d", p=P)).then_inc(s_x, 16)
                k, n = src.shape[1:]
                dst = slot_view(i)[:, 0:k, 0:n] if n <= 512 else slot_view(i, k)
                sp.dma_start(dst, src).then_inc(ring_in[slot_of[i]], 16)
            sp.wait_ge(x2_done, 2 * TT)
            sp.dma_start(w_route[:, :, 0:GROUPS], A["w_rg"].rearrange("(k p) n -> p k n", p=P)).then_inc(s_route_w, 16)
            sp.dma_start(w_route[:, :, GROUPS:NR], A["w_re"].rearrange("(k p) n -> p k n", p=P)).then_inc(s_route_w, 16)
            sp.dma_start(b_route[:, 0:GROUPS], A["b_rg"].partition_broadcast(P)).then_inc(s_route_w, 16)
            sp.dma_start(b_route[:, GROUPS:NR], A["b_re"].partition_broadcast(P)).then_inc(s_route_w, 16)
            w13 = [A[n].rearrange("e (p k) n -> e p k n", k=KT)[:, :, 4 * half:4 * half + 4, :] for half in range(2) for n in ("w1", "w3")]
            w2_src = A["w2"].rearrange("e (p k) n -> e p k n", k=4)

            def load_pieces(e, pieces=range(PIECES)):
                for q in pieces:
                    if not (isinstance(e, int) and e == 0):
                        sp.wait_ge(lo_done, PIECES * e + q - 3)
                    src = w13[q][e] if isinstance(e, int) else w13[q][bass.ds(e, 1)].rearrange("e p k n -> (e p) k n")
                    sp.dma_start(raw[:, q, :, :], src).then_inc(raw_in[q], 16)

            def load_w2(e, b):
                if not (isinstance(e, int) and e < 2):
                    sp.wait_ge(w2_mm, e - 1)
                src = w2_src[e] if isinstance(e, int) else w2_src[bass.ds(e, 1)].rearrange("e p k n -> (e p) k n")
                sp.dma_start(w2s[:, b, :, :], src).then_inc(w2_in[b], 16)

            load_pieces(0)
            for t in range(TT):
                sp.wait_ge(h2_v, t + 1)
                sp.dma_start(h2_table[P * t:P * t + P, :], h2[:, t, :]).then_inc(h2_stored, 16)
            sp.wait_ge(h2_stored, 16 * TT)
            sp.wait_ge(logit_mm, 1)

            def load_step(e, b):
                load_pieces(e, range(3))
                load_w2(e - 1, 1 - b)
                load_pieces(e, (3,))

            load_w2(0, 0)
            load_w2(1, 1)
            load_pieces(1)
            load_pieces(2)
            with sp.Fori(0, (NEXP - 4) // 2) as i:
                for b in range(2):
                    load_step(2 * i + 3 + b, 1 - b)
            load_step(NEXP - 1, 1)
            load_w2(NEXP - 1, 1)
            n_over = sp.value_load(passes[0:1, 0:1], min_val=0, max_val=MAXOV)
            with sp.If(n_over > 0):
                with sp.Fori(0, n_over) as j:
                    sp.wait_ge(ov_ready, j + 1)
                    e = sp.value_load(passes[0:1, bass.ds(j + 1, 1)], min_val=0, max_val=NEXP - 1)
                    for q in range(PIECES):
                        sp.dma_start(raw[:, q, :, :], w13[q][bass.ds(e, 1)].rearrange("e p k n -> (e p) k n")).then_inc(ov_in, 16)
                    sp.dma_start(w2s[:, 0, :, :], w2_src[bass.ds(e, 1)].rearrange("e p k n -> (e p) k n")).then_inc(ov_w2, 16)
            sp.wait_ge(y_stored, 1)
            both = y_rows.rearrange("(k t p) d -> k p t d", k=2, p=P)
            for t in range(TT):
                for k in range(2):
                    sp.dma_start((sum0, sum1)[k][:, t, :], both[k][:, t, :]).then_inc(s_sum[t], 16)
            for t in range(TT):
                sp.wait_ge(s_final, t + 1)
                sp.dma_start(out[P * t:P * t + P, :], x[:, t, :]).then_inc(s_done, 16)
            sp.wait_ge(s_done, 16 * TT)

        def sum_bank(n):
            return bank[2 if n >= 10 else n % 2][:, :]

        ADA_AFTER = (2, 4, 6, 8, 10, 12)

        def ring_wait(eng, i):
            eng.wait_ge(ring_in[slot_of[i]], 16 * nth_in_slot[i])

        MM_EVENTS = ["ab", "rb", "ak", "rk", "t0", "p1"] + [f"{x}{l + (x == 'p')}" for l in range(1, 5) for x in "npm"] + ["m5"]
        MM_EVENTS += ["x", "wu", "q", "gh0", "gh1", "y"]
        V_EVENTS = ["ab", "tt", "rb", "ak", "rk", "n0", "m0"] + [f"p{l}" for l in range(1, 6)] + ["q", "d0", "g0", "d1", "g1", "y"]
        A_EVENTS = [f"{x}{l}" for l in range(1, 6) for x in "nm" if (x, l) != ("n", 5)] + ["x", "wu", "h0", "h1"]
        mm_at = lambda sc, e: len(MM_EVENTS) * sc + MM_EVENTS.index(e) + 1
        v_at = lambda sc, e: len(V_EVENTS) * sc + V_EVENTS.index(e) + 1
        a_at = lambda sc, e: len(A_EVENTS) * sc + A_EVENTS.index(e) + 1

        def weight_of(e):
            w = table[0:SLOTS, :, 2].bitcast(f32)
            return w[:, e:e + 1] if isinstance(e, int) else w[:, bass.ds(e, 1)]

        def turned(b):
            return bank[b][:, :].rearrange("p (k n) -> p k n", k=KT)

        @block.scalar
        def _(act):
            act.dma_start(ident, A["consts"][:, 0:P]).then_inc(s_c, 16)
            at = 0
            rows_of = [(A["c"][0], 8), (A["mu_shift"], 14)] + [(A[n], CT) for n in ("w0", "a0", "k_k", "k_a", "r_k", "lnx_g", "lnx_b")]
            rows_of += [(A["b_ada"][0:2 * D], 2 * KT), (A["ln1_g"], KT)]
            for src, k in rows_of:
                act.dma_start(prow[at:at + k, :], src.rearrange("(k p) -> k p", p=P)).then_inc(s_c, 16)
                at += k
            act.dma_start(mod[0:1, :, :].rearrange("p a b -> p (a b)"), A["b_ada"][2 * D:6 * D].rearrange("(a n) -> a n", a=1)).then_inc(s_bias2, 16)
            act.wait_ge(s_cols, 1)
            act.activation(small[:, 8:8 + KT], small[:, 0:KT], ACT.Silu).then_inc(silu_ssq, 1)
            act.wait_ge(s_x, 16)
            for t in range(TT):
                act.activation(x_n[:, t, :], x[:, t, :], ACT.Square,
                               accum_out=small[:, 16 + t:17 + t]).then_inc(silu_ssq, 1)
            act.wait_ge(s_stat1, 1)
            act.activation(small[:, 28:32], small[:, 20:24], ACT.Sqrt).then_inc(s_rstd1, 1)
            act.wait_ge(s_stat1, 2)
            for t in range(TT):
                act.activation(x_n[:, t, :], x[:, t, :], ACT.Copy, scale=small[:, 24 + t:25 + t]).then_inc(s_xn, 1)
            act.dma_start(consts[:, P:], A["consts"][:, P:]).then_inc(s_const, 16)
            for k in range(KT):
                act.wait_ge(first_turned, k + 2)
                act.activation(hT[:, k, :], bank[2 + k % 2][:, :], ACT.Copy).then_inc(s_xT, 1)

            def cut_hi(dst, src):
                act.activation(dst, src, ACT.Copy).then_inc(cut_a, 1)

            def cut_z_item(n):
                ring_wait(act, Z_AT[n])
                if Z_CUT_FREE[n]:
                    act.wait_ge(z_mm, Z_CUT_FREE[n])
                cols_ = slice(0, 256 if n == 0 else 512)
                for half in (slice(0, 4), slice(4, 8)):
                    cut_hi(z_cut_views(n)[0][:, half, cols_], slot_view(Z_AT[n])[:, half, cols_])

            cut_z_item(0)
            act.wait_ge(s_mod1, 1)
            act.wait_ge(s_xT, KT)
            for k in range(KT + 1):
                if k < KT:
                    act.activation(hT[:, k, :], hT[:, k, :], ACT.Identity, scale=scale1[:, k:k + 1], bias=shift1[:, k:k + 1]).then_inc(s_hT, 1)
                if k:
                    act.wait_ge(s_hT, k)
                    cut_hi(h_hi[:, k - 1, :], hT[:, k - 1, :])
            cut_z_item(1)
            act.wait_ge(s_mod1, 3)
            for j, ct in enumerate(Z_TILES):
                act.wait_ge(z_mm, j + 1)
                act.activation(zr[:, ct, :], bank[4 + j % 4][:, :], ACT.Copy, scale=mu1[:, ct:ct + 1]).then_inc(z_scaled, 1)
                if j == 1:
                    act.wait_ge(z_shifted, 2)
                    act.activation(zr[0:64, 12, :], zr[0:64, 12, :], ACT.Tanh)
                    act.activation(zr[:, 13, :], zr[:, 13, :], ACT.Sigmoid).then_inc(s_act_in, 1)
                if j in Z_CUT_AFTER:
                    cut_z_item(Z_CUT_AFTER[j])

            def att_copy(j):
                act.wait_ge(att_mm, j + 1)
                act.activation(qkv[:, j % TT, 512 * (j // TT):512 * (j // TT) + 512], bank[6 + j % 2][:, :], ACT.Copy).then_inc(att_out, 1)

            for ct in range(CT):
                r_, k_, c1 = zr[:, ct, :], zr[:, 4 + ct, :], slice(ct, ct + 1)
                if ct:
                    act.wait_ge(prep_done, ct)
                if ct == 0:
                    act.wait_ge(h_whole, KT)
                act.wait_ge(lora_mm, 2 * ct + 1)
                act.activation(xs[0], bank[0][:, :], ACT.Sigmoid, bias=col["w0"][:, c1]).then_inc(lora_act, 1)
                act.wait_ge(lora_mm, 2 * ct + 2)
                act.activation(xs[1], bank[1][:, :], ACT.Sigmoid, bias=col["a0"][:, c1]).then_inc(lora_act, 1)
                act.activation(xs[2], k_, ACT.Square, scale=col["k_k"][:, c1]).then_inc(sq_act, 1)
                act.wait_ge(scan_done, ct + 1)
                act.activation(xs[6], xs[3], ACT.Exp, scale=-DECAY).then_inc(exp_act, 1)
                act.wait_ge(eprev_in, ct + 1)
                act.activation(xs[0], xs[0], ACT.Exp, scale=-DECAY).then_inc(exp_act, 1)
                act.activation(xs[3], xs[3], ACT.Exp, scale=DECAY).then_inc(exp_act, 1)
                act.wait_ge(ss_mm, ct + 1)
                act.activation(xs[2], bank[2][:, :], ACT.Sqrt).then_inc(ss_act, 1)
                att_copy(3 * ct)
                att_copy(3 * ct + 1)
                for t in (1, 3):
                    act.wait_ge(turn_mm, TT * ct + t + 1)
                    act.activation(tokm[:, t, ct, :, :].rearrange("p a b -> p (a b)"), bank[5][:, :], ACT.Copy).then_inc(turn_a, 1)
                att_copy(3 * ct + 2)
            for sc in range(TT):
                if sc == 2:
                    act.wait_ge(ssq_qk, 1)
                    act.activation(rms_qk, ssq, ACT.Sqrt).then_inc(sqrt_qk, 1)
                for ev in A_EVENTS:
                    for g in range(2):
                        B = bank[4 * g:4 * g + 4]
                        act.wait_ge(solve_mm[g], mm_at(sc, ev if ev[0] != "h" else "gh" + ev[1]))
                        if ev[0] == "h":
                            c = int(ev[1])
                            if c == 1:
                                act.wait_ge(solve_a[g], a_at(sc, "h0"))
                            if sc and c == 0:
                                act.wait_ge(chain_v, 2 * sc)
                            src, dst = B[3 if c == 0 else 0][0:HD, 256:512], HH[c][:, 256 * g:256 * g + 256]
                        else:
                            src, dst = {"n": (B[2], INV), "m": (B[3], INVT), "x": (B[0], XX), "w": (B[2], WU)}[ev[0]]
                            n = 256 if ev == "x" else 512
                            src, dst = src[:, 0:n], dst[g].rearrange("p h n -> p (h n)")
                        act.activation(dst, src, ACT.Copy).then_inc(solve_a[g], 1)
            act.wait_ge(rope_done, 2 * TT)
            for ct in range(CT):
                act.wait_ge(gn_mm, 2 * CT if ct == CT - 1 else CT + ct + 1)
                act.activation(xs[4 + ct], bank[4 + ct][:, :], ACT.Copy).then_inc(gn_a, 1)
            for ct in range(CT):
                act.wait_ge(gn_mm, 2 * CT + ct + 1)
                act.activation(xs[ct], bank[ct][:, :], ACT.Sqrt, bias=eps_x, scale=1.0 / HD).then_inc(gn_a, 1)
            for j in range(8):
                act.wait_ge(qk_mm, j + 1)
                act.activation((qT, kT)[j // 4][:, j % 4, :], bank[4 + j % 4][:, :], ACT.Copy).then_inc(qk_a, 1)

            def exps(h):
                if h >= 2:
                    act.wait_ge(pt_mm, h - 1)
                act.wait_ge(max_v, h + 1)
                for unit in UNITS:
                    for i in unit:
                        act.activation(PROB[h % 2][i], S_AT[i], ACT.Exp, bias=stat[:, 4 * (h % 2) + i:4 * (h % 2) + i + 1], scale=HD ** -0.5,
                                       accum_out=stat[:, 8 + 4 * (h % 4) + i:9 + 4 * (h % 4) + i]).then_inc(exp_a, 1)

            def cut_item(n):
                i, _, free = CUT[n]
                ring_wait(act, i)
                if free:
                    act.wait_ge(mg_mm, free)
                for half in (slice(0, 4), slice(4, 8)):
                    cut_hi(cut_views(i)[0][:, half, :], slot_view(i)[:, half, :])

            exps(0)
            for h in range(HEADS):
                if h + 1 < HEADS:
                    exps(h + 1)
                act.wait_ge(pt_mm, h + 1)
                if h >= 2:
                    act.wait_ge(pv_mm, h - 1)
                for i in (0, 2):
                    act.activation(PROBT[h % 2][i], PT_AT[i], ACT.Copy).then_inc(pt_a, 1)
                if h in CUT_H_AT:
                    half = slice(4 * CUT_H_AT.index(h), 4 * CUT_H_AT.index(h) + 4)
                    act.wait_ge(gn_v, 3 * CT)
                    cut_hi(h_hi[:, half, :], hT[:, half, :])
            cut_item(0)
            for j in range(2 * KT):
                act.wait_ge(mg_mm, j + 1)
                if j >= 2:
                    act.wait_ge(mg_v, j - 1)
                act.activation(msc[j % 2], bank[2 + j % 2][:, :], ACT.Sigmoid).then_inc(mg_sig, 1)
                if j in CUT_AFTER:
                    cut_item(CUT_AFTER[j])
            for k in range(KT):
                act.wait_ge(mg_v, KT + k + 1)
                if k == 0:
                    act.wait_ge(mg_mm, 2 * KT)
                cut_hi(m_hi[:, k, :], merged[:, k, :])
            cut_item(5)
            for t in range(TT):
                act.wait_ge(x2_done, TT + t + 1)
                if t == 0:
                    act.activation(spare, const("token_id"), ACT.Sqrt)
                act.activation(h2[:, t, :], x[:, t, :], ACT.Square, accum_out=ln_stat[:, t:t + 1]).then_inc(ssq2, 1)
            act.wait_ge(var2, 1)
            act.activation(ln_stat[:, 8:12], ln_stat[:, 4:8], ACT.Sqrt).then_inc(sqrt2, 1)
            for k in range(0, KT, 2):
                act.wait_ge(h2t_mm, k + 1)
                act.activation(h2T[:, k, :], bank[4 + k % 4][:, :], ACT.Copy).then_inc(h2t_a, 1)
            def split_hi(q):
                return act.activation(hi[:, q, :, :], raw[:, q, :, :], ACT.Copy)

            def hi_piece(e, q):
                act.wait_ge(raw_in[q], 16 * e + 16)
                if not (isinstance(e, int) and e == 0):
                    act.wait_ge(piece_mm, PIECES * e + q - 3)
                split_hi(q).then_inc(hi_done, 1)

            for q in range(PIECES):
                hi_piece(0, q)
            for i, n in ((1, 16), (2, 4)):
                act.wait_ge(exp_in, i)
                ap = gtmp if i == 1 else stats[5]
                act.activation(ap, ap, ACT.Exp).then_inc(exp_out, 1)

            def y_half(e, b):
                act.wait_ge(w2_mm, e + 1)
                if not (isinstance(e, int) and e < 2):
                    act.wait_ge(y_out[b], 16 * (e // 2))
                act.activation(ys[:, b, 0:512], bank[5][0:SLOTS, :], ACT.Copy, scale=weight_of(e)).then_inc(y_a, 1)

            def turn_x(e, b):
                act.wait_ge(xt_mm, e + 1)
                act.activation(xT[:, b, :, 0:SLOTS], turned(b), ACT.Copy).then_inc(xt_a, 1)

            def halves(e):
                act.wait_ge(piece_mm, PIECES * e + 4)
                if not (isinstance(e, int) and e == 0):
                    act.wait_ge(b_v, e)
                act.activation(half_a[:, :], bank[2][SLOTS:P, :], ACT.Copy).then_inc(ab_a, 1)
                act.activation(half_b[:, :], bank[3][SLOTS:P, :], ACT.Copy).then_inc(ab_a, 1)
                act.wait_ge(a_v, e + 1)
                act.activation(silu_a[:, :], half_a[:, :], ACT.Silu).then_inc(silu_done, 1)

            def turn_hid(e):
                act.wait_ge(ht_mm, e + 1)
                act.activation(hidT[:, :, :].rearrange("p k n -> p (k n)"), bank[4][:, 0:4 * SLOTS], ACT.Copy).then_inc(ht_a, 1)

            def act_step(e, b, last=False, head=0):
                if head >= 2:
                    y_half(e - 2, b)
                if not last:
                    hi_piece(e + 1, 0)
                    hi_piece(e + 1, 1)
                if head >= 1:
                    turn_hid(e - 1)
                if not last:
                    hi_piece(e + 1, 2)
                    turn_x(e + 1, 1 - b)
                    hi_piece(e + 1, 3)
                halves(e)

            turn_x(0, 0)
            act_step(0, 0)
            act_step(1, 1, head=1)
            act_step(2, 0, head=2)
            act_step(3, 1, head=2)
            with act.Fori(0, (NEXP - 6) // 2) as i:
                for b in range(2):
                    act_step(2 * i + 4 + b, b, head=2)
            act_step(NEXP - 2, 0, head=2)
            act_step(NEXP - 1, 1, head=2, last=True)
            y_half(NEXP - 2, 0)
            turn_hid(NEXP - 1)
            y_half(NEXP - 1, 1)
            n_over = act.value_load(passes[0:1, 0:1], min_val=0, max_val=MAXOV)
            with act.If(n_over > 0):
                with act.Fori(0, n_over) as j:
                    act.wait_ge(ov_ready, j + 1)
                    act.wait_ge(ov_in, 64 * j + 64)
                    for q in range(PIECES):
                        split_hi(q).then_inc(ov_hi, 1)
                    act.wait_ge(ov_xt, j + 1)
                    act.activation(xT[:, 0, :, 0:SLOTS], turned(0), ACT.Copy).then_inc(ov_xe_a, 1)
                    act.wait_ge(ov_mm, j + 1)
                    act.activation(half_a[:, :], bank[2][SLOTS:P, :], ACT.Copy).then_inc(ov_half, 1)
                    act.activation(half_b[:, :], bank[3][SLOTS:P, :], ACT.Copy).then_inc(ov_half, 1)
                    act.wait_ge(ov_hid, 2 * j + 1)
                    act.activation(silu_a[:, :], half_a[:, :], ACT.Silu).then_inc(ov_half, 1)
                    act.wait_ge(ov_ht, j + 1)
                    act.activation(hidT[:, :, :].rearrange("p k n -> p (k n)"), bank[4][:, 0:4 * SLOTS], ACT.Copy).then_inc(ov_hte, 1)
                    act.wait_ge(ov_y, j + 1)
                    act.activation(ys[:, 0, 0:512], bank[5][0:SLOTS, :], ACT.Copy, scale=weight_of(NEXP + j)).then_inc(ov_ys, 1)


        @block.gpsimd
        def _(pool):
            made = [0]

            def seq(ins):
                made[0] += 1
                ins.then_inc(pool_chain, 1)
                pool.wait_ge(pool_chain, made[0])

            pool.wait_ge(prep_done, CT)
            pool.wait_ge(lora_mm, 2 * CT)
            pool.dma_start(gqk[:, 0, :], A["q_norm_g"].partition_broadcast(P)).then_inc(s_gqk, 16)
            pool.dma_start(gqk[:, 1, :], A["k_norm_g"].partition_broadcast(P)).then_inc(s_gqk, 16)
            pool.wait_ge(att_out, 12)
            heads = lambda ap: ap.rearrange("p (h d) -> p h d", d=HD)
            for i in range(2 * TT):
                t, q = i // 2, heads(qkv[:, i // 2, W * (i % 2):W * (i % 2) + W])
                seq(pool.tensor_tensor(heads(xs[5]), q, q, ALU.mult))
                n = HD // 2
                while n >= 1:
                    a = heads(xs[5])
                    dst = a[:, :, 0:n] if n > 1 else ssq[:, 8 * i:8 * i + 8].unsqueeze(2)
                    seq(pool.tensor_tensor(dst, a[:, :, 0:n], a[:, :, n:2 * n], ALU.add))
                    n //= 2
            pool.tensor_scalar(ssq, ssq, 1.0 / HD, NORM_EPS, ALU.mult, ALU.add).then_inc(ssq_qk, 1)
            pool.wait_ge(rstd_qk, 1)
            pool.wait_ge(s_gqk, 32)
            for i in range(2 * TT):
                t, q = i // 2, heads(qkv[:, i // 2, W * (i % 2):W * (i % 2) + W])
                bc = lambda ap: ap.unsqueeze(1).to_broadcast([P, HEADS, ap.shape[1]])
                cos2, sin2 = (bc(const(n)[:, HD * t:HD * t + HD]) for n in ("cos2", "sin2"))
                seq(pool.tensor_tensor(q, q, ssq[:, 8 * i:8 * i + 8].unsqueeze(2).to_broadcast([P, HEADS, HD]), ALU.mult))
                seq(pool.tensor_tensor(q, q, bc(gqk[:, i % 2, :]), ALU.mult))
                half = HD // 2
                t1 = heads(xs[5])
                pool.tensor_tensor(t1[:, :, 0:half], q[:, :, half:HD], sin2[:, :, 0:half], ALU.mult)
                seq(pool.tensor_tensor(t1[:, :, half:HD], q[:, :, 0:half], sin2[:, :, half:HD], ALU.mult))
                seq(pool.tensor_tensor(q, q, cos2, ALU.mult))
                pool.tensor_tensor(q, q, t1, ALU.add).then_inc(rope_done, 1)
                pool.wait_ge(rope_done, i + 1)

            pool.wait_ge(x2_done, 2 * TT)
            pool.memset(fresh, BIG_INDEX).then_inc(fresh_v, 1)
            pool.wait_ge(fresh_v, 1)
            pool.dma_start(slot_table.rearrange("(p n) c -> p n c", p=SLOTS), fresh).then_inc(fresh_in, 16)
            pool.memset(picked[0:SLOTS, 0, :], 0.0).then_inc(fresh_v, 1)
            pool.wait_ge(fresh_in, 16)
            pool.wait_ge(entry_v, 1)
            for j in range(2 * TT):
                pool.indirect_dma_start(slot_table, IOA(entry_row[:, j:j + 1].bitcast(u32), 0), entry[:, j, :], None,
                                        bounds_check=SLOTS * NPASS - 1, oob_is_err=False).then_inc(entry_in, 16)
            pool.wait_ge(entry_in, 16 * 2 * TT)
            pool.dma_start(table[:, :, :], slot_table.rearrange("(p n) c -> p n c", p=SLOTS)).then_inc(table_in, 16)
            pool.wait_ge(h2_stored, 16 * TT)

            def current(src, at, e):
                n = src.shape[0]
                pool.sem_inc(past, 1)
                pool.tensor_copy(now[0:n, at:at + 1], src[:, e:e + 1] if isinstance(e, int) else src[:, bass.ds(e, 1)]).then_inc(now_p, 1)

            def gather(b, e, sem_):
                current(gather_at[:, :], b, e)
                pool.wait_ge(now_p, now_n(e, 0))
                pool.sem_inc(past, 1)
                pool.indirect_dma_start(picked[0:SLOTS, b, :], None, h2_table, IOA(now[0:SLOTS, b:b + 1].bitcast(u32), 0),
                                        bounds_check=SEQ - 1, oob_is_err=False).then_inc(sem_, 16)

            def scatter(b, e, sem_):
                current(table[0:SLOTS, :, 1], 2 + b, e)
                pool.wait_ge(now_p, now_n(e, 1))
                pool.sem_inc(past, 1)
                pool.indirect_dma_start(y_rows, IOA(now[0:SLOTS, 2 + b:3 + b].bitcast(u32), 0), ys[:, b, :], None,
                                        bounds_check=2 * SEQ - 1, oob_is_err=False).then_inc(sem_, 16)

            def now_n(e, scattering):
                if scattering:
                    return 2 * e + 6 if not isinstance(e, int) or e < NEXP - 4 else NEXP + e + 1
                return e + 1 if isinstance(e, int) and e < 4 else 2 * e - 3

            pool.wait_ge(gather_v, 2)
            gather(0, 0, rows_in[0])
            gather(1, 1, rows_in[1])

            def gather_next(e, b):
                pool.wait_ge(xt_mm, e + 1)
                gather(b, e + 2, rows_in[b])

            def scatter_last(e, b):
                pool.wait_ge(y_a, e + 1)
                pool.wait_ge(y_v, e + 1)
                scatter(b, e, y_out[b])

            gather_next(0, 0)
            gather_next(1, 1)
            with pool.Fori(0, (NEXP - 4) // 2) as i:
                for b in range(2):
                    gather_next(2 * i + 2 + b, b)
                    scatter_last(2 * i + b, b)
            for e in range(NEXP - 4, NEXP):
                scatter_last(e, e % 2)
            for b in range(2):
                pool.wait_ge(y_out[b], 16 * NEXP // 2)
            n_over = pool.value_load(passes[0:1, 0:1], min_val=0, max_val=MAXOV)
            with pool.If(n_over > 0):
                with pool.Fori(0, n_over) as j:
                    pool.wait_ge(ov_ready, j + 1)
                    current(gather_at[:, :], 0, j + NEXP)
                    pool.wait_ge(now_p, 2 * j + 2 * NEXP + 1)
                    pool.sem_inc(past, 1)
                    pool.indirect_dma_start(picked[0:SLOTS, 0, :], None, h2_table, IOA(now[0:SLOTS, 0:1].bitcast(u32), 0),
                                            bounds_check=SEQ - 1, oob_is_err=False).then_inc(ov_rows, 16)
                    pool.wait_ge(ov_ys, 2 * j + 2)
                    current(table[0:SLOTS, :, 1], 2, j + NEXP)
                    pool.wait_ge(now_p, 2 * j + 2 * NEXP + 2)
                    pool.sem_inc(past, 1)
                    pool.indirect_dma_start(y_rows, IOA(now[0:SLOTS, 2:3].bitcast(u32), 0), ys[:, 0, :], None,
                                            bounds_check=2 * SEQ - 1, oob_is_err=False).then_inc(ov_out, 16)
                    pool.wait_ge(ov_out, 16 * j + 16)
                    pool.sem_inc(ov_ready, 1)
            pool.sem_inc(y_stored, 1)
            for t in range(TT):
                pool.wait_ge(s_sum[t], 32)
                pool.tensor_tensor(sum0[:, t, :], sum0[:, t, :], sum1[:, t, :], ALU.add).then_inc(s_added, 1)

        @block.vector
        def _(dve):
            made = [0]

            def seq(ins):
                made[0] += 1
                ins.then_inc(dve_chain, 1)
                dve.wait_ge(dve_chain, made[0])

            dve.wait_ge(first_turned, 1)
            dve.memset(eps_x, LN_X_EPS)
            dve.memset(one, 1.0)
            dve.tensor_copy(small[:, 0:8], bank[7][:, 0:8])
            dve.tensor_copy(mu, bank[7][:, 8:22])
            dve.tensor_copy(cols[:, 28:56], bank[7][:, 22:50])
            dve.tensor_copy(cols[:, 60:84], bank[7][:, 50:74]).then_inc(s_cols, 1)

            def ada_item(n):
                ring_wait(dve, ADA_AT[n])
                if n >= 2:
                    dve.wait_ge(ada_mm, n - 1)
                w = slot_view(ADA_AT[n])
                for k in range(KT):
                    acc, c_ = ada_acc(n)[k % 2], small[:, 8 + k:9 + k]
                    if k < 2:
                        ins = dve.tensor_scalar(acc, w[:, k, :], c_, None, ALU.mult)
                    else:
                        dve.wait_ge(ada_chain, (KT - 2) * n + k - 1)
                        ins = dve.scalar_tensor_tensor(acc, w[:, k, :], c_, acc, ALU.mult, ALU.add)
                    ins.then_inc(ada_chain if k < KT - 2 else ada_in, 1)

            def ada_bank(n):
                dve.wait_ge(ada_mm, n + 1)
                dve.tensor_copy(mod[:, n - 4, :], sum_bank(n)).then_inc(ada_out, 1)

            dve.wait_ge(silu_ssq, TT + 1)
            dve.tensor_scalar(small[:, 20:24], small[:, 16:20], 1.0 / D, NORM_EPS, ALU.mult, ALU.add).then_inc(s_stat1, 1)
            dve.wait_ge(s_rstd1, 1)
            dve.reciprocal(small[:, 24:28], small[:, 28:32]).then_inc(s_stat1, 1)
            for n in range(4):
                ada_item(n)
            dve.wait_ge(ada_mm, 4)
            seq(dve.tensor_tensor(cols[:, 84:100], bank[0][:, 0:16], bias1, ALU.add))
            dve.scalar_tensor_tensor(scale1, scale1, 1.0, ln1, ALU.add, ALU.mult).then_inc(s_mod1, 1)

            def cut_lo(dst, src, hi_, n):
                dve.wait_ge(cut_a, n)
                dve.tensor_tensor(dst, src, hi_.bitcast(f32), ALU.subtract).then_inc(cut_v, 1)

            def cut_z_item(n):
                cols_ = slice(0, 256 if n == 0 else 512)
                hi_, lo_ = z_cut_views(n)
                for a, half in enumerate((slice(0, 4), slice(4, 8))):
                    cut_lo(lo_[:, half, cols_], slot_view(Z_AT[n])[:, half, cols_], hi_[:, half, cols_], z_cut_count(n) + a + 1)

            cut_z_item(0)
            for k in range(KT):
                cut_lo(h_lo[:, k, :], hT[:, k, :], h_hi[:, k, :], 2 + k + 1)
            cut_z_item(1)
            dve.tensor_scalar(col["k_a1"], col["k_a"], -1.0, 1.0, ALU.mult, ALU.add).then_inc(s_mod1, 1)
            dve.tensor_scalar(mu1, mu, -1.0, 1.0, ALU.mult, ALU.add).then_inc(s_mod1, 1)
            for j, ct in enumerate(Z_TILES):
                dve.wait_ge(z_scaled, j + 1)
                dve.scalar_tensor_tensor(zr[:, ct, 1:SEQ], bank[4 + j % 4][:, 0:SEQ - 1], mu[:, ct:ct + 1], zr[:, ct, 1:SEQ],
                                         ALU.mult, ALU.add).then_inc(z_shifted, 1)
                if j in Z_CUT_AFTER:
                    cut_z_item(Z_CUT_AFTER[j])
                if j in ADA_AFTER:
                    n = 4 + ADA_AFTER.index(j)
                    ada_item(n)
                    if n > 4:
                        ada_bank(n - 1)
            for k in range(KT):
                dve.tensor_tensor(hT[:, k, :], h_hi[:, k, :].bitcast(f32), h_lo[:, k, :].bitcast(f32), ALU.add).then_inc(h_whole, 1)
                if k == KT // 2:
                    ada_bank(9)
            dve.wait_ge(s_const, 16)
            chunks = lambda ap: ap.rearrange("p (c s) -> p c s", s=CH)
            for ct in range(CT):
                r_, k_, v_, c1 = zr[:, ct, :], zr[:, 4 + ct, :], zr[:, 8 + ct, :], slice(ct, ct + 1)
                dve.wait_ge(lora_act, 2 * ct + 1)
                dve.tensor_tensor_scan(xs[3], const("scan_keep"), xs[0], 0.0, ALU.mult, ALU.add).then_inc(scan_done, 1)
                dve.wait_ge(scan_done, ct + 1)
                dve.tensor_tensor(xs[0], xs[3], xs[0], ALU.subtract).then_inc(eprev_in, 1)
                dve.wait_ge(lora_act, 2 * ct + 2)
                seq(dve.tensor_scalar(xs[5], xs[1], col["k_a"][:, c1], col["k_a1"][:, c1], ALU.mult, ALU.add))
                dve.wait_ge(sq_act, ct + 1)
                seq(dve.tensor_scalar(xs[4], k_, col["k_k"][:, c1], None, ALU.mult))
                seq(dve.tensor_tensor(k_, k_, xs[5], ALU.mult))
                dve.scalar_tensor_tensor(xs[5], r_, col["r_k"][:, c1], k_, ALU.mult, ALU.mult).then_inc(bonus_in, 1)
                dve.wait_ge(ss_act, ct + 1)
                seq(dve.tensor_scalar(xs[2], xs[2], 1e-12, None, ALU.max))
                seq(dve.reciprocal(xs[2], xs[2]))
                seq(dve.tensor_tensor(xs[4], xs[4], xs[2], ALU.mult))
                dve.wait_ge(exp_act, 3 * ct + 3)
                dve.tensor_tensor(ahat[:, ct, :], xs[4], xs[0], ALU.mult)
                seq(dve.scalar_tensor_tensor(xs[1], xs[4], -1.0, xs[1], ALU.mult, ALU.mult))
                dve.tensor_copy(decay_end[:, ct, :], chunks(xs[6])[:, :, CH - 1])
                seq(dve.tensor_tensor(bhat[:, ct, :], xs[1], xs[3], ALU.mult))
                seq(dve.tensor_tensor(k_, k_, xs[3], ALU.mult))
                seq(dve.tensor_tensor(r_, r_, xs[6], ALU.mult))
                end = decay_end[:, ct, :].unsqueeze(2).to_broadcast([P, NCH, CH])
                dve.tensor_tensor(chunks(xs[1]), chunks(bhat[:, ct, :]), end, ALU.mult)
                dve.tensor_tensor(chunks(xs[4]), chunks(k_), end, ALU.mult).then_inc(forms_done, 1)
                for t in (0, 2):
                    dve.wait_ge(turn_mm, TT * ct + t + 1)
                    dve.tensor_copy(tokm[:, t, ct, :, :].rearrange("p a b -> p (a b)"), bank[4][:, :]).then_inc(turn_v, 1)
                dve.wait_ge(bonus_mm, ct + 1)
                dve.wait_ge(turn_mm, TT * (ct + 1))
                dve.tensor_tensor(v_, v_, bank[3][:, :], ALU.mult).then_inc(prep_done, 1)
                if ct in (1, 2):
                    ada_bank(9 + ct)
                if ct in (0, 1):
                    ada_item(10 + ct)
            for h in range(HEADS):
                ins = dve.tensor_copy(decay_end8[:, h, :], decay_end[HD * (h % 2):HD * (h % 2) + HD, h // 2, :])
            ins.then_inc(s_de8, 1)
            dve.wait_ge(s_de8, 1)

            def bc4(name, at=0, n=P, parts=P):
                return const(name, parts)[:, at:at + n].unsqueeze(1).to_broadcast([parts, 4, n])

            def f4(ap):
                return ap.rearrange("p (h n) -> p h n", h=4)

            for sc in range(TT):
                toks = slice(P * sc, P * sc + P)
                if sc == 2:
                    dve.wait_ge(sqrt_qk, 1)
                    dve.reciprocal(ssq, rms_qk).then_inc(rstd_qk, 1)
                for ev in V_EVENTS:
                    for g in range(2):
                        B = bank[4 * g:4 * g + 4]
                        if ev in MM_EVENTS and (ev, g) != ("y", 0):
                            dve.wait_ge(solve_mm[g], mm_at(sc, {"ab": "rb", "ak": "rk"}.get(ev, ev)))
                        if ev in ("ab", "rb", "ak", "rk"):
                            strict = ev[0] == "a"
                            dst = {"ab": TT1, "rb": RB, "ak": AK, "rk": RK}[ev][g]
                            mask = const("causal_t")[:, 0 if strict else P:P if strict else 2 * P]
                            for half in range(2):
                                src = f4(B[half + (0 if ev[1] == "b" else 2)])
                                ins = dve.tensor_tensor(dst[:, half::2, :], src[:, 0:2, :] if strict else src[:, 2:4, :],
                                                        mask.unsqueeze(1).to_broadcast([P, 2, P]), ALU.mult)
                        elif ev == "tt":
                            dve.wait_ge(solve_v[g], v_at(sc, "ab"))
                            ins = dve.tensor_tensor(TT1[g], TT1[g], bc4("ident"), ALU.add)
                        elif ev == "n0":
                            dve.wait_ge(solve_mm[g], mm_at(sc, "t0"))
                            ins = dve.tensor_tensor(INV[g], f4(B[0]), bc4("level0"), ALU.mult)
                        elif ev == "m0":
                            dve.wait_ge(solve_v[g], v_at(sc, "tt"))
                            ins = dve.tensor_tensor(INVT[g], TT1[g], bc4("level0_t"), ALU.mult)
                        elif ev[0] == "p":
                            ins = dve.tensor_tensor(PP[g], f4(B[1]), bc4("level" + ev[1]), ALU.mult)
                        elif ev == "q":
                            for half in range(2):
                                ins = dve.tensor_tensor(QQ[g][:, half::2, :], f4(B[1][0:HD, :])[:, half::2, :],
                                                        zr[HD * half:HD * half + HD, 2 * g:2 * g + 2, toks], ALU.add)
                        elif ev[0] == "d":
                            c = int(ev[1])
                            if c == 1:
                                dve.wait_ge(solve_v[g], v_at(sc, "g0"))
                            ins = dve.tensor_tensor(DE_[g], bc4("ident", 0, HD, HD),
                                                    decay_end8[:, 4 * g:4 * g + 4, 2 * sc + c].unsqueeze(2).to_broadcast([HD, 4, HD]), ALU.mult)
                        elif ev[0] == "g":
                            c = int(ev[1])
                            dve.wait_ge(solve_v[g], v_at(sc, f"d{c}"))
                            dve.wait_ge(solve_a[g], a_at(sc, f"h{c}"))
                            ins = dve.tensor_tensor(GG[c][g], f4(B[3 if c == 0 else 0][0:HD, 0:256]), DE_[g], ALU.add)
                        elif ev == "y":
                            if g == 0:
                                for c in range(2):
                                    n = 2 * sc + c
                                    for g2 in range(2):
                                        dve.wait_ge(solve_a[g2], a_at(sc, f"h{c}"))
                                    H = HH[c].rearrange("p (h n) -> p h n", h=HEADS)
                                    if n == 0:
                                        dve.tensor_copy(STATE[1], H).then_inc(chain_v, 1)
                                    else:
                                        dve.wait_ge(chain_mm, n)
                                        dve.tensor_tensor(STATE[(n + 1) % 3], bank[2 if c == 0 else 6][0:HD, :].rearrange("p (h n) -> p h n", h=HEADS),
                                                          H, ALU.add).then_inc(chain_v, 1)
                                dve.wait_ge(solve_mm[g], mm_at(sc, "y"))
                            for half in range(2):
                                ins = dve.tensor_copy(ahat[HD * half:HD * half + HD, 2 * g:2 * g + 2, toks],
                                                      f4(B[1][0:HD, :])[:, half::2, :])
                        ins.then_inc(solve_v[g], 1)
            for g in range(2):
                dve.wait_ge(solve_v[g], v_at(TT - 1, "y"))
            for ct in range(CT):
                dve.wait_ge(gn_mm, ct + 1)
                y_ = ahat[:, ct, :]
                dve.scalar_tensor_tensor(y_, bank[ct][:, :], -1.0 / HD, y_, ALU.mult, ALU.add).then_inc(gn_v, 1)
            for ct in range(CT):
                dve.wait_ge(gn_v, ct + 1)
                dve.tensor_tensor(xs[ct], ahat[:, ct, :], ahat[:, ct, :], ALU.mult).then_inc(gn_v, 1)

            def norm_tile(ct):
                y_, c1 = ahat[:, ct, :], slice(ct, ct + 1)
                dve.wait_ge(gn_a, CT + ct + 1)
                seq(dve.reciprocal(xs[ct], xs[ct]))
                seq(dve.tensor_tensor(y_, y_, xs[ct], ALU.mult))
                seq(dve.tensor_scalar(y_, y_, col["lnx_g"][:, c1], col["lnx_b"][:, c1], ALU.mult, ALU.add))
                seq(dve.tensor_tensor(y_, y_, zr[:, 8 + ct, :], ALU.add))
                dve.tensor_tensor(y_, y_, xs[4 + ct], ALU.mult).then_inc(gn_v, 1)

            def row_max(h):
                b = 4 * (h % 2)
                for u, unit in enumerate(UNITS):
                    dve.wait_ge(s_mm, len(UNITS) * h + u + 1)
                    for i in unit:
                        ins = dve.reduce_max(stat[:, 24 + i:25 + i], S_AT[i], AX.X)
                seq(ins)
                dve.tensor_scalar(stat[:, b:b + 4], stat[:, 24:28], -HD ** -0.5, None, ALU.mult).then_inc(max_v, 1)

            def y_att(h):
                b, r = 8 + 4 * (h % 4), 28 + 4 * (h % 2)
                seq(dve.reciprocal(stat[:, r:r + 4], stat[:, b:b + 4]))
                dve.wait_ge(pv_mm, h + 1)
                dve.tensor_tensor(y_tok[:, :, HD * h:HD * h + HD], bank[3 + 4 * (h % 2)][:, 0:TT * HD].rearrange("p (t n) -> p t n", t=TT),
                                  stat[:, r:r + 4].unsqueeze(2).to_broadcast([P, TT, HD]), ALU.mult).then_inc(pv_out, 1)

            def cut_item(n):
                i = CUT[n][0]
                for a, half in enumerate((slice(0, 4), slice(4, 8))):
                    cut_lo(cut_views(i)[1][:, half, :], slot_view(i)[:, half, :], cut_views(i)[0][:, half, :], cut_count(n) + a + 1)

            row_max(0)
            for h in range(HEADS):
                if h + 1 < HEADS:
                    dve.wait_ge(exp_a, TT * h + TT)
                    row_max(h + 1)
                if h < CT:
                    norm_tile(h)
                dve.wait_ge(pt_mm, h + 1)
                if h >= 2:
                    dve.wait_ge(pv_mm, h - 1)
                for i in (1, 3):
                    dve.tensor_copy(PROBT[h % 2][i], PT_AT[i]).then_inc(pt_v, 1)
                if h:
                    y_att(h - 1)
                if h in CUT_H_AT:
                    half = slice(4 * CUT_H_AT.index(h), 4 * CUT_H_AT.index(h) + 4)
                    cut_lo(h_lo[:, half, :], hT[:, half, :], h_hi[:, half, :], Z_CUTS + CUT_H_AT.index(h) + 1)
            y_att(HEADS - 1)
            cut_item(0)
            for ct in range(CT):
                dve.wait_ge(yt_mm, ct + 1)
                dve.tensor_copy(bhat[:, ct, :], bank[4 + ct][:, :]).then_inc(yt_v, 1)
            for j in range(2 * KT):
                ct = j % KT
                dve.wait_ge(mg_sig, j + 1)
                if j < KT:
                    dve.tensor_tensor(merged[:, ct, :], msc[j % 2], bank[j % 2][:, :], ALU.mult).then_inc(mg_v, 1)
                else:
                    seq(dve.tensor_tensor(msc[j % 2], msc[j % 2], bank[j % 2][:, :], ALU.mult))
                    dve.tensor_tensor(merged[:, ct, :], merged[:, ct, :], msc[j % 2], ALU.add).then_inc(mg_v, 1)
                if j in CUT_AFTER:
                    cut_item(CUT_AFTER[j])
            for k in range(KT):
                cut_lo(m_lo[:, k, :], merged[:, k, :], m_hi[:, k, :], cut_count(4) + 2 + k + 1)
            cut_item(5)
            shift2, a2 = (mod[:, i:i + 2, :].rearrange("p a n -> p (a n)") for i in (2, 4))
            dve.wait_ge(s_ln2, 16)
            seq(dve.scalar_tensor_tensor(a2, a2, 1.0, ln2_bc, ALU.add, ALU.mult))
            dve.wait_ge(s_x, 32)
            for j in range(2 * TT):
                n, t = j // TT, j % TT
                dve.wait_ge(out_mm, j + 1)
                if j >= 4:
                    dve.wait_ge(x2_done, j - 3)
                elif j == 0:
                    dve.wait_ge(mg_v, 2 * KT)
                seq(dve.tensor_tensor(msc[j % 4], bank[4 + t][:, :], mod[:, n, :], ALU.mult))
                xx = x[:, t, 512 * n:512 * n + 512]
                dve.tensor_tensor(xx, xx, msc[j % 4], ALU.add).then_inc(x2_done, 1)
            dve.wait_ge(ssq2, TT)
            dve.tensor_scalar(ln_stat[:, 4:8], ln_stat[:, 0:4], 1.0 / D, NORM_EPS, ALU.mult, ALU.add).then_inc(var2, 1)
            dve.wait_ge(sqrt2, 1)
            seq(dve.reciprocal(ln_stat[:, 12:16], ln_stat[:, 8:12]))
            for t in range(TT):
                seq(dve.scalar_tensor_tensor(h2[:, t, :], x[:, t, :], ln_stat[:, 12 + t:13 + t], a2, ALU.mult, ALU.mult))
                dve.tensor_tensor(h2[:, t, :], h2[:, t, :], shift2, ALU.add).then_inc(h2_v, 1)
            for k in range(1, KT, 2):
                dve.wait_ge(h2t_mm, k + 1)
                dve.tensor_copy(h2T[:, k, :], bank[4 + k % 4][:, :]).then_inc(h2t_v, 1)

            def split_lo(q):
                return dve.tensor_tensor(lo[:, q, :, :], raw[:, q, :, :], hi[:, q, :, :].bitcast(f32), ALU.subtract)

            def lo_piece(e, q):
                dve.wait_ge(hi_done, PIECES * e + q + 1)
                split_lo(q).then_inc(lo_done, 1)

            for q in range(2):
                lo_piece(0, q)

            def of_token(i):
                return stats[i].unsqueeze(2).to_broadcast([P, TT, NEXP])

            def const4(name, n=NEXP):
                return const(name)[:, 0:n].unsqueeze(1).to_broadcast([P, TT, n])

            def pick(dst, values, top, cand, n):
                t4 = stats[top].unsqueeze(2).to_broadcast([P, TT, n])
                seq(dve.reduce_max(stats[top], values, AX.X))
                seq(dve.tensor_tensor(cand, values, t4, ALU.is_equal))
                seq(dve.tensor_tensor(cand, cand, const4("first_wins", n), ALU.mult))
                seq(dve.reduce_max(stats[19], cand, AX.X))
                seq(dve.tensor_tensor(dst, cand, stats[19].unsqueeze(2).to_broadcast([P, TT, n]), ALU.is_equal))

            dve.wait_ge(s_route_w, 64)
            dve.wait_ge(logit_mm, 1)
            seq(dve.tensor_tensor(L, bank[0][:, 0:TT * NR].rearrange("p (t n) -> p t n", n=NR),
                                  b_route.unsqueeze(1).to_broadcast([P, TT, NR]), ALU.add))
            LG = L[:, :, 0:GROUPS]
            pick(gsel, LG, 0, gtmp, GROUPS)
            dve.tensor_tensor(gtmp, LG, stats[0].unsqueeze(2).to_broadcast([P, TT, GROUPS]), ALU.subtract).then_inc(exp_in, 1)
            dve.wait_ge(exp_out, 1)
            seq(dve.reduce_sum(stats[1], gtmp, AX.X))
            seq(dve.reciprocal(stats[1], stats[1]))
            seq(dve.tensor_scalar(gsel, gsel, -NEG, NEG, ALU.mult, ALU.add))
            for t in range(TT):
                ins = dve.tensor_tensor(LE[:, t, :].rearrange("p (g e) -> p g e", g=GROUPS),
                                        L[:, t, GROUPS:NR].rearrange("p (g e) -> p g e", g=GROUPS),
                                        gsel[:, t, :].unsqueeze(2).to_broadcast([P, GROUPS, EPG]), ALU.add)
            seq(ins)
            pick(PICK1, LE, 2, CAND, NEXP)
            seq(dve.scalar_tensor_tensor(LE, PICK1, 2 * NEG, LE, ALU.mult, ALU.add))
            pick(PICK2, LE, 3, CAND, NEXP)
            dve.memset(ones, 1.0)
            dve.memset(ones32, 1.0)
            seq(dve.tensor_tensor(PICKS, PICK1, PICK2, ALU.add))
            seq(dve.tensor_copy(picked_to[:, 0, :], PICKS[:, 0, :]))
            for t in range(1, TT):
                ins = dve.tensor_tensor(picked_to[:, t, :], picked_to[:, t - 1, :], PICKS[:, t, :], ALU.add)
                if t + 1 < TT:
                    seq(ins)
            ins.then_inc(picks_v, 1)
            dve.tensor_tensor(stats[5], stats[3], stats[2], ALU.subtract).then_inc(exp_in, 1)
            dve.wait_ge(exp_out, 2)
            seq(dve.tensor_scalar(stats[4], stats[5], 1.0, None, ALU.add))
            seq(dve.reciprocal(stats[4], stats[4]))
            seq(dve.tensor_tensor(stats[4], stats[4], stats[1], ALU.mult))
            seq(dve.tensor_tensor(stats[5], stats[5], stats[4], ALU.mult))
            dve.wait_ge(rank_mm, 1)
            seq(dve.tensor_copy(RANK, bank[1][:, 0:TT * NEXP].rearrange("p (t n) -> p t n", n=NEXP)))
            seq(dve.tensor_copy(counts, bank[1][:, TT * NEXP:TT * NEXP + NEXP]))
            starts = const("pass_starts")
            NS = SEQ // SLOTS - 1

            def of_starts(ap, n):
                return ap.unsqueeze(2).to_broadcast([P, n, NS]), starts.unsqueeze(1).to_broadcast([P, n, NS])

            seq(dve.tensor_tensor(steps, *of_starts(counts, NEXP), ALU.is_gt))
            seq(dve.reduce_sum(over, steps, AX.X))
            seq(dve.tensor_tensor_scan(over_to, ones32, over, 0.0, ALU.mult, ALU.add))
            seq(dve.tensor_tensor(over_from, over_to, over, ALU.subtract))
            rank, expert, start, full, row = (rt[:, 468 + 8 * i:476 + 8 * i] for i in range(3, 8))
            picks = rt2[:, 256:512].rearrange("p (k t n) -> p k t n", k=2, t=TT)
            prod = rt2[:, 0:256].rearrange("p (k t n) -> p k t n", k=2, t=TT)
            for dst, of in ((rank, RANK), (expert, const4("expert_id")), (start, over_from.unsqueeze(1).to_broadcast([P, TT, NEXP]))):
                for k in range(2):
                    ins = dve.tensor_tensor(prod[:, k], picks[:, k], of, ALU.mult)
                seq(ins)
                seq(dve.reduce_sum(dst, prod.rearrange("p k t n -> p (k t) n"), AX.X))
            seq(dve.tensor_tensor(steps[:, 0:2 * TT, :], *of_starts(rank, 2 * TT), ALU.is_ge))
            seq(dve.reduce_sum(full, steps[:, 0:2 * TT, :], AX.X))
            seq(dve.scalar_tensor_tensor(rank, full, -float(SLOTS), rank, ALU.mult, ALU.add))
            seq(dve.tensor_tensor(start, start, full, ALU.add))
            seq(dve.scalar_tensor_tensor(start, start, float(NEXP - 1), expert, ALU.add, ALU.subtract))
            seq(dve.tensor_scalar(full, full, 1.0, None, ALU.min))
            seq(dve.tensor_tensor(start, start, full, ALU.mult))
            seq(dve.tensor_tensor(start, start, expert, ALU.add))
            seq(dve.scalar_tensor_tensor(row, rank, float(NPASS), start, ALU.mult, ALU.add))
            dve.tensor_copy(entry_row[:, :], row)
            for k in range(2):
                at = slice(TT * k, TT * k + TT)
                dve.tensor_copy(entry[:, at, 0], const("token_id"))
                dve.tensor_scalar(entry[:, at, 1], const("token_id"), float(SEQ * k), None, ALU.add)
                dve.tensor_copy(entry[:, at, 2].bitcast(f32), stats[4 + k])
                ins = dve.tensor_copy(entry[:, at, 3], const("token_id"))
            ins.then_inc(entry_v, 1)
            dve.tensor_copy(passes[:, 0:1], over_to[0:1, NEXP - 1:NEXP])
            ended = rt2[0:1, 0:NEXP * MAXOV].rearrange("p (j n) -> p j n", n=NEXP)
            dve.wait_ge(entry_v, 1)
            for j in range(MAXOV):
                ins = dve.tensor_scalar(ended[:, j, :], over_to[0:1, :], float(j), None, ALU.is_le)
            seq(ins)
            seq(dve.reduce_sum(pass_tmp[:, 0:MAXOV], ended, AX.X))
            seq(dve.tensor_scalar(pass_tmp[:, 0:MAXOV], pass_tmp[:, 0:MAXOV], float(NEXP - 1), None, ALU.min))
            seq(dve.tensor_copy(passes[:, 1:1 + MAXOV], pass_tmp[:, 0:MAXOV]))
            dve.memset(picked[0:SLOTS, 1, :], 0.0).then_inc(gather_v, 1)
            for q in range(2, PIECES):
                lo_piece(0, q)
            dve.wait_ge(table_in, 16)
            dve.tensor_copy(gather_at[0:SLOTS, :], table[0:SLOTS, :, 0]).then_inc(gather_v, 1)

            def y_half(e, b):
                dve.wait_ge(w2_mm, e + 1)
                if not (isinstance(e, int) and e < 2):
                    dve.wait_ge(y_out[b], 16 * (e // 2))
                dve.tensor_scalar(ys[:, b, 512:D], bank[6][0:SLOTS, :], weight_of(e), None, ALU.mult).then_inc(y_v, 1)

            def turn_x(e, b):
                dve.wait_ge(xt_a, e + 1)
                dve.tensor_tensor(xT[:, b, :, SLOTS:P], turned(b), xT[:, b, :, 0:SLOTS].bitcast(f32), ALU.subtract).then_inc(xt_v, 1)

            def hidden(e):
                dve.wait_ge(ab_a, 2 * e + 2)
                dve.tensor_tensor(half_a[:, :], bank[2][0:SLOTS, :], half_a[:, :], ALU.add).then_inc(a_v, 1)
                dve.tensor_tensor(half_b[:, :], bank[3][0:SLOTS, :], half_b[:, :], ALU.add).then_inc(b_v, 1)
                dve.wait_ge(silu_done, e + 1)
                dve.wait_ge(b_v, e + 1)
                if not (isinstance(e, int) and e == 0):
                    dve.wait_ge(ht_mm, e)
                dve.tensor_tensor(hid[:, :], silu_a[:, :], half_b[:, :], ALU.mult).then_inc(hid_v, 1)

            def dve_step(e, b, last=False, head=0):
                if head >= 2:
                    y_half(e - 2, b)
                if not last:
                    for q in range(3):
                        lo_piece(e + 1, q)
                    turn_x(e + 1, 1 - b)
                    lo_piece(e + 1, 3)
                hidden(e)

            turn_x(0, 0)
            dve_step(0, 0)
            dve_step(1, 1, head=1)
            dve_step(2, 0, head=2)
            dve_step(3, 1, head=2)
            with dve.Fori(0, (NEXP - 6) // 2) as i:
                for b in range(2):
                    dve_step(2 * i + 4 + b, b, head=2)
            dve_step(NEXP - 2, 0, head=2)
            dve_step(NEXP - 1, 1, head=2, last=True)
            y_half(NEXP - 2, 0)
            y_half(NEXP - 1, 1)
            n_over = dve.value_load(passes[0:1, 0:1], min_val=0, max_val=MAXOV)
            for b in range(2):
                dve.wait_ge(y_out[b], 16 * NEXP // 2)
            dve.wait_ge(y_a, NEXP)
            dve.sem_inc(ov_ready, 1)
            with dve.If(n_over > 0):
                with dve.Fori(0, n_over) as j:
                    for q in range(PIECES):
                        dve.wait_ge(ov_hi, 4 * j + q + 1)
                        split_lo(q).then_inc(ov_lo, 1)
                    dve.wait_ge(ov_xe_a, j + 1)
                    dve.tensor_tensor(xT[:, 0, :, SLOTS:P], turned(0), xT[:, 0, :, 0:SLOTS].bitcast(f32), ALU.subtract).then_inc(ov_xe_v, 1)
                    dve.wait_ge(ov_half, 3 * j + 2)
                    dve.tensor_tensor(half_a[:, :], bank[2][0:SLOTS, :], half_a[:, :], ALU.add).then_inc(ov_hid, 1)
                    dve.tensor_tensor(half_b[:, :], bank[3][0:SLOTS, :], half_b[:, :], ALU.add).then_inc(b_v, 1)
                    dve.wait_ge(b_v, j + NEXP + 1)
                    dve.wait_ge(ov_half, 3 * j + 3)
                    dve.tensor_tensor(hid[:, :], silu_a[:, :], half_b[:, :], ALU.mult).then_inc(ov_hid, 1)
                    dve.wait_ge(ov_y, j + 1)
                    dve.tensor_scalar(ys[:, 0, 512:D], bank[6][0:SLOTS, :], weight_of(j + NEXP), None, ALU.mult).then_inc(ov_ys, 1)
            gate2 = mod[:, 6:8, :].rearrange("p a n -> p (a n)")
            for t in range(TT):
                dve.wait_ge(s_added, t + 1)
                seq(dve.tensor_tensor(sum0[:, t, :], sum0[:, t, :], gate2, ALU.mult))
                dve.tensor_tensor(x[:, t, :], x[:, t, :], sum0[:, t, :], ALU.add).then_inc(s_final, 1)

        @block.tensor
        def _(pe):
            def ada(n):
                pe.wait_ge(ada_in, 2 * n + 2)
                even, odd = ada_acc(n)
                if n < 4:
                    for i in range(4):
                        dst = bank[0][:, 4 * n + i:4 * n + i + 1]
                        pe.matmul(dst, even[:, P * i:P * i + P], one, start=True, stop=False)
                        mm = pe.matmul(dst, odd[:, P * i:P * i + P], one, start=False, stop=True)
                    mm.then_inc(ada_mm, 1)
                    return
                if 6 <= n < 10:
                    pe.wait_ge(ada_out, n - 5)
                dst, ones_ = sum_bank(n), one.to_broadcast([P, P])
                pe.matmul(dst, ones_, even, start=True, stop=False)
                pe.matmul(dst, ones_, odd, start=False, stop=False)
                pe.matmul(dst, one[0:1, :].to_broadcast([1, P]), mod[0:1, n - 4, :], start=False, stop=True).then_inc(ada_mm, 1)

            pe.wait_ge(s_c, 16 * 12)
            pe.transpose(bank[7][:, 0:74], prow[0:74, :], ident[0:74, 0:74]).then_inc(first_turned, 1)
            pe.wait_ge(s_cols, 1)
            for k in range(KT):
                if k >= 2:
                    pe.wait_ge(s_xT, k - 1)
                for t in range(TT):
                    if k == 0:
                        pe.wait_ge(s_xn, t + 1)
                    mm = pe.transpose(bank[2 + k % 2][:, t * P:t * P + P], x_n[:, t, k * P:k * P + P], ident)
                mm.then_inc(first_turned, 1)
            for n in range(4):
                ada(n)
            pe.wait_ge(s_bias2, 16)
            def three_passes(dst, a, b, k, col_a, col_b):
                for n, (i, l) in enumerate(((0, 0), (0, 1), (1, 0))):
                    mm = pe.matmul(dst, a[i][:, k, col_a], b[l][:, k, col_b], start=(k == 0 and n == 0), stop=(k == KT - 1 and n == 2))
                return mm

            for j, ct in enumerate(Z_TILES):
                if j in (0, 2, 6, 10):
                    item = (j + 2) // 4
                    pe.wait_ge(cut_v, z_cut_count(item) + 2)
                if j >= 4:
                    pe.wait_ge(z_shifted, j - 3)
                for k in range(KT):
                    if j == 0:
                        pe.wait_ge(cut_v, 2 + k + 1)
                    mm = three_passes(bank[4 + j % 4][:, :], z_cut_views(item), (h_hi, h_lo), k, slice((ct % 4) * P, (ct % 4) * P + P), slice(0, SEQ))
                mm.then_inc(z_mm, 1)
                if j - 2 in ADA_AFTER:
                    ada(4 + ADA_AFTER.index(j - 2))
            def att_tile(j):
                if j % TT == 0:
                    ring_wait(pe, ATT_AT[j // TT])
                w = slot_view(ATT_AT[j // TT])
                if j == 0:
                    pe.wait_ge(z_shifted, 14)
                if j >= 2:
                    pe.wait_ge(att_out, j - 1)
                for k in range(KT):
                    if j == 0:
                        pe.wait_ge(h_whole, k + 1)
                    mm = pe.matmul(bank[6 + j % 2][:, :], hT[:, k, (j % TT) * P:(j % TT) * P + P], w[:, k, :], start=(k == 0), stop=(k == KT - 1))
                mm.then_inc(att_mm, 1)

            def lora(ct):
                for i, rows in enumerate((slice(0, 64), slice(64, 128))):
                    if ct:
                        pe.wait_ge(lora_act, 2 * ct - 1 + i)
                    pe.matmul(bank[i][:, :], lora_wa[rows, P * ct:P * ct + P], zr[rows, 12, :], start=True, stop=True).then_inc(lora_mm, 1)

            ada(9)
            att_tile(0)
            pe.wait_ge(ada_out, 6)
            pe.wait_ge(s_const, 16)
            pe.wait_ge(s_act_in, 1)
            pe.wait_ge(s_lora_w, 32)
            lora(0)
            for ct in range(CT):
                v_ = zr[:, 8 + ct, :]
                if ct:
                    att_tile(3 * ct)
                pe.wait_ge(sq_act, ct + 1)
                if ct == 2:
                    pe.wait_ge(ada_out, 7)
                elif ct == 3:
                    pe.wait_ge(ada_out, 8)
                pe.matmul(bank[2][:, :], const("head_ones"), xs[2], start=True, stop=True).then_inc(ss_mm, 1)
                if ct + 1 < CT:
                    lora(ct + 1)
                att_tile(3 * ct + 1)
                pe.wait_ge(bonus_in, ct + 1)
                if ct:
                    pe.wait_ge(prep_done, ct)
                pe.matmul(bank[3][:, :], const("head_ones"), xs[5], start=True, stop=True).then_inc(bonus_mm, 1)
                if ct in (1, 2):
                    pe.wait_ge(ss_act, ct + 1)
                    ada(9 + ct)
                att_tile(3 * ct + 2)
                pe.wait_ge(forms_done, ct + 1)
                for t in range(TT):
                    if TT * ct + t >= 2:
                        pe.wait_ge((turn_v, turn_a)[t % 2], (TT * ct + t) // 2)
                    for i, src in enumerate((v_, xs[1], xs[4], ahat[:, ct, :])):
                        mm = pe.transpose(bank[4 + t % 2][:, P * i:P * i + P], src[:, P * t:P * t + P], ident)
                    mm.then_inc(turn_mm, 1)
            pe.wait_ge(att_out, 12)
            pe.wait_ge(prep_done, CT)
            pe.wait_ge(turn_v, 2 * CT)
            pe.wait_ge(turn_a, 2 * CT)
            pe.wait_ge(ada_out, 8)
            for sc in range(TT):
                toks = slice(P * sc, P * sc + P)
                for ev in MM_EVENTS:
                    for g in range(2):
                        B = bank[4 * g:4 * g + 4]
                        if ev == "y" and g == 0:
                            for c in range(2):
                                n = 2 * sc + c
                                if n:
                                    for g2 in range(2):
                                        pe.wait_ge(solve_v[g2], v_at(sc, f"g{c}"))
                                    pe.wait_ge(chain_v, n)
                                    for h in range(HEADS):
                                        mm = pe.matmul(bank[2 if c == 0 else 6][0:HD, HD * h:HD * h + HD], GG[c][h // 4][:, h % 4, :],
                                                       STATE[n % 3][:, h, :], start=True, stop=True)
                                    mm.then_inc(chain_mm, 1)
                            for g2 in range(2):
                                pe.wait_ge(solve_v[g2], v_at(sc, "q"))
                        if ev == "ab":
                            if sc:
                                pe.wait_ge(solve_v[g], v_at(sc - 1, "y"))
                                pe.wait_ge(solve_a[g], a_at(sc - 1, "h1"))
                                pe.wait_ge(chain_v, 2 * sc)
                        need_v = {"t0": "rb", "p1": "n0", "n1": "p1", "x": "ak", "q": "rb", "y": "q"}
                        if ev in need_v:
                            pe.wait_ge(solve_v[g], v_at(sc, need_v[ev]))
                        elif ev[0] == "p":
                            pe.wait_ge(solve_a[g], a_at(sc, f"n{int(ev[1]) - 1}"))
                        elif ev[0] == "n" or ev == "m5":
                            pe.wait_ge(solve_v[g], v_at(sc, "p" + ev[1]))
                            pe.wait_ge(solve_a[g], a_at(sc, f"m{int(ev[1]) - 1}"))
                        elif ev[0] == "m":
                            pe.wait_ge(solve_a[g], a_at(sc, "n" + ev[1]))
                        if ev == "n1":
                            pe.wait_ge(solve_v[g], v_at(sc, "m0"))
                        if ev == "wu":
                            pe.wait_ge(solve_a[g], a_at(sc, "x"))
                        if ev == "q":
                            pe.wait_ge(solve_a[g], a_at(sc, "wu"))
                        for i in range(4):
                            h = 4 * g + i
                            ct, rows = h // 2, slice(HD * (h % 2), HD * (h % 2) + HD)
                            hc = slice(HD * (h % 2), HD * (h % 2) + HD)
                            at = slice(P * i, P * i + P)
                            V_, Bt, Kt_, Ah = (tokm[:, sc, ct, q, hc] for q in range(4))
                            a_, b_ = ahat[rows, ct, toks], bhat[rows, ct, toks]
                            k_, r_ = zr[rows, 4 + ct, toks], zr[rows, ct, toks]
                            if ev == "ab":
                                mm = pe.matmul(B[i % 2][:, P * (i // 2):P * (i // 2) + P], b_, a_, start=True, stop=True)
                            elif ev == "rb":
                                mm = pe.matmul(B[i % 2][:, P * (2 + i // 2):P * (2 + i // 2) + P], b_, r_, start=True, stop=True)
                            elif ev == "ak":
                                mm = pe.matmul(B[2 + i % 2][:, P * (i // 2):P * (i // 2) + P], k_, a_, start=True, stop=True)
                            elif ev == "rk":
                                mm = pe.matmul(B[2 + i % 2][:, P * (2 + i // 2):P * (2 + i // 2) + P], k_, r_, start=True, stop=True)
                            elif ev == "t0":
                                mm = pe.transpose(B[0][:, at], TT1[g][:, i, :], ident)
                            elif ev[0] == "p":
                                mm = pe.matmul(B[1][:, at], TT1[g][:, i, :], INV[g][:, i, :], start=True, stop=True)
                            elif ev[0] == "n":
                                mm = pe.matmul(B[2][:, at], INVT[g][:, i, :], PP[g][:, i, :], start=True, stop=True)
                            elif ev[0] == "m" and ev != "m5":
                                mm = pe.transpose(B[3][:, at], INV[g][:, i, :], ident)
                            elif ev[0] == "m":
                                mm = pe.matmul(B[3][:, at], PP[g][:, i, :], INVT[g][:, i, :], start=True, stop=True)
                            elif ev == "x":
                                mm = pe.matmul(B[0][:, HD * i:HD * i + HD], AK[g][:, i, :], V_, start=True, stop=True)
                            elif ev == "wu":
                                pe.matmul(B[2][:, P * i:P * i + HD], INVT[g][:, i, :], Ah, start=True, stop=True)
                                mm = pe.matmul(B[2][:, P * i + HD:P * i + P], INVT[g][:, i, :], XX[g][:, i, :], start=True, stop=True)
                            elif ev == "q":
                                mm = pe.matmul(B[1][0:HD, at], WU[g][:, i, 0:HD], RB[g][:, i, :], start=True, stop=True)
                            elif ev[:2] == "gh":
                                c = int(ev[2])
                                cr = slice(CH * c, CH * c + CH)
                                dst = B[3 if c == 0 else 0]
                                if i == 0 and c == 0:
                                    pe.wait_ge(solve_a[g], a_at(sc, "m5"))
                                pe.matmul(dst[0:HD, HD * i:HD * i + HD], WU[g][cr, i, 0:HD], Bt[cr, :], start=True, stop=True)
                                pe.matmul(dst[0:HD, 256 + HD * i:256 + HD * i + HD], Bt[cr, :], WU[g][cr, i, HD:P], start=True, stop=False)
                                mm = pe.matmul(dst[0:HD, 256 + HD * i:256 + HD * i + HD], Kt_[cr, :], V_[cr, :], start=False, stop=True)
                            elif ev == "y":
                                pe.matmul(B[1][0:HD, at], WU[g][:, i, HD:P], RB[g][:, i, :], start=True, stop=False)
                                mm = pe.matmul(B[1][0:HD, at], V_, RK[g][:, i, :], start=False, stop=False)
                                for c in range(2):
                                    n = 2 * sc + c
                                    if n:
                                        if i == 0:
                                            pe.wait_ge(chain_v, n)
                                        mm = pe.matmul(B[1][0:HD, P * i + CH * c:P * i + CH * c + CH], STATE[n % 3][:, h, :],
                                                       QQ[g][:, i, CH * c:CH * c + CH], start=False, stop=(c == 1))
                        mm.then_inc(solve_mm[g], 1)
            for g in range(2):
                pe.wait_ge(solve_v[g], v_at(TT - 1, "y"))
            for ct in range(CT):
                pe.matmul(bank[ct][:, :], const("head_ones"), ahat[:, ct, :], start=True, stop=True).then_inc(gn_mm, 1)
            pe.wait_ge(s_lora_w, 48)
            for ct in range(CT):
                pe.matmul(bank[4 + ct][:, :], lora_g[:, P * ct:P * ct + P], zr[:, 13, :], start=True, stop=True).then_inc(gn_mm, 1)
            for ct in range(CT):
                pe.wait_ge(gn_v, CT + ct + 1)
                pe.matmul(bank[ct][:, :], const("head_ones"), xs[ct], start=True, stop=True).then_inc(gn_mm, 1)
            for j in range(8):
                if j >= 4:
                    pe.wait_ge(qk_a, j - 3)
                else:
                    pe.wait_ge(gn_a, j + 1)
                for t in range(TT):
                    if j in (0, 4):
                        pe.wait_ge(rope_done, 2 * t + 1 + j // 4)
                    c0 = W * (j // 4) + P * (j % 4)
                    mm = pe.transpose(bank[4 + j % 4][:, P * t:P * t + P], qkv[:, t, c0:c0 + P], ident)
                mm.then_inc(qk_mm, 1)
            pe.wait_ge(gn_a, 2 * CT)
            pe.wait_ge(qk_a, 8)

            def scores(h):
                rows, ct = slice(HD * (h % 2), HD * (h % 2) + HD), h // 2
                done = 0
                for unit in UNITS:
                    done += len(unit)
                    if h:
                        pe.wait_ge(exp_a, TT * (h - 1) + done)
                    for i in unit:
                        q_ = qT[rows, ct, P * i:P * i + P]
                        if i:
                            pe.matmul(S_AT[i][:, 0:P * i], q_, kT[rows, ct, 0:P * i], start=True, stop=True)
                        pe.matmul(S_AT[i][:, P * i:P * i + P], q_, kT[rows, ct, P * i:P * i + P], start=True, stop=False)
                        mm = pe.matmul(S_AT[i][:, P * i:P * i + P], ident, const("diag_mask"), start=False, stop=True)
                    mm.then_inc(s_mm, 1)

            def weighted(h):
                pe.wait_ge(pt_a, 2 * h + 2)
                pe.wait_ge(pt_v, 2 * h + 2)
                if h >= 2:
                    pe.wait_ge(pv_out, h - 1)
                for i in range(TT):
                    for kt in range(i + 1):
                        mm = pe.matmul(bank[3 + 4 * (h % 2)][:, HD * i:HD * i + HD], PROBT[h % 2][kt][:, P * (i - kt):P * (i - kt) + P],
                                       qkv[:, kt, 2 * W + HD * h:2 * W + HD * h + HD], start=(kt == 0), stop=(kt == i))
                mm.then_inc(pv_mm, 1)

            scores(0)
            for h in range(HEADS):
                if h + 1 < HEADS:
                    scores(h + 1)
                if h:
                    weighted(h - 1)
                pe.wait_ge(exp_a, TT * h + TT)
                for kt in range(TT):
                    for i in range(kt, TT):
                        mm = pe.transpose(PT_AT[kt][:, P * (i - kt):P * (i - kt) + P], PROB[h % 2][i][:, P * kt:P * kt + P], ident)
                mm.then_inc(pt_mm, 1)
            weighted(HEADS - 1)
            def project(j):
                b, ct = j // KT, j % KT
                at = N_BEFORE_MERGE + 3 * b
                ring_wait(pe, at)
                if j >= 2:
                    pe.wait_ge(mg_v, j - 1)
                if j == KT:
                    pe.wait_ge(yt_v, CT)
                for k in range(CT):
                    pe.matmul(bank[j % 2][:, :], slot_view(at, CT)[:, k, P * ct:P * ct + P], (ahat, bhat)[b][:, k, :], start=(k == 0), stop=(k == CT - 1))

            def gate(j):
                b, ct = j // KT, j % KT
                i = N_BEFORE_MERGE + 3 * b + 1 + ct // 4
                if j == 1:
                    pe.wait_ge(pv_out, HEADS - 1)
                pe.wait_ge(cut_v, cut_count(CUT_OF[i]) + 2)
                for k in range(KT):
                    mm = three_passes(bank[2 + j % 2][:, :], cut_views(i), (h_hi, h_lo), k,
                                      slice(P * (ct % 4), P * (ct % 4) + P), slice(0, SEQ))
                mm.then_inc(mg_mm, 1)

            for b in range(2):
                project(KT * b)
                project(KT * b + 1)
                if b == 0:
                    pe.wait_ge(pv_out, HEADS)
                    for c in range(CT):
                        for t in range(TT):
                            mm = pe.transpose(bank[4 + c][:, P * t:P * t + P], y_tok[:, t, P * c:P * c + P], ident)
                        mm.then_inc(yt_mm, 1)
                for ct in range(KT):
                    if ct >= 2:
                        project(KT * b + ct)
                    gate(KT * b + ct)
            pe.wait_ge(yt_v, CT)
            for j in range(2 * TT):
                i = len(items) - 2 + j // TT
                if j == TT:
                    pe.wait_ge(cut_v, cut_count(5) + 2)
                if j >= TT:
                    pe.wait_ge(x2_done, j - TT + 1)
                for k in range(KT):
                    if j == 0:
                        pe.wait_ge(cut_v, cut_count(4) + 2 + k + 1)
                    mm = three_passes(bank[4 + j % TT][:, :], (m_hi, m_lo), cut_views(i), k,
                                      slice(P * (j % TT), P * (j % TT) + P), slice(0, 512))
                mm.then_inc(out_mm, 1)
            for k in range(KT):
                if k >= 4:
                    pe.wait_ge((h2t_a, h2t_v)[k % 2], k // 2 - 1)
                for t in range(TT):
                    if k == 0:
                        pe.wait_ge(h2_v, t + 1)
                    mm = pe.transpose(bank[4 + k % 4][:, t * P:t * P + P], h2[:, t, k * P:k * P + P], ident)
                mm.then_inc(h2t_mm, 1)
            pe.wait_ge(h2t_a, 4)
            pe.wait_ge(h2t_v, 4)
            pe.wait_ge(s_route_w, 64)
            for t in range(TT):
                for k in range(KT):
                    mm = pe.matmul(bank[0][:, NR * t:NR * t + NR], h2T[:, k, P * t:P * t + P], w_route[:, k, :], start=(k == 0), stop=(k == KT - 1))
            mm.then_inc(logit_mm, 1)
            pe.wait_ge(picks_v, 1)
            later = bank[1][:, NEXP:TT * NEXP]
            pe.matmul(bank[1][:, 0:NEXP], const("before"), PICKS[:, 0, :], start=True, stop=True)
            pe.matmul(later, const("before"), PICKS[:, 1:TT, :], start=True, stop=False)
            pe.matmul(later, ones, picked_to[:, 0:TT - 1, :], start=False, stop=True)
            mm = pe.matmul(bank[1][:, TT * NEXP:TT * NEXP + NEXP], ones, picked_to[:, TT - 1, :], start=True, stop=True)
            mm.then_inc(rank_mm, 1)

            def turn_rows(b):
                for k in range(KT):
                    mm = pe.transpose(turned(b)[:, k, :], picked[0:SLOTS, b, k:D:KT], ident[0:SLOTS, 0:SLOTS])
                return mm

            def piece(q, b):
                for k in range(4):
                    for part in (hi, lo):
                        mm = pe.matmul(bank[2 + q % 2][:, :], xT[:, b, 4 * (q // 2) + k, :], part[:, q, k, :],
                                       start=(q < 2 and k == 0 and part is hi), stop=(q >= 2 and k == 3 and part is lo))
                return mm

            def turn_hid():
                for k in range(4):
                    mm = pe.transpose(bank[4][:, SLOTS * k:SLOTS * k + SLOTS], hid[:, k:DE:4], ident[0:SLOTS, 0:SLOTS])
                return mm

            def down(b):
                for k in range(4):
                    for n in range(2):
                        mm = pe.matmul(bank[5 + n][0:SLOTS, :], hidT[:, k, :], w2s[:, b, k, 512 * n:512 * n + 512], start=(k == 0), stop=(k == 3))
                return mm

            def do_rows(e, b):
                first_one = isinstance(e, int) and e == 0
                pe.wait_ge(rows_in[b], 16 * (e // 2 + 1) if isinstance(e, int) else 16 * (e // 2) + 16)
                if not first_one:
                    pe.wait_ge(xt_v, e)
                    pe.sem_inc(past, 1)
                turn_rows(b).then_inc(xt_mm, 1)

            def do_piece(e, q, b):
                if q == 0:
                    pe.wait_ge(xt_v, e + 1)
                    if not (isinstance(e, int) and e == 0):
                        pe.wait_ge(b_v, e)
                pe.wait_ge(lo_done, PIECES * e + q + 1)
                piece(q, b).then_inc(piece_mm, 1)

            def do_turn_hid(e):
                pe.wait_ge(hid_v, e + 1)
                pe.sem_inc(past, 1)
                turn_hid().then_inc(ht_mm, 1)

            def do_down(e, b):
                pe.wait_ge(ht_a, e + 1)
                pe.wait_ge(w2_in[b], 16 * (e // 2 + 1) if isinstance(e, int) else 16 * (e // 2) + 16)
                if not (isinstance(e, int) and e == 0):
                    pe.wait_ge(y_a, e)
                    pe.wait_ge(y_v, e)
                down(b).then_inc(w2_mm, 1)

            def pe_step(e, b, last=False):
                for q in range(3):
                    do_piece(e, q, b)
                do_turn_hid(e - 1)
                do_piece(e, 3, b)
                if not last:
                    do_rows(e + 1, 1 - b)
                do_down(e - 1, 1 - b)

            do_rows(0, 0)
            for q in range(PIECES):
                do_piece(0, q, 0)
            do_rows(1, 1)
            pe_step(1, 1)
            with pe.Fori(0, (NEXP - 4) // 2) as i:
                for b in range(2):
                    pe_step(2 * i + 2 + b, b)
            pe_step(NEXP - 2, 0)
            pe_step(NEXP - 1, 1, last=True)
            do_turn_hid(NEXP - 1)
            do_down(NEXP - 1, 1)
            n_over = pe.value_load(passes[0:1, 0:1], min_val=0, max_val=MAXOV)
            with pe.If(n_over > 0):
                with pe.Fori(0, n_over) as j:
                    pe.wait_ge(ov_rows, 16 * j + 16)
                    pe.sem_inc(past, 1)
                    turn_rows(0).then_inc(ov_xt, 1)
                    pe.wait_ge(ov_xe_v, j + 1)
                    pe.wait_ge(ov_lo, 4 * j + 4)
                    for q in range(PIECES):
                        mm = piece(q, 0)
                    mm.then_inc(ov_mm, 1)
                    pe.wait_ge(ov_hid, 2 * j + 2)
                    pe.sem_inc(past, 1)
                    turn_hid().then_inc(ov_ht, 1)
                    pe.wait_ge(ov_hte, j + 1)
                    pe.wait_ge(ov_w2, 16 * j + 16)
                    down(0).then_inc(ov_y, 1)


_INS = ["x", "c", "w_ada", "b_ada", "ln1_g", "ln2_g", "w_in", "mu_shift", "w0", "w_lora_up", "a0", "a_lora_up",
        "g_lora_up", "k_k", "k_a", "r_k", "lnx_g", "lnx_b", "q_norm_g", "k_norm_g", "w_br_rwkv", "w_br_moba",
        "w_out", "w_rg", "b_rg", "w_re", "b_re", "w1", "w3", "w2"]


def kernel(**inputs):
    import numpy as _np
    import concourse.bacc as _bacc
    from concourse import mybir as _mybir
    from concourse.bass_utils import run_bass_kernel_spmd as _run

    nc = _bacc.Bacc("TRN2", target_bir_lowering=False, num_devices=1)
    arrays, A = {}, {}
    for name in _INS:
        a = _np.ascontiguousarray(inputs[name])
        if name not in ("c",):
            a = a.reshape(a.shape[1:])
        if name == "r_k":
            a = a.reshape(-1)
        arrays[f"in_{name}"] = a
        A[name] = nc.dram_tensor(f"in_{name}", a.shape, _mybir.dt.from_np(a.dtype), kind="ExternalInput").ap()
    arrays["in_consts"] = CONSTS
    A["consts"] = nc.dram_tensor("in_consts", CONSTS.shape, _mybir.dt.float32, kind="ExternalInput").ap()
    out = nc.dram_tensor("out", (SEQ, D), _mybir.dt.float32, kind="ExternalOutput").ap()
    hybrid_layer(nc, A, out)
    r = _run(nc, [arrays], core_ids=[0])
    return r.results[0]["out"].reshape(1, SEQ, D)
```
